# Optimizing a Trainium2 kernel written in Bass

```python
import jax, jax.numpy as jnp
from jax import lax
import numpy as np

D_MODEL = 1024
BATCH = 1
SEQ = 256
DEPTH = 1
DEC_BATCH = 1
DEC_SEQ = 1024
PAST_LEN = 128

N_ATT_HEADS = 16
N_KV_GROUPS = 4
ATT_HEAD_DIM = D_MODEL // N_ATT_HEADS
ATT_WIDTH = N_ATT_HEADS * ATT_HEAD_DIM
KV_WIDTH = N_KV_GROUPS * ATT_HEAD_DIM
WINDOW = 128
BLOCK = 128
N_MLSTM_HEADS = 4
MLSTM_WIDTH = D_MODEL
MLSTM_HEAD_DIM = MLSTM_WIDTH // N_MLSTM_HEADS
CHUNK = 128
FORGET_BIAS = 3.0
D_FF = 2816
CONV_WIDTH = 3
EPS = 1e-6

SPLIT_SIZES = (ATT_WIDTH, KV_WIDTH, KV_WIDTH,
               MLSTM_WIDTH, MLSTM_WIDTH, MLSTM_WIDTH, MLSTM_WIDTH,
               2 * N_MLSTM_HEADS, 2 * N_MLSTM_HEADS, 2 * D_MODEL)
IN_WIDTH = int(sum(SPLIT_SIZES))
SPLIT_POINTS = tuple(int(c) for c in np.cumsum(SPLIT_SIZES)[:-1])

kernel_name = "hybrid_bidir_mlstm_swa_encoder"

F32 = jnp.float32

def rmsnorm(x, w):
    xf = x.astype(F32)
    y = xf * lax.rsqrt(jnp.mean(xf * xf, axis=-1, keepdims=True) + EPS)
    return (y * w.astype(F32)).astype(x.dtype)

def alibi_slopes(n_heads):
    return 2.0 ** (-8.0 * jnp.arange(1, n_heads + 1, dtype=F32) / n_heads)

def windowed_gqa_attention(q, k, v, sink):
    B, S, H, hd = q.shape
    G = k.shape[2]
    R = H // G
    nb = S // BLOCK
    qb = q.reshape(B, nb, BLOCK, G, R, hd)

    def windows(t):
        tb = t.reshape(B, nb, BLOCK, G, hd)
        pad = jnp.zeros((B, 1, BLOCK, G, hd), t.dtype)
        tp = jnp.concatenate([pad, tb, pad], axis=1)
        return jnp.concatenate([tp[:, :-2], tp[:, 1:-1], tp[:, 2:]], axis=2)

    kw = windows(k)
    vw = windows(v)
    rel = (jnp.arange(3 * BLOCK)[None, :] - BLOCK) - jnp.arange(BLOCK)[:, None]
    in_window = jnp.abs(rel) <= WINDOW
    alibi = (-alibi_slopes(H)[:, None, None] * jnp.abs(rel).astype(F32)[None]).reshape(G, R, BLOCK, 3 * BLOCK)
    sink_g = sink.astype(F32).reshape(G, R)
    scale = hd ** -0.5

    def block_fn(args):
        j, qj, kj, vj = args
        kpos = j * BLOCK - BLOCK + jnp.arange(3 * BLOCK)
        valid = in_window & ((kpos >= 0) & (kpos < S))[None, :]
        s = jnp.einsum('bqgrd,bkgd->bgrqk', qj.astype(F32), kj.astype(F32)) * scale + alibi
        s = jnp.where(valid, s, -jnp.inf)
        sink_col = jnp.broadcast_to(sink_g[None, :, :, None, None], s.shape[:-1] + (1,))
        p = jax.nn.softmax(jnp.concatenate([s, sink_col], axis=-1), axis=-1)[..., :-1]
        o = jnp.einsum('bgrqk,bkgd->bqgrd', p, vj.astype(F32))
        return o.astype(qj.dtype)

    out = lax.map(block_fn, (jnp.arange(nb), jnp.moveaxis(qb, 1, 0),
                             jnp.moveaxis(kw, 1, 0), jnp.moveaxis(vw, 1, 0)))
    return jnp.moveaxis(out, 0, 1).reshape(B, S, H * hd)

def mlstm_chunkwise(q, k, v, log_i, log_f):
    B, H, S, dh = q.shape
    nc = S // CHUNK

    def to_chunks(t):
        return jnp.moveaxis(t.reshape((B, H, nc, CHUNK) + t.shape[3:]), 2, 0)

    lower = jnp.tril(jnp.ones((CHUNK, CHUNK), dtype=bool))

    def step(carry, xs):
        C, n, m = carry
        qc, kc, vc, li, lf = xs
        b = jnp.cumsum(lf, axis=-1)
        d = b[..., :, None] - b[..., None, :] + li[..., None, :]
        d = jnp.where(lower, d, -jnp.inf)
        m_inter = b + m[..., None]
        m_t = jnp.maximum(m_inter, jnp.max(d, axis=-1))
        w_inter = jnp.exp(m_inter - m_t)
        a = jnp.einsum('bhtd,bhsd->bhts', qc, kc) * jnp.exp(d - m_t[..., None])
        num = w_inter[..., None] * jnp.einsum('bhtd,bhde->bhte', qc, C) + jnp.einsum('bhts,bhse->bhte', a, vc)
        den = w_inter * jnp.einsum('bhtd,bhd->bht', qc, n) + jnp.sum(a, axis=-1)
        h = num / jnp.maximum(jnp.abs(den), jnp.exp(-m_t))[..., None]
        b_last = b[..., -1]
        g = b_last[..., None] - b + li
        m_new = jnp.maximum(b_last + m, jnp.max(g, axis=-1))
        decay = jnp.exp(b_last + m - m_new)
        wk = jnp.exp(g - m_new[..., None])[..., None] * kc
        C_new = decay[..., None, None] * C + jnp.einsum('bhsd,bhse->bhde', wk, vc)
        n_new = decay[..., None] * n + jnp.sum(wk, axis=-2)
        return (C_new, n_new, m_new), h

    init = (jnp.zeros((B, H, dh, dh), F32), jnp.zeros((B, H, dh), F32), jnp.zeros((B, H), F32))
    _, hs = lax.scan(step, init, (to_chunks(q), to_chunks(k), to_chunks(v),
                                  to_chunks(log_i), to_chunks(log_f)))
    return jnp.moveaxis(hs, 0, 2).reshape(B, H, S, dh)

def bidirectional_mlstm(mq, mk, mv, mo, mi, mf, norm_w):
    B, S, _ = mq.shape
    Hm, dh = N_MLSTM_HEADS, MLSTM_HEAD_DIM

    def heads(t):
        return jnp.transpose(t.astype(F32).reshape(B, S, Hm, dh), (0, 2, 1, 3))

    q = heads(mq)
    k = heads(mk) * (dh ** -0.5)
    v = heads(mv)
    li = jnp.transpose(mi.astype(F32).reshape(B, S, 2, Hm), (2, 0, 3, 1))
    lf = jax.nn.log_sigmoid(jnp.transpose(mf.astype(F32).reshape(B, S, 2, Hm), (2, 0, 3, 1)) + FORGET_BIAS)
    h_fwd = mlstm_chunkwise(q, k, v, li[0], lf[0])
    flip = lambda t: jnp.flip(t, axis=2)
    h_bwd = flip(mlstm_chunkwise(flip(q), flip(k), flip(v), jnp.flip(li[1], -1), jnp.flip(lf[1], -1)))
    h = jax.nn.sigmoid(heads(mo)) * (h_fwd + h_bwd)
    h = h * lax.rsqrt(jnp.mean(h * h, axis=-1, keepdims=True) + EPS)
    h = jnp.transpose(h, (0, 2, 1, 3)).reshape(B, S, Hm * dh) * norm_w.astype(F32)
    return h.astype(mq.dtype)

def centred_depthwise_conv(a, w, b):
    S = a.shape[1]
    half = CONV_WIDTH // 2
    ap = jnp.pad(a, ((0, 0), (half, half), (0, 0)))
    out = sum(ap[:, t:t + S] * w[t] for t in range(CONV_WIDTH))
    return out + b

def encoder_layer(x, pre_mix_norm, w_in, b_in, attn_sink, mlstm_norm, w_att_branch,
                  w_mlstm_branch, w_out, post_mix_norm, pre_ffn_norm, w_ffn_up,
                  ffn_conv_w, ffn_conv_b, w_ffn_down, post_ffn_norm):
    B, S, _ = x.shape
    h = rmsnorm(x, pre_mix_norm)
    z = h @ w_in + b_in
    aq, ak, av, mq, mk, mv, mo, mi, mf, gates = jnp.split(z, SPLIT_POINTS, axis=-1)
    ya = windowed_gqa_attention(aq.reshape(B, S, N_ATT_HEADS, ATT_HEAD_DIM),
                                ak.reshape(B, S, N_KV_GROUPS, ATT_HEAD_DIM),
                                av.reshape(B, S, N_KV_GROUPS, ATT_HEAD_DIM), attn_sink)
    ym = bidirectional_mlstm(mq, mk, mv, mo, mi, mf, mlstm_norm)
    g_att, g_mlstm = jnp.split(jax.nn.sigmoid(gates), 2, axis=-1)
    merged = g_att * (ya @ w_att_branch) + g_mlstm * (ym @ w_mlstm_branch)
    x = x + rmsnorm(merged @ w_out, post_mix_norm)
    h2 = rmsnorm(x, pre_ffn_norm)
    a, gate = jnp.split(h2 @ w_ffn_up, 2, axis=-1)
    a = centred_depthwise_conv(a, ffn_conv_w, ffn_conv_b)
    f = jax.nn.gelu(a, approximate=True) * gate
    x = x + rmsnorm(f @ w_ffn_down, post_ffn_norm)
    return x

def setup_inputs(seed: int = 0) -> dict:
    key = jax.random.key(seed)
    ks = jax.random.split(key, 20)
    nrm = lambda k, shape, s: jax.random.normal(k, shape, F32) * s
    gain = lambda k, n: 1.0 + nrm(k, (DEPTH, n), 0.05)
    return {
        "x_prompt": nrm(ks[0], (BATCH, SEQ, D_MODEL), 1.0),
        "x_sample": nrm(ks[1], (DEC_BATCH, DEC_SEQ, D_MODEL), 1.0),
        "pre_mix_norm": gain(ks[2], D_MODEL),
        "w_in": nrm(ks[3], (DEPTH, D_MODEL, IN_WIDTH), D_MODEL ** -0.5),
        "b_in": nrm(ks[4], (DEPTH, IN_WIDTH), 0.02),
        "attn_sink": nrm(ks[5], (DEPTH, N_ATT_HEADS), 0.5),
        "mlstm_norm": gain(ks[6], MLSTM_WIDTH),
        "w_att_branch": nrm(ks[7], (DEPTH, ATT_WIDTH, D_MODEL), ATT_WIDTH ** -0.5),
        "w_mlstm_branch": nrm(ks[8], (DEPTH, MLSTM_WIDTH, D_MODEL), MLSTM_WIDTH ** -0.5),
        "w_out": nrm(ks[9], (DEPTH, D_MODEL, D_MODEL), D_MODEL ** -0.5),
        "post_mix_norm": gain(ks[10], D_MODEL),
        "pre_ffn_norm": gain(ks[11], D_MODEL),
        "w_ffn_up": nrm(ks[12], (DEPTH, D_MODEL, 2 * D_FF), D_MODEL ** -0.5),
        "ffn_conv_w": nrm(ks[13], (DEPTH, CONV_WIDTH, D_FF), CONV_WIDTH ** -0.5),
        "ffn_conv_b": nrm(ks[14], (DEPTH, D_FF), 0.02),
        "w_ffn_down": nrm(ks[15], (DEPTH, D_FF, D_MODEL), D_FF ** -0.5),
        "post_ffn_norm": gain(ks[16], D_MODEL),
    }

def reference(x_prompt, x_sample, pre_mix_norm, w_in, b_in, attn_sink, mlstm_norm,
              w_att_branch, w_mlstm_branch, w_out, post_mix_norm, pre_ffn_norm,
              w_ffn_up, ffn_conv_w, ffn_conv_b, w_ffn_down, post_ffn_norm):
    def trunk(x):
        for l in range(DEPTH):
            x = encoder_layer(x, pre_mix_norm[l], w_in[l], b_in[l], attn_sink[l], mlstm_norm[l],
                              w_att_branch[l], w_mlstm_branch[l], w_out[l], post_mix_norm[l],
                              pre_ffn_norm[l], w_ffn_up[l], ffn_conv_w[l], ffn_conv_b[l],
                              w_ffn_down[l], post_ffn_norm[l])
        return x

    y_prompt = trunk(x_prompt)
    y_sample = trunk(x_sample)
    return (y_prompt, y_sample)


_drawn_inputs = setup_inputs


def setup_inputs(seed=0):
    import zlib

    import numpy as np

    out = dict(_drawn_inputs(seed))
    spreads = {}
    factors = {'attn_sink': 7.523, 'ffn_conv_b': 4.97}
    for name, (base, spread) in spreads.items():
        noise = np.random.default_rng([zlib.crc32(name.encode()), seed]).standard_normal(out[name].shape)
        drawn = base * np.exp(spread * noise) if base else spread * noise
        out[name] = __import__('jax').numpy.asarray(drawn.astype(out[name].dtype))
    for name, factor in factors.items():
        out[name] = (out[name] * factor).astype(out[name].dtype)
    return out
```

```python
import numpy as np
import concourse.bass as bass
from concourse import mybir

F32 = mybir.dt.float32
F32R = mybir.dt.float32r
ALU = mybir.AluOpType
ACT = mybir.ActivationFunctionType
AX = mybir.AxisListType

P = 128
D = 1024
KT = D // P
SEQ_A, SEQ_B = 256, 1024
T = SEQ_A + SEQ_B
NB = T // P
NB_A = SEQ_A // P
HEADS = 4
DH = 256
HD = 64
QPG = 4
FF = 2816
FT = FF // P
EPS = 1e-6
FORGET_BIAS = 3.0
HALF = T // 2
WIN = HALF + 2
BIG = 1e30

C_MQ, C_MK, C_AQ, C_AKV, C_G, C_IF = 0, 8, 16, 24, 28, 44
C_PRE, C_MLN, C_POSTMIX, C_PREFFN, C_POSTFFN = 45, 53, 61, 69, 77
C_CW, C_CB = 85, 85 + 3 * FT
NCOL = C_CB + FT

M_UNITS, A_UNITS = 8, 7
U_B = 1 + HEADS * (M_UNITS + A_UNITS)
U_OUT = U_B + 2 * KT
U_UP = U_OUT + KT
U_DOWN = U_UP + 2 * FT
N_UNITS = U_DOWN + 3 * KT
HALF_UNITS = N_UNITS - U_B

S_AT = {0: 0, 2: 3 * P, 3: 6 * P, 1: 9 * P}

CHUNKS = [(0, 512), (512, 1024), (1024, 1280)]
WCH = [(0, 322), (322, WIN)]


def m_unit(h, k):
    return 1 + (M_UNITS + A_UNITS) * h + k


def a_unit(h, k):
    return 1 + (M_UNITS + A_UNITS) * h + M_UNITS + k


def unit_tables():
    ring, raw, last = [1], [1], [("if", 0, 2)]
    for h in range(HEADS):
        for k in range(M_UNITS):
            ring.append((2 + k) % 4)
            raw.append(k % 2)
            last.append(("M", h, 3 * k + 2 if k < 4 else 21))
        for k in range(A_UNITS):
            ring.append((3 + k) % 4)
            raw.append(k % 2)
            last.append(("A", h, 3 * k + 2))
    return ring, raw, last


RING, RAW, LAST_GROUP = unit_tables()
for _u in range(2 * HALF_UNITS):
    RING.append(_u % 4)
    RAW.append(_u % 2)


def prev_user(slots, n):
    for m in range(n - 1, -1, -1):
        if slots[m] == slots[n]:
            return m
    return None


def group_tables():
    order = [("if", 0, c) for c in range(3)]
    out = {}
    for h in range(HEADS):
        order += [("M", h, g) for g in range(22)]
        order += [("A", h, g) for g in range(21)]
    count = {"act": 0, "dve": 0}
    last = {}
    for i, key in enumerate(order):
        bank = key[2] % 2
        eng = "dve" if key[0] == "M" and key[2] >= 12 else "act"
        count[eng] += 1
        out[key] = (i, bank, eng, count[eng], last.get(bank))
        last[bank] = (eng, count[eng])
    return out, count


GROUPS, GROUP_COUNT = group_tables()


def lin(f, h):
    if isinstance(h, int):
        return f(h)
    a, b = f(0), f(1)
    assert f(2) == 2 * b - a
    return h * (b - a) + a if b != a else a


def build(nc, w, xt, cols, bvo, sink, outs):
    zo = nc.dram_tensor("zo_scratch", (HEADS, NB, P, DH), F32).ap()
    gs = nc.dram_tensor("gate_scratch", (4 * HEADS, P, T), F32).ap()
    ya_d = nc.dram_tensor("ya_scratch", (D, T), F32).ap()
    ym_d = nc.dram_tensor("ym_scratch", (D, T), F32).ap()
    x1_d = nc.dram_tensor("x1_scratch", (2, KT, P, WIN), F32).ap()
    rows_d = nc.dram_tensor("rows_scratch", (5, 8, T), F32).ap()
    dec_d = nc.dram_tensor("decay_scratch", (8, NB), F32).ap()

    base = ((nc.sbuf_base + 63) // 64) * 64

    def at(name, off, shape, dt=F32):
        return nc.alloc_sbuf_tensor_at(name, shape, dt, offset=base + off)

    ring_h = at("ring_h", 0, [P, KT, 512], F32R)
    ring_l = at("ring_l", 16384, [P, KT, 512], F32R)
    raw = at("raw", 32768, [P, 2, KT, P])
    ht_h = at("ht_h", 40960, [P, KT, T], F32R)
    ht_l = at("ht_l", 81920, [P, KT, T], F32R)
    mq_t = at("mq_t", 122880, [P, 2, T])
    mk_t = at("mk_t", 133120, [P, 2, T])
    v_tok = at("v_tok", 143360, [P, NB, DH + 1])
    h_acc = at("h_acc", 153664, [P, NB, DH])
    c_st = at("c_st", 163904, [P, 2, 2, DH + 1])
    prob = at("prob", 153664, [P, QPG, 3 * P])
    prob_t = at("prob_t", 159808, [P, 3, QPG * P])
    ya_st = at("ya_st", 165952, [HD, QPG, P])
    aq_t = at("aq_t", 168032, [P, 2, T])
    kk_t = at("kk_t", 178272, [P, T])
    av_t = at("av_t", 183392, [P, T])
    ident = at("ident", 188512, [P, P])
    mask = at("mask", 189024, [P, 2, P])
    absrel = at("absrel", 190048, [P, 3 * P])
    tokcol = at("tokcol", 191584, [P, 4, 2 * HEADS * NB])
    urows = at("urows", 192864, [2 * HEADS * NB, P])
    decay = at("decay", 193376, [P, 2 * HEADS * NB])
    pick = at("pick", 193696, [P, 2 * NB])
    slope8 = at("slope8", 193792, [P, 16])
    sinks = at("sinks", 193856, [P, 16])
    bias_vo = at("bias_vo", 194240, [P, 2 * DH])
    ex = at("ex", 196288, [P, 2, P])
    nd = at("nd", 197312, [P, 2, DH + 1])
    wk = at("wk", 199392, [P, 2, DH])
    av_tok = at("av_tok", 197312, [P, NB, HD])
    g_st = at("g_st", 201440, [P, 2, 512])
    o_st = at("o_st", 205536, [P, 2, DH])
    o_ld = at("o_ld", 207584, [P, 2, DH])
    y_st = at("y_st", 209632, [P, 2, 2, P])
    small = at("small", 211680, [P, 64])
    hc = at("hc", 211936, [P, 40])
    HC_AQ, HC_AKV, HC_G, HC_MLN, HC_MQ, HC_MK = 20, 22, 23, 27, 30, 32
    colt = at("colt", 212096, [P, NCOL + 2])
    eps_col = colt[:, NCOL:NCOL + 1]
    one_col = colt[:, NCOL + 1:NCOL + 2]
    xs = at("xs", 122880, [P, KT, T])
    sq0 = at("sq0", 168032, [P, 2, T])
    rs0 = at("rs0", 178272, [P, T])
    ones0 = at("ones0", 196288, [P, P])
    r_if = at("r_if", 153664, [P, T])
    r_li = at("r_li", 158784, [P, T])
    r_f = at("r_f", 163904, [P, T])
    r_b = at("r_b", 169024, [P, T])
    r_m = at("r_m", 174144, [P, T])
    r_u = at("r_u", 179264, [P, T])
    r_mp = at("r_mp", 184384, [P, NB])
    r_dec = at("r_dec", 184448, [P, NB])
    r80 = at("r80", 184512, [P, 4, P])
    r_rst = at("r_rst", 197312, [P, T])
    ya_h = at("ya_h", 40960, [P, KT, WIN], F32R)
    ya_l = at("ya_l", 61504, [P, KT, WIN], F32R)
    ym_h = at("ym_h", 82048, [P, KT, WIN], F32R)
    ym_l = at("ym_l", 102592, [P, KT, WIN], F32R)
    mg_h = at("mg_h", 123136, [P, KT, WIN], F32R)
    mg_l = at("mg_l", 143680, [P, KT, WIN], F32R)
    y_raw = at("y_raw", 164224, [P, 2, WIN])
    g_ld = at("g_ld", 169376, [P, 2, 2, WIN])
    x_ld = at("x_ld", 179648, [P, 2, WIN])
    mt = at("mt", 184800, [P, 2, WIN])
    x1 = at("x1", 40960, [P, KT, WIN])
    f_h = at("f_h", 40960, [P, FT, HALF], F32R)
    f_l = at("f_l", 97280, [P, FT, HALF], F32R)
    h2_h = at("h2_h", 153600, [P, KT, WIN], F32R)
    h2_l = at("h2_l", 174144, [P, KT, WIN], F32R)
    yo = at("yo", 153600, [P, KT, HALF])
    xo = at("xo", 174144, [P, KT, HALF])
    a_s = at("a_s", 194688, [P, 648])
    cv = at("cv", 197312, [P, HALF])
    fs = at("fs", 199872, [P, HALF])
    sq = at("sq", 202432, [P, 2, WIN])
    rs = at("rs", 207584, [P, WIN])
    ones = at("ones", 210176, [P, P])

    ps = nc.alloc_psum_tensor("ps", [P, 8, 512], F32)

    def sem(name):
        return nc.alloc_semaphore(name)

    s_raw = [sem("raw_landed0"), sem("raw_landed1")]
    s_split = sem("unit_split")
    s_used = sem("unit_used")
    s_xl = [sem(f"x_landed{k}") for k in range(KT)]
    s_cols = sem("cols_landed")
    s_cst = sem("consts_dve")
    s_cstp = sem("consts_pool")
    s_sq = sem("sq_ready")
    s_sqm = sem("sq_summed")
    s_rs = sem("rstd_ready")
    s_xn = sem("x_normed")
    s_xh = sem("x_hi")
    s_ht = sem("ht_ready")
    d_done = sem("dense_done")
    ev_act = sem("dense_evac_act")
    ev_dve = sem("dense_evac_dve")
    s_bvo = sem("bias_vo_landed")
    s_os = [sem("o_stored0"), sem("o_stored1")]
    s_g1 = sem("gate_summed")
    s_gs = [sem("gate_stored0"), sem("gate_stored1")]
    p_z = sem("rows_zeroed")
    p_in = sem("rows_split")
    p_abs = sem("abs_f")
    p_ln = sem("softplus")
    p_args = sem("row_args")
    p_out = sem("rows_stored")
    p_80 = sem("rows80_landed")
    p_exp = sem("rows80_exp")
    p_col = sem("cols_transposed")
    p_tc = sem("tokcol_ready")
    m_sel = sem("m_head_columns")
    a_sel = sem("a_next_head_columns")
    m_sc = sem("m_scores")
    m_e = sem("m_exponents")
    m_x = sem("m_exp")
    m_a = sem("m_weights")
    m_wk = sem("m_wk")
    m_nd = sem("m_numden")
    m_qc = sem("m_inter_scaled")
    m_ndx = sem("m_numden_read")
    m_cu = sem("m_update")
    m_c = sem("m_state")
    m_ol = sem("m_o_loaded")
    m_ze = sem("m_o_exp")
    m_ss = sem("m_gated")
    m_rs = sem("m_rstd")
    m_yn = sem("m_normed")
    m_y = sem("m_y_transposed")
    s_ym = sem("ym_stored")
    m_ye = sem("m_y_evacuated")
    a_avt = sem("a_v_transposed")
    a_av = sem("a_v_tokens")
    a_even = sem("a_even_heads")
    a_s_done = sem("a_scores")
    a_m = sem("a_max")
    a_x = sem("a_exp")
    a_p = sem("a_probs")
    a_t = sem("a_probs_transposed")
    a_pt = sem("a_pt_evacuated")
    a_v = sem("a_out")
    a_o = sem("a_out_evacuated")
    s_ya = sem("ya_stored")
    s_yr = [sem("yraw_landed0"), sem("yraw_landed1")]
    b_hi = sem("b_y_hi")
    b_lo = sem("b_y_lo")
    s_gl = [sem("g_landed0"), sem("g_landed1")]
    b_mix = sem("b_mixed")
    b_ml = sem("b_mixed_lo")
    o_ev = sem("o_evacuated")
    n_sq = sem("n_squares")
    n_sum = sem("n_summed")
    n_rs = sem("n_rstd")
    n_rel = sem("n_bank_free")
    s_xr = [sem("x_again0"), sem("x_again1")]
    n_x1 = sem("n_x1")
    s_x1 = sem("x1_stored")
    n_h2 = sem("n_h2_value")
    n_hh = sem("n_h2_hi")
    n_hl = sem("n_h2_lo")
    c_pad = sem("c_pads")
    c_ae = sem("c_a_evacuated")
    c_cv = sem("c_conv")
    c_ge = sem("c_gelu")
    c_fl = sem("c_f_lo")
    e_ev = sem("e_evacuated")
    s_xo = sem("x1_again")
    e_y = sem("e_out_ready")
    s_out = sem("out_stored")

    def used(half, n):
        return half * HALF_UNITS + n - U_B + 1

    def bank_free(eng, key_of, h):
        who = GROUPS[key_of(h if isinstance(h, int) else 1)][4]
        if who is None:
            return
        s = ev_act if who[0] == "act" else ev_dve
        eng.wait_ge(s, lin(lambda k: GROUPS[key_of(k)][4][1], h))

    def seq_of(c):
        return (0, NB_A) if c < NB_A else (NB_A, NB)

    def kblocks(j):
        lo, hi = seq_of(j)
        return list(range(max(lo, j - 1), min(hi, j + 2)))

    def chunk_of(d, i):
        return i if d == 0 else NB - 1 - i

    def fresh(d, i):
        c = chunk_of(d, i)
        lo, hi = seq_of(c)
        return c == (lo if d == 0 else hi - 1)

    def updates(d, i):
        return i + 1 < NB and not fresh(d, i + 1)

    def tcol(q, d, h, c):
        return tokcol[:, q, bass.ds(h * NB + (d * HEADS * NB + c), 1)]

    ctx_block = nc.Block()
    with ctx_block as block:

        @block.sync
        def _(sp):
            for k in range(KT):
                sp.dma_start(xs[:, k, :], xt[k]).then_inc(s_xl[k], 16)
            sp.dma_start(colt[:, 0:NCOL], cols[:]).then_inc(s_cols, 16)
            sp.dma_start(sinks[:], sink[0:1, :].to_broadcast([P, 16])).then_inc(s_cols, 16)

            def load(unit_of, h):
                n1 = unit_of(1 if not isinstance(h, int) else h)
                slot = RAW[n1]
                if prev_user(RAW, n1) is not None:
                    sp.wait_ge(s_split, lin(lambda k: prev_user(RAW, unit_of(k)) + 1, h))
                sp.dma_start(raw[:, slot], w[bass.ds(lin(unit_of, h), 1)]
                             .rearrange("o p (k c) -> (o p) k c", c=P)).then_inc(s_raw[slot], 16)

            def store_gate(k, h):
                for c, (a, b) in enumerate(CHUNKS):
                    pos = (k - 3) * 3 + c
                    sp.wait_ge(s_g1, lin(lambda hh: 12 * hh + pos + 1, h))
                    sp.dma_start(gs[bass.ds(h * 4 + (k - 3), 1), :, a:b].rearrange("o p t -> (o p) t"),
                                 g_st[:, pos % 2, 0:b - a]).then_inc(s_gs[pos % 2], 16)

            def store_o(h):
                for blk in range(NB):
                    sp.wait_ge(ev_dve, lin(lambda k: GROUPS[("M", k, 12 + blk)][3], h))
                    sp.dma_start(zo[bass.ds(h, 1), blk].rearrange("o p t -> (o p) t"),
                                 o_st[:, blk % 2, :]).then_inc(s_os[blk % 2], 16)

            def m_loads(h, gates_h):
                for k in range(M_UNITS):
                    load(lambda hh, k=k: m_unit(hh + 1, k), h)
                    if gates_h is not None and k < 3:
                        store_gate(4 + k, gates_h)
                    if k == 3:
                        if gates_h is not None:
                            sp.wait_ge(ev_dve, lin(lambda hh: NB * (hh + 1), gates_h))
                        sp.dma_start(bias_vo[:], bvo[bass.ds(h + 1, 1), :].to_broadcast([P, 2 * DH])
                                     ).then_inc(s_bvo, 16)

            def a_loads(h, last):
                for k in range(A_UNITS):
                    load(lambda hh, k=k: a_unit(hh, k), h)
                    if k == 1:
                        store_o(h)
                store_gate(3, h)
                if last:
                    for k in range(4, 7):
                        store_gate(k, h)

            load(lambda hh: 0, 0)
            m_first = [lambda k=k: load(lambda hh: m_unit(0, k), 0) for k in range(M_UNITS)]
            m_first[0]()
            sp.dma_start(bias_vo[:], bvo[0:1, :].to_broadcast([P, 2 * DH])).then_inc(s_bvo, 16)
            sp.wait_ge(ev_act, 3)
            sp.wait_ge(p_z, 1)
            for d in range(2):
                sp.dma_start(r_li[32 * d:32 * d + 4, :], r_if[4 * d:4 * d + 4, :]).then_inc(p_in, 16)
                sp.dma_start(r_f[32 * d:32 * d + 4, :], r_if[8 + 4 * d:12 + 4 * d, :]).then_inc(p_in, 16)
            m_first[1]()
            m_first[2]()
            sp.wait_ge(p_args, 1)
            for q, rows in enumerate((r_u, r_li, r_f, r_m, r_b)):
                for d in range(2):
                    sp.dma_start(rows_d[q, 4 * d:4 * d + 4, :], rows[32 * d:32 * d + 4, :]).then_inc(p_out, 16)
            for d in range(2):
                sp.dma_start(dec_d[4 * d:4 * d + 4, :], r_dec[32 * d:32 * d + 4, :]).then_inc(p_out, 16)
            m_first[3]()
            sp.wait_ge(p_out, 12 * 16)
            by_chunk = rows_d.rearrange("q r (c t) -> q (r c) t", t=P)
            sp.dma_start(urows[:], by_chunk[0]).then_inc(p_80, 16)
            sp.dma_start(r80[0:2 * HEADS * NB], by_chunk[1:5].rearrange("q r t -> r q t")).then_inc(p_80, 16)
            sp.dma_start(decay[:], dec_d.rearrange("(o r) c -> o (r c)", o=1).to_broadcast([P, 2 * HEADS * NB])
                         ).then_inc(p_80, 16)
            for k in range(4, M_UNITS):
                m_first[k]()
            with sp.Fori(0, HEADS - 1) as h:
                a_loads(h, False)
                m_loads(h, h)
            a_loads(HEADS - 1, True)

            def load_loop(half, u0, count):
                with sp.Fori(0, count // 2) as i:
                    for s in range(2):
                        n = U_B + half * HALF_UNITS + u0 + s
                        sp.wait_ge(s_split, i * 2 + (n - 1))
                        sp.dma_start(raw[:, RAW[n]], w[bass.ds(i * 2 + (U_B + u0 + s), 1)]
                                     .rearrange("o p (k c) -> (o p) k c", c=P)).then_inc(s_raw[RAW[n]], 16)

            for half in range(2):
                t0 = half * (T - WIN)
                if half == 0:
                    sp.wait_ge(s_split, U_B)
                    sp.wait_ge(s_ya, 16 * HEADS * NB)
                    sp.wait_ge(s_ym, 16 * 2 * HEADS * NB // 2)
                    for s in range(2):
                        sp.wait_ge(s_gs[s], 16 * HEADS * 6)
                for n in range(2 * KT):
                    if n >= 2 or half:
                        sp.wait_ge(b_lo, half * 2 * KT + n - 1)
                    src = (ya_d if n < KT else ym_d).rearrange("(k p) t -> k p t", p=P)[n % KT]
                    sp.dma_start(y_raw[:, n % 2, :], src[:, t0:t0 + WIN]).then_inc(s_yr[n % 2], 16)
                with sp.Fori(0, KT // 2) as i:
                    for s in range(2):
                        for e in range(2):
                            n = U_B + half * HALF_UNITS + 2 * s + e
                            sp.wait_ge(s_split, i * 4 + (n - 1))
                            sp.dma_start(raw[:, RAW[n]], w[bass.ds(i * 4 + (U_B + 2 * s + e), 1)]
                                         .rearrange("o p (k c) -> (o p) k c", c=P)).then_inc(s_raw[RAW[n]], 16)
                        sp.wait_ge(b_mix, i * 2 + (half * (KT + 2) + s + 1))
                        for br in range(2):
                            sp.dma_start(g_ld[:, s, br, :],
                                         gs[bass.ds(i * 4 + (2 * br + s), 1), :, t0:t0 + WIN]
                                         .rearrange("o p t -> (o p) t")).then_inc(s_gl[s], 16)
                load_loop(half, U_OUT - U_B, 2)
                load_loop(half, U_OUT - U_B + 2, KT - 2)
                for k in range(KT):
                    if k >= 2 or half:
                        sp.wait_ge(n_x1, half * KT + k - 1)
                    sp.dma_start(x_ld[:, k % 2, :], xt[k, :, t0:t0 + WIN]).then_inc(s_xr[k % 2], 16)
                for k in range(KT):
                    sp.wait_ge(n_x1, half * KT + k + 1)
                    sp.dma_start(x1_d[half, k], x1[:, k, :]).then_inc(s_x1, 16)
                load_loop(half, U_UP - U_B, 2 * FT)
                load_loop(half, U_DOWN - U_B, 3 * KT)
                sp.wait_ge(s_x1, 16 * KT * (half + 1))
                sp.wait_ge(s_used, used(half, U_DOWN))
                o0 = 2 * half
                sp.dma_start(xo[:], x1_d[half].rearrange("k p t -> p k t")[:, :, o0:o0 + HALF]).then_inc(s_xo, 16)
                for k in range(KT):
                    sp.wait_ge(e_y, half * KT + k + 1)
                    sp.dma_start(outs[k, :, half * HALF:(half + 1) * HALF], yo[:, k, :]).then_inc(s_out, 16)
            sp.wait_ge(s_out, 16 * 2 * KT)

        @block.gpsimd
        def _(pool):
            nc.gpsimd.memset(ident[:], 0.0)
            nc.gpsimd.memset(mask[:], 0.0)
            nc.gpsimd.memset(one_col, 1.0)
            nc.gpsimd.iota(absrel[:], pattern=[[1, 3 * P]], base=-P, channel_multiplier=-1,
                           allow_small_or_imprecise_dtypes=True)
            pool.drain()
            nc.gpsimd.affine_select(out=ident[:], in_=ident[:], compare_op=ALU.not_equal, fill=1.0, base=0,
                                    pattern=[[-1, P]], channel_multiplier=1)
            nc.gpsimd.affine_select(out=mask[:, 0], in_=mask[:, 0], compare_op=ALU.is_ge, fill=-BIG, base=0,
                                    pattern=[[1, P]], channel_multiplier=-1)
            nc.gpsimd.affine_select(out=mask[:, 1], in_=mask[:, 1], compare_op=ALU.is_ge, fill=-BIG, base=0,
                                    pattern=[[-1, P]], channel_multiplier=1).then_inc(s_cstp, 1)

            def split(slot, rslot):
                nc.gpsimd.tensor_tensor(ring_h[:, :, slot * P:(slot + 1) * P], raw[:, rslot],
                                        one_col.unsqueeze(2).to_broadcast([P, KT, P]), ALU.mult)
                pool.drain()
                nc.gpsimd.tensor_tensor(ring_l[:, :, slot * P:(slot + 1) * P], raw[:, rslot],
                                        ring_h[:, :, slot * P:(slot + 1) * P].bitcast(F32),
                                        ALU.subtract).then_inc(s_split, 1)

            def take(unit_of, h):
                n1 = unit_of(1 if not isinstance(h, int) else h)
                rslot, slot = RAW[n1], RING[n1]
                pool.wait_ge(s_raw[rslot], lin(lambda k: 16 * RAW[:unit_of(k) + 1].count(rslot), h))
                if prev_user(RING, n1) is not None:
                    pool.wait_ge(d_done, lin(lambda k: GROUPS[LAST_GROUP[prev_user(RING, unit_of(k))]][0] + 1, h))
                split(slot, rslot)

            take(lambda k: 0, 0)
            for u in range(M_UNITS):
                take(lambda k, u=u: m_unit(k, u), 0)
            with pool.Fori(0, HEADS - 1) as h:
                for u in range(A_UNITS):
                    take(lambda k, u=u: a_unit(k, u), h)
                for u in range(M_UNITS):
                    take(lambda k, u=u: m_unit(k + 1, u), h)
            for u in range(A_UNITS):
                take(lambda k, u=u: a_unit(k, u), HEADS - 1)
            for n in range(U_B, U_B + 4):
                take(lambda k, n=n: n, 0)
            with pool.Fori(0, (2 * HALF_UNITS - 4) // 4) as i:
                for s in range(4):
                    n = U_B + 4 + s
                    pool.wait_ge(s_raw[RAW[n]], i * 32 + 16 * RAW[:n + 1].count(RAW[n]))
                    pool.wait_ge(s_used, i * 4 + s + 1)
                    split(RING[n], RAW[n])

        def halves_act(act):
            for half in range(2):
                for n in range(2 * KT):
                    act.wait_ge(s_yr[n % 2], 16 * (half * KT + n // 2 + 1))
                    nc.scalar.activation((ya_h if n < KT else ym_h)[:, n % KT], y_raw[:, n % 2], ACT.Identity
                                         ).then_inc(b_hi, 1)
                for k in range(KT):
                    act.wait_ge(s_used, used(half, U_OUT + k))
                    for c, (a, b) in enumerate(WCH):
                        last = nc.scalar.activation(x1[:, k, a:b], ps[:, 2 * (k % 4) + c, 0:b - a], ACT.Copy)
                    last.then_inc(o_ev, 1)
                norm_act(act, half * 3 + 0, o_ev, half * KT, x1, WIN, D)
                norm_act(act, half * 3 + 1, n_x1, half * KT, x1, WIN, D)
                for k in range(KT):
                    act.wait_ge(n_h2, half * KT + k + 1)
                    nc.scalar.activation(h2_h[:, k], x1[:, k], ACT.Identity).then_inc(n_hh, 1)
                with act.Fori(0, FT // 2) as i:
                    for s in range(2):
                        act.wait_ge(s_used, i * 4 + used(half, U_UP + 2 * s))
                        act.wait_ge(c_pad, half + 1)
                        act.wait_ge(c_cv, i * 2 + (half * (FT + 1) + s + 1))
                        if half == 0:
                            pieces = [(0, 0, 256, 1), (0, 256, 322, 258), (1, 322, WIN, 324)]
                        else:
                            pieces = [(0, 0, 322, 0), (1, 322, WIN, 322)]
                        for c, a, b, o in pieces:
                            w0 = WCH[c][0]
                            last = nc.scalar.activation(a_s[:, o:o + b - a], ps[:, 4 * s + c, a - w0:b - w0], ACT.Copy)
                        last.then_inc(c_ae, 1)
                        act.wait_ge(c_cv, i * 2 + (half * (FT + 1) + 1 + s + 1))
                        act.wait_ge(c_fl, i * 2 + (half * (FT + 2) + s + 2))
                        nc.scalar.activation(fs[:], cv[:], ACT.Gelu_apprx_tanh).then_inc(c_ge, 1)
                for k in range(KT):
                    act.wait_ge(s_used, used(half, U_DOWN + 3 * k + 2))
                    for c in range(2):
                        last = nc.scalar.activation(yo[:, k, c * 320:(c + 1) * 320], ps[:, 2 * (k % 4) + c, 0:320],
                                                    ACT.Copy)
                    last.then_inc(e_ev, 1)
                norm_act(act, half * 3 + 2, e_ev, half * KT, yo, HALF, D)

        def norm_act(act, n, ready, ready0, src, width, dim):
            for k in range(KT):
                act.wait_ge(ready, ready0 + k + 1)
                if k >= 2 or n:
                    act.wait_ge(n_sum, n * KT + k - 1)
                nc.scalar.activation(sq[:, k % 2, 0:width], src[:, k], ACT.Square).then_inc(n_sq, 1)
            act.wait_ge(n_sum, (n + 1) * KT)
            for c in range(2):
                a, b = WCH[c] if width == WIN else (320 * c, 320 * c + 320)
                nc.scalar.activation(rs[:, a:b], ps[:, 6 + c, 0:b - a], ACT.Ln, bias=eps_col, scale=1.0 / dim)
            act.drain()
            nc.scalar.activation(rs[:, 0:width], rs[:, 0:width], ACT.Exp, scale=-0.5).then_inc(n_rs, 1)

        @block.scalar
        def _(act):
            nc.scalar.preload_act_table_set("natural_log_exp_and_others")
            for k in range(KT):
                act.wait_ge(s_xl[k], 16)
                if k >= 2:
                    act.wait_ge(s_sqm, k - 1)
                nc.scalar.activation(sq0[:, k % 2], xs[:, k], ACT.Square).then_inc(s_sq, 1)
            act.wait_ge(s_sqm, KT)
            act.wait_ge(s_cst, 1)
            for c, (a, b) in enumerate(CHUNKS):
                nc.scalar.activation(rs0[:, a:b], ps[:, 2 + c, 0:b - a], ACT.Ln, bias=eps_col, scale=1.0 / D)
            act.drain()
            nc.scalar.activation(rs0[:], rs0[:], ACT.Exp, scale=-0.5).then_inc(s_rs, 1)
            for k in range(KT):
                act.wait_ge(s_xn, k + 1)
                nc.scalar.activation(ht_h[:, k], xs[:, k], ACT.Identity).then_inc(s_xh, 1)

            def evac(key_of, h, dst, bias, scale=1.0, func=ACT.Identity, rows=slice(0, P)):
                key1 = key_of(h if isinstance(h, int) else 1)
                a, b = CHUNKS[key1[2] % 3]
                src = ps[rows, key1[2] % 2, 0:b - a]
                act.wait_ge(d_done, lin(lambda k: GROUPS[key_of(k)][0] + 1, h))
                return nc.scalar.activation(dst, src, func, bias=bias, scale=scale)

            for c, (a, b) in enumerate(CHUNKS):
                evac(lambda k, c=c: ("if", 0, c), 0, r_if[:, a:b], colt[:, C_IF:C_IF + 1]).then_inc(ev_act, 1)

            def evac_m(g, h, shift=0):
                a, b = CHUNKS[g % 3]
                u = g // 3
                dst = (mq_t if u < 2 else mk_t)[:, u % 2, a:b]
                col = (HC_MQ if u < 2 else HC_MK) + u % 2
                if g == 0:
                    act.wait_ge(a_sel, lin(lambda k: k + shift + 1, h))
                evac(lambda k: ("M", k + shift, g), h, dst, hc[:, col:col + 1],
                     1.0 if u < 2 else DH ** -0.5).then_inc(ev_act, 1)

            for g in range(3):
                evac_m(g, 0)
            act.wait_ge(p_abs, 1)
            nc.scalar.activation(r_b[0:36], r_b[0:36], ACT.Exp, scale=-1.0)
            act.drain()
            nc.scalar.activation(r_b[0:36], r_b[0:36], ACT.Ln, bias=1.0).then_inc(p_ln, 1)
            for g in range(3, 12):
                evac_m(g, 0)
            act.wait_ge(p_80, 48)
            nc.scalar.activation(r80[0:80, 1:4], r80[0:80, 1:4], ACT.Exp)
            nc.scalar.activation(decay[:], decay[:], ACT.Exp).then_inc(p_exp, 1)

            def evac_a(g, h):
                a, b = CHUNKS[g % 3]
                u = g // 3
                if u < 2:
                    evac(lambda k: ("A", k, g), h, aq_t[:, u, a:b], hc[:, HC_AQ + u:HC_AQ + u + 1]
                         ).then_inc(ev_act, 1)
                elif u == 2:
                    for r in range(2):
                        evac(lambda k: ("A", k, g), h, kk_t[r * HD:(r + 1) * HD, a:b],
                             hc[0:HD, HC_AKV:HC_AKV + 1], rows=slice(0, HD))
                    evac(lambda k: ("A", k, g), h, av_t[HD:P, a:b], hc[HD:P, HC_AKV:HC_AKV + 1],
                         rows=slice(HD, P)).then_inc(ev_act, 1)
                else:
                    pos = g - 9
                    if pos >= 2:
                        act.wait_ge(s_gs[pos % 2], lin(lambda k: 16 * (6 * k + pos // 2), h))
                    evac(lambda k: ("A", k, g), h, g_st[:, pos % 2, 0:b - a],
                         hc[:, HC_G + u - 3:HC_G + u - 2], -1.0, ACT.Exp).then_inc(ev_act, 1)

            def mlstm(h):
                act.wait_ge(m_sel, lin(lambda k: k + 1, h))
                for i in range(NB):
                    act.wait_ge(m_e, lin(lambda k: NB * k + i + 1, h))
                    nc.scalar.activation(ex[:], ex[:], ACT.Exp).then_inc(m_x, 1)
                    if i >= 5:
                        act.wait_ge(m_ol, lin(lambda k: 32 * (5 * k + i - 4), h))
                        nc.scalar.activation(o_ld[:], o_ld[:], ACT.Exp, scale=-1.0).then_inc(m_ze, 1)
                    evac_a(2 * i, h)
                    inter = [d for d in range(2) if not fresh(d, i)]
                    if inter:
                        act.wait_ge(m_nd, lin(lambda k: NB * k + i + 1, h))
                        for d in inter:
                            last = nc.scalar.activation(nd[:, d], ps[:, 3 + 2 * d, 0:DH + 1], ACT.Copy,
                                                        scale=hc[:, d * NB + chunk_of(d, i):d * NB + chunk_of(d, i) + 1])
                        last.then_inc(m_qc, 1)
                    if i > 5:
                        finish_y(i - 1, h)
                    evac_a(2 * i + 1, h)
                    if i >= 5:
                        rstd(i, h)
                    if i >= 4 and i < NB - 1:
                        load_o(i + 1, h)
                evac_a(20, h)
                finish_y(NB - 1, h)

            def load_o(i, h):
                if i > 5:
                    act.wait_ge(m_yn, lin(lambda k: 5 * k + i - 5, h))
                for s in range(2):
                    act.wait_ge(s_os[s], lin(lambda k: 16 * 5 * (k + 1), h))
                for d in range(2):
                    act.dma_start(o_ld[:, d, :], zo[bass.ds(h, 1), chunk_of(d, i)]
                                  .rearrange("o p t -> (o p) t")).then_inc(m_ol, 16)

            def rstd(i, h):
                act.wait_ge(m_ss, lin(lambda k: 5 * k + i - 4, h))
                nc.scalar.activation(small[:, 8:10], small[:, 6:8], ACT.Ln, bias=eps_col, scale=1.0 / DH)
                act.drain()
                nc.scalar.activation(small[:, 10:12], small[:, 8:10], ACT.Exp, scale=-0.5).then_inc(m_rs, 1)

            def finish_y(i, h):
                act.wait_ge(m_y, lin(lambda k: 5 * k + i - 4, h))
                if i > 5:
                    act.wait_ge(s_ym, lin(lambda k: 32 * (5 * k + i - 5), h))
                for dt in range(2):
                    last = nc.scalar.activation(y_st[:, dt], ps[:, 7, 256 * dt:256 * dt + 256]
                                                .rearrange("p (c t) -> p c t", c=2), ACT.Copy,
                                                scale=hc[:, HC_MLN + dt:HC_MLN + dt + 1])
                last.then_inc(m_ye, 1)
                act.wait_ge(m_ye, lin(lambda k: 5 * k + i - 4, h))
                for d in range(2):
                    c = chunk_of(d, i)
                    act.dma_start(ym_d.rearrange("(h e p) t -> h p e t", e=2, p=P)[bass.ds(h, 1), :, :, c * P:(c + 1) * P]
                                  .rearrange("o p e t -> (o p) e t"), y_st[:, :, d, :]).then_inc(s_ym, 16)

            def exps(j, h):
                act.wait_ge(a_m, lin(lambda k: NB * k + j + 1, h))
                kb = kblocks(j)
                a, b = (kb[0] - j + 1) * P, (kb[-1] - j + 2) * P
                for r in range(QPG):
                    nc.scalar.activation(prob[:, r, a:b], prob[:, r, a:b], ACT.Exp, bias=small[:, 20 + r:21 + r],
                                         scale=HD ** -0.5, accum_out=small[:, 24 + r:25 + r])
                nc.scalar.activation(small[:, 32:36], small[:, 28:32], ACT.Exp).then_inc(a_x, 1)

            def evac_pt(j, h):
                act.wait_ge(a_t, lin(lambda k: NB * k + j + 1, h))
                for n in range(len(kblocks(j))):
                    last = nc.scalar.activation(prob_t[:, n], ps[:, 5 + n, :], ACT.Copy)
                last.then_inc(a_pt, 1)

            def evac_o(j, h):
                act.wait_ge(a_v, lin(lambda k: NB * k + j + 1, h))
                if j > 0:
                    act.wait_ge(s_ya, lin(lambda k: 16 * (NB * k + j), h))
                nc.scalar.activation(ya_st[:], ps[0:HD, 5, :].rearrange("p (r t) -> p r t", r=QPG),
                                     ACT.Copy).then_inc(a_o, 1)
                act.wait_ge(a_o, lin(lambda k: NB * k + j + 1, h))
                act.dma_start(ya_d.rearrange("(h r p) t -> h p r t", r=QPG, p=HD)[bass.ds(h, 1), :, :, j * P:(j + 1) * P]
                              .rearrange("o p r t -> (o p) r t"), ya_st[:]).then_inc(s_ya, 16)

            def attend(h, dense):
                exps(0, h)
                for j in range(NB):
                    if dense and 2 * j < 12:
                        evac_m(2 * j, h, 1)
                    evac_pt(j, h)
                    if j + 1 < NB:
                        exps(j + 1, h)
                    if dense and 2 * j + 1 < 12:
                        evac_m(2 * j + 1, h, 1)
                    evac_o(j, h)
                for s in range(2):
                    act.wait_ge(s_gs[s], lin(lambda k: 16 * 6 * (k + 1), h))
                act.wait_ge(s_ym, lin(lambda k: 160 * (k + 1), h))

            with act.Fori(0, HEADS - 1) as h:
                mlstm(h)
                attend(h, True)
            mlstm(HEADS - 1)
            attend(HEADS - 1, False)
            halves_act(act)

        @block.vector
        def _(dve):
            V = nc.vector
            V.memset(ones0[:], 1.0)
            V.memset(eps_col, EPS).then_inc(s_cst, 1)
            for r in range(16):
                V.memset(slope8[:, r:r + 1], -(2.0 ** (-8.0 * (r + 1) / 16)) * HD ** 0.5)
            dve.wait_ge(s_cstp, 1)
            V.scalar_tensor_tensor(absrel[:], absrel[:], -1.0, absrel[:], ALU.mult, ALU.max)
            dve.drain()
            V.tensor_scalar(g_st[:, 0, 0:3 * P], absrel[:], float(P), BIG, ALU.is_gt, ALU.mult)
            dve.drain()
            V.tensor_tensor(absrel[:], absrel[:], g_st[:, 0, 0:3 * P], ALU.max)
            dve.wait_ge(s_cols, 32)
            V.tensor_scalar(colt[:, C_MK:C_MK + 8], colt[:, C_MK:C_MK + 8], DH ** -0.5, None, ALU.mult)
            V.tensor_scalar(colt[:, C_G:C_G + 16], colt[:, C_G:C_G + 16], -1.0, None, ALU.mult)
            dve.drain()
            V.tensor_copy(hc[:, HC_MQ:HC_MQ + 2], colt[:, C_MQ:C_MQ + 2])
            V.tensor_copy(hc[:, HC_MK:HC_MK + 2], colt[:, C_MK:C_MK + 2]).then_inc(a_sel, 1)
            dve.wait_ge(s_rs, 1)
            for k in range(KT + 1):
                if k < KT:
                    V.scalar_tensor_tensor(xs[:, k], xs[:, k], colt[:, C_PRE + k:C_PRE + k + 1], rs0[:],
                                           ALU.mult, ALU.mult).then_inc(s_xn, 1)
                if k > 0:
                    dve.wait_ge(s_xh, k)
                    V.tensor_tensor(ht_l[:, k - 1], xs[:, k - 1], ht_h[:, k - 1].bitcast(F32),
                                    ALU.subtract).then_inc(s_ht, 1)
            dve.drain()
            V.memset(v_tok[:, :, DH:DH + 1], 1.0)
            V.memset(r_li[0:36], 0.0)
            V.memset(r_f[0:36], 0.0)
            V.memset(r_m[0:36], 0.0)
            V.memset(r_mp[0:36], 0.0)
            dve.drain()
            V.memset(r_rst[0:36], 1.0).then_inc(p_z, 1)
            dve.drain()
            V.memset(r_rst[0:4].rearrange("p (c t) -> p c t", t=P)[:, :, 0:1], 0.0)
            V.memset(r_rst[32:36].rearrange("p (c t) -> p c t", t=P)[:, :, P - 1:P], 0.0)
            dve.wait_ge(p_in, 64)
            V.tensor_scalar(r_f[0:36], r_f[0:36], FORGET_BIAS, None, ALU.add)
            dve.drain()
            V.scalar_tensor_tensor(r_b[0:36], r_f[0:36], -1.0, r_f[0:36], ALU.mult, ALU.max).then_inc(p_abs, 1)
            dve.wait_ge(p_ln, 1)
            V.scalar_tensor_tensor(r_f[0:36], r_f[0:36], 0.0, r_b[0:36], ALU.min, ALU.subtract)
            dve.drain()
            V.tensor_tensor_scan(r_b[0:4], r_rst[0:4], r_f[0:4], 0.0, ALU.mult, ALU.add)
            V.tensor_tensor_scan(r_b[32:36][:, ::-1], r_rst[32:36][:, ::-1], r_f[32:36][:, ::-1], 0.0,
                                 ALU.mult, ALU.add)
            for a, b in ((0, SEQ_A), (SEQ_A, T)):
                V.tensor_tensor_scan(r_m[0:4, a:b], r_f[0:4, a:b], r_li[0:4, a:b], 0.0, ALU.add, ALU.max)
                V.tensor_tensor_scan(r_m[32:36, a:b][:, ::-1], r_f[32:36, a:b][:, ::-1],
                                     r_li[32:36, a:b][:, ::-1], 0.0, ALU.add, ALU.max)
            dve.drain()
            mch = r_m[:, :].rearrange("p (c t) -> p c t", t=P)
            for lo, hi in ((0, NB_A), (NB_A, NB)):
                V.tensor_copy(r_mp[0:4, lo + 1:hi].unsqueeze(2), mch[0:4, lo:hi - 1, P - 1:P])
                V.tensor_copy(r_mp[32:36, lo:hi - 1].unsqueeze(2), mch[32:36, lo + 1:hi, 0:1])
            V.tensor_tensor(r_u[0:36], r_b[0:36], r_m[0:36], ALU.subtract)
            V.tensor_tensor(r_li[0:36], r_li[0:36], r_b[0:36], ALU.subtract)
            dve.drain()
            uch = r_u[:, :].rearrange("p (c t) -> p c t", t=P)
            ulast = small[:, 40:50]
            V.tensor_copy(ulast[0:36].unsqueeze(2), uch[0:36, :, P - 1:P])
            dve.drain()
            V.tensor_copy(ulast[32:36].unsqueeze(2), uch[32:36, :, 0:1])
            dve.drain()
            V.tensor_tensor(r_dec[0:36], ulast[0:36], r_mp[0:36], ALU.add)
            V.tensor_tensor(r_f[0:36].rearrange("p (c t) -> p c t", t=P), uch[0:36],
                            r_mp[0:36].unsqueeze(2).to_broadcast([36, NB, P]), ALU.add)
            V.tensor_tensor(r_b[0:36].rearrange("p (c t) -> p c t", t=P),
                            r_li[0:36].rearrange("p (c t) -> p c t", t=P),
                            ulast[0:36].unsqueeze(2).to_broadcast([36, NB, P]), ALU.add)
            V.tensor_scalar(r_m[0:36], r_m[0:36], -1.0, None, ALU.mult).then_inc(p_args, 1)

            def evac_vo(blk, h, shift=0):
                hh = h
                dve.wait_ge(d_done, lin(lambda k: GROUPS[("M", k + shift, 12 + blk)][0] + 1, hh))
                if blk == 0:
                    dve.wait_ge(s_bvo, lin(lambda k: 16 * (k + shift + 1), hh))
                if blk >= 2:
                    dve.wait_ge(s_os[blk % 2], lin(lambda k: 16 * (5 * (k + shift) + blk // 2), hh))
                elif shift:
                    dve.wait_ge(s_os[blk % 2], lin(lambda k: 16 * 5 * (k + shift), hh))
                bank = (12 + blk) % 2
                V.tensor_tensor(v_tok[:, blk, 0:DH], ps[:, bank, 0:DH], bias_vo[:, 0:DH], ALU.add)
                V.tensor_tensor(o_st[:, blk % 2], ps[:, bank, DH:2 * DH], bias_vo[:, DH:2 * DH],
                                ALU.add).then_inc(ev_dve, 1)

            for blk in range(NB):
                evac_vo(blk, 0)
            dve.wait_ge(p_col, 1)
            V.tensor_copy(tokcol[:], ps[:, 2, 0:320].rearrange("p (q r) -> p q r", q=4)).then_inc(p_tc, 1)

            def evac_gate(g, h):
                if g < 9:
                    return
                a, b = CHUNKS[g % 3]
                pos = g - 9
                dve.wait_ge(ev_act, lin(lambda k: GROUPS[("A", k, g)][3], h))
                st = g_st[:, pos % 2, 0:b - a]
                V.tensor_scalar(st, st, 1.0, None, ALU.add)
                dve.drain()
                V.reciprocal(st, st).then_inc(s_g1, 1)

            def mlstm(h):
                dve.drain()
                for d in range(2):
                    V.tensor_copy(pick[0:80, d * NB:(d + 1) * NB],
                                  ident[0:80, bass.ds(h * NB + d * HEADS * NB, NB)])
                    V.tensor_copy(hc[:, d * NB:(d + 1) * NB],
                                  tokcol[:, 1, bass.ds(h * NB + d * HEADS * NB, NB)])
                V.tensor_copy(hc[:, HC_AQ:HC_AQ + 2], colt[:, bass.ds(h * 2 + C_AQ, 2)])
                V.tensor_copy(hc[:, HC_AKV:HC_AKV + 1], colt[:, bass.ds(h + C_AKV, 1)])
                V.tensor_copy(hc[:, HC_G:HC_G + 4], colt[:, bass.ds(h * 4 + C_G, 4)])
                V.tensor_copy(hc[:, HC_MLN:HC_MLN + 2], colt[:, bass.ds(h * 2 + C_MLN, 2)]).then_inc(m_sel, 1)
                for i in range(NB):
                    step = lambda k, i=i: NB * k + i + 1
                    ch = [chunk_of(d, i) for d in range(2)]
                    dve.wait_ge(m_sc, lin(step, h))
                    for d in range(2):
                        last = V.scalar_tensor_tensor(ex[:, d], ps[:, 2, 256 * d + P:256 * d + 2 * P],
                                                      tcol(0, d, h, ch[d]), mask[:, d], ALU.add, ALU.add)
                    last.then_inc(m_e, 1)
                    for d in range(2):
                        last = V.tensor_scalar(wk[:, d], ps[:, 7, 256 * d:256 * d + 256], tcol(3, d, h, ch[d]),
                                               None, ALU.mult)
                    last.then_inc(m_wk, 1)
                    dve.wait_ge(m_x, lin(step, h))
                    V.tensor_tensor(ex[:], ex[:], ps[:, 2, :].rearrange("p (d e t) -> p d e t", d=2, e=2)[:, :, 0, :],
                                    ALU.mult).then_inc(m_a, 1)
                    evac_gate(2 * i - 1, h)
                    dve.wait_ge(m_nd, lin(step, h))
                    if any(not fresh(d, i) for d in range(2)):
                        dve.wait_ge(m_qc, lin(lambda k: 9 * k + i, h))
                    for d in range(2):
                        if fresh(d, i):
                            last = V.tensor_copy(nd[:, d], ps[:, 4 + 2 * d, 0:DH + 1])
                        else:
                            last = V.tensor_tensor(nd[:, d], nd[:, d], ps[:, 4 + 2 * d, 0:DH + 1], ALU.add)
                    last.then_inc(m_ndx, 1)
                    dve.drain()
                    V.scalar_tensor_tensor(small[:, 4:6], nd[:, :, DH], -1.0, nd[:, :, DH], ALU.mult, ALU.max)
                    dve.drain()
                    for d in range(2):
                        V.tensor_tensor(small[:, d:d + 1], small[:, 4 + d:5 + d], tcol(2, d, h, ch[d]), ALU.max)
                    dve.drain()
                    V.reciprocal(small[:, 2:4], small[:, 0:2])
                    dve.drain()
                    for d in range(2):
                        if i < 5:
                            V.tensor_scalar(h_acc[:, ch[d]], nd[:, d, 0:DH], small[:, 2 + d:3 + d], None, ALU.mult)
                        else:
                            V.scalar_tensor_tensor(h_acc[:, ch[d]], nd[:, d, 0:DH], small[:, 2 + d:3 + d],
                                                   h_acc[:, ch[d]], ALU.mult, ALU.add)
                    evac_gate(2 * i, h)
                    if i + 1 < NB:
                        dve.wait_ge(m_cu, lin(lambda k: 9 * k + i + 1, h))
                        for d in range(2):
                            if not updates(d, i):
                                continue
                            for dt in range(2):
                                src = ps[:, 3 + 2 * d + dt, 0:DH + 1]
                                if fresh(d, i):
                                    last = V.tensor_copy(c_st[:, d, dt], src)
                                else:
                                    last = V.scalar_tensor_tensor(
                                        c_st[:, d, dt], c_st[:, d, dt],
                                        decay[:, bass.ds(h * NB + (d * HEADS * NB + ch[d]), 1)], src,
                                        ALU.mult, ALU.add)
                        last.then_inc(m_c, 1)
                    if i >= 5:
                        dve.wait_ge(m_ze, lin(lambda k: 5 * k + i - 4, h))
                        V.tensor_scalar(o_ld[:], o_ld[:], 1.0, None, ALU.add)
                        dve.drain()
                        V.reciprocal(o_ld[:], o_ld[:])
                        dve.drain()
                        for d in range(2):
                            V.tensor_tensor(h_acc[:, ch[d]], h_acc[:, ch[d]], o_ld[:, d], ALU.mult)
                        dve.drain()
                        for d in range(2):
                            last = V.scalar_tensor_tensor(o_ld[:, d], h_acc[:, ch[d]], 1.0, h_acc[:, ch[d]],
                                                          ALU.mult, ALU.mult, accum_out=small[:, 6 + d:7 + d])
                        last.then_inc(m_ss, 1)
                        dve.wait_ge(m_rs, lin(lambda k: 5 * k + i - 4, h))
                        for d in range(2):
                            last = V.tensor_scalar(h_acc[:, ch[d]], h_acc[:, ch[d]], small[:, 10 + d:11 + d],
                                                   None, ALU.mult)
                        last.then_inc(m_yn, 1)
                evac_gate(19, h)
                evac_gate(20, h)

            def soften(j, h):
                kb = kblocks(j)
                a, b = (kb[0] - j + 1) * P, (kb[-1] - j + 2) * P
                dve.wait_ge(a_s_done, lin(lambda k: NB * k + j + 1, h))
                flat = ps[:, 2:5, :].rearrange("p b t -> p (b t)")
                if j > 0:
                    dve.wait_ge(a_t, lin(lambda k: NB * k + j, h))
                for r in range(QPG):
                    V.scalar_tensor_tensor(prob[:, r, a:b], absrel[:, a:b], slope8[:, bass.ds(h * QPG + r, 1)],
                                           flat[:, S_AT[r] + a:S_AT[r] + b], ALU.mult, ALU.add)
                dve.drain()
                V.tensor_reduce(small[:, 16:20], prob[:, :, a:b], AX.X, ALU.max)
                dve.drain()
                V.scalar_tensor_tensor(small[:, 16:20], sinks[:, bass.ds(h * QPG, QPG)], HD ** 0.5, small[:, 16:20],
                                       ALU.mult, ALU.max)
                dve.drain()
                V.tensor_scalar(small[:, 20:24], small[:, 16:20], -(HD ** -0.5), None, ALU.mult)
                dve.drain()
                V.tensor_tensor(small[:, 28:32], sinks[:, bass.ds(h * QPG, QPG)], small[:, 20:24],
                                ALU.add).then_inc(a_m, 1)
                dve.wait_ge(a_x, lin(lambda k: NB * k + j + 1, h))
                V.tensor_tensor(small[:, 36:40], small[:, 32:36], small[:, 24:28], ALU.add)
                dve.drain()
                V.reciprocal(small[:, 36:40], small[:, 36:40])
                dve.drain()
                for r in range(QPG):
                    last = V.tensor_scalar(prob[:, r, a:b], prob[:, r, a:b], small[:, 36 + r:37 + r], None, ALU.mult)
                last.then_inc(a_p, 1)

            def next_columns(h):
                V.tensor_copy(hc[:, HC_MQ:HC_MQ + 2], colt[:, bass.ds(h * 2 + C_MQ, 2)])
                V.tensor_copy(hc[:, HC_MK:HC_MK + 2], colt[:, bass.ds(h * 2 + C_MK, 2)]).then_inc(a_sel, 1)

            def attend(h, dense):
                dve.drain()
                if dense:
                    next_columns(h + 1)
                dve.wait_ge(a_avt, lin(lambda k: k + 1, h))
                for n in range(2):
                    last = V.tensor_copy(av_tok[:, 5 * n:5 * n + 5], ps[:, 6 + n, 0:320]
                                         .rearrange("p (c e) -> p c e", c=5))
                last.then_inc(a_av, 1)
                dve.wait_ge(m_y, lin(lambda k: 5 * (k + 1), h))
                soften(0, h)
                for j in range(NB):
                    if dense and 2 * j >= 12:
                        evac_vo(2 * j - 12, h, 1)
                    if j + 1 < NB:
                        soften(j + 1, h)
                    if dense and 2 * j + 1 >= 12:
                        evac_vo(2 * j + 1 - 12, h, 1)
                if dense:
                    evac_vo(8, h, 1)
                    evac_vo(9, h, 1)
                dve.wait_ge(s_ya, lin(lambda k: 16 * NB * (k + 1), h))
                dve.wait_ge(m_ye, lin(lambda k: 5 * (k + 1), h))

            with dve.Fori(0, HEADS - 1) as h:
                mlstm(h)
                attend(h, True)
            mlstm(HEADS - 1)
            attend(HEADS - 1, False)

            dve.wait_ge(a_v, NB * HEADS)
            V.memset(ones[:], 1.0)
            dve.drain()
            for half in range(2):
                for n in range(2 * KT):
                    dve.wait_ge(b_hi, half * 2 * KT + n + 1)
                    dst, hi = (ya_l, ya_h) if n < KT else (ym_l, ym_h)
                    V.tensor_tensor(dst[:, n % KT], y_raw[:, n % 2], hi[:, n % KT].bitcast(F32),
                                    ALU.subtract).then_inc(b_lo, 1)
                dve.sem_inc(b_mix, 2)
                with dve.Fori(0, KT // 2) as i:
                    for s in range(2):
                        dve.wait_ge(s_gl[s], i * 32 + (half * 16 * KT + 32))
                        dve.wait_ge(s_used, i * 4 + used(half, U_B + 2 * s + 1))
                        for c, (a, b) in enumerate(WCH):
                            V.tensor_tensor(g_ld[:, s, 0, a:b], g_ld[:, s, 0, a:b], ps[:, 4 * s + c, 0:b - a], ALU.mult)
                            V.tensor_tensor(g_ld[:, s, 1, a:b], g_ld[:, s, 1, a:b], ps[:, 4 * s + 2 + c, 0:b - a],
                                            ALU.mult)
                        dve.drain()
                        V.tensor_tensor(mt[:, s], g_ld[:, s, 0], g_ld[:, s, 1], ALU.add).then_inc(b_mix, 1)
                        dve.drain()
                        V.tensor_scalar(mg_h[:, bass.ds(i * 2 + s, 1), :].rearrange("p o t -> p (o t)"), mt[:, s],
                                        1.0, None, ALU.mult)
                        dve.drain()
                        V.tensor_tensor(mg_l[:, bass.ds(i * 2 + s, 1), :].rearrange("p o t -> p (o t)"), mt[:, s],
                                        mg_h[:, bass.ds(i * 2 + s, 1), :].rearrange("p o t -> p (o t)").bitcast(F32),
                                        ALU.subtract).then_inc(b_ml, 1)
                dve.wait_ge(n_rs, half * 3 + 1)
                for k in range(KT):
                    V.scalar_tensor_tensor(x1[:, k], x1[:, k], colt[:, C_POSTMIX + k:C_POSTMIX + k + 1], rs[:],
                                           ALU.mult, ALU.mult)
                    dve.drain()
                    dve.wait_ge(s_xr[k % 2], 16 * (half * KT // 2 + k // 2 + 1))
                    V.tensor_tensor(x1[:, k], x1[:, k], x_ld[:, k % 2], ALU.add).then_inc(n_x1, 1)
                dve.wait_ge(n_rs, half * 3 + 2)
                dve.wait_ge(s_x1, 16 * KT * (half + 1))
                for k in range(KT + 1):
                    if k < KT:
                        V.scalar_tensor_tensor(x1[:, k], x1[:, k], colt[:, C_PREFFN + k:C_PREFFN + k + 1], rs[:],
                                               ALU.mult, ALU.mult).then_inc(n_h2, 1)
                    if k > 0:
                        dve.wait_ge(n_hh, half * KT + k)
                        V.tensor_tensor(h2_l[:, k - 1], x1[:, k - 1], h2_h[:, k - 1].bitcast(F32),
                                        ALU.subtract).then_inc(n_hl, 1)
                dve.drain()
                if half == 0:
                    V.memset(a_s[:, 0:1], 0.0)
                    V.memset(a_s[:, 257:258], 0.0).then_inc(c_pad, 1)
                    segments = [(0, 256, 0), (256, HALF, 257)]
                else:
                    V.memset(a_s[:, WIN:WIN + 1], 0.0).then_inc(c_pad, 1)
                    segments = [(0, HALF, 1)]
                dve.drain()
                dve.sem_inc(c_cv, 1)
                dve.sem_inc(c_fl, 2)
                with dve.Fori(0, FT // 2) as i:
                    for s in range(2):
                        dve.wait_ge(c_ae, i * 2 + (half * FT + s + 1))
                        col = lambda n: colt[:, bass.ds(i * 2 + (C_CW + n * FT + s), 1)]
                        for a, b, o in segments:
                            V.tensor_scalar(cv[:, a:b], a_s[:, o + 1:o + 1 + b - a], col(1), col(3), ALU.mult, ALU.add)
                        dve.drain()
                        for a, b, o in segments:
                            V.scalar_tensor_tensor(cv[:, a:b], a_s[:, o:o + b - a], col(0), cv[:, a:b],
                                                   ALU.mult, ALU.add)
                        dve.drain()
                        for a, b, o in segments:
                            last = V.scalar_tensor_tensor(cv[:, a:b], a_s[:, o + 2:o + 2 + b - a], col(2), cv[:, a:b],
                                                          ALU.mult, ALU.add)
                        last.then_inc(c_cv, 1)
                        dve.wait_ge(c_ge, i * 2 + (half * FT + s + 1))
                        dve.wait_ge(s_used, i * 4 + used(half, U_UP + 2 * s + 1))
                        for c in range(2):
                            V.tensor_tensor(fs[:, 320 * c:320 * c + 320], fs[:, 320 * c:320 * c + 320],
                                            ps[:, 4 * s + 2 + c, 0:320], ALU.mult)
                        dve.drain()
                        V.tensor_scalar(f_h[:, bass.ds(i * 2 + s, 1), :].rearrange("p o t -> p (o t)"), fs[:],
                                        1.0, None, ALU.mult)
                        dve.drain()
                        V.tensor_tensor(f_l[:, bass.ds(i * 2 + s, 1), :].rearrange("p o t -> p (o t)"), fs[:],
                                        f_h[:, bass.ds(i * 2 + s, 1), :].rearrange("p o t -> p (o t)").bitcast(F32),
                                        ALU.subtract).then_inc(c_fl, 1)
                dve.wait_ge(n_rs, half * 3 + 3)
                dve.wait_ge(s_xo, 16 * (half + 1))
                for k in range(KT):
                    V.scalar_tensor_tensor(yo[:, k], yo[:, k], colt[:, C_POSTFFN + k:C_POSTFFN + k + 1],
                                           rs[:, 0:HALF], ALU.mult, ALU.mult)
                    dve.drain()
                    V.tensor_tensor(yo[:, k], yo[:, k], xo[:, k], ALU.add).then_inc(e_y, 1)

        @block.tensor
        def _(pe):
            mm = nc.tensor.matmul

            def dense(out_ap, slot, rhs, kts=KT, k_first=0, first=True, last=True):
                hi, lo = rhs
                for k in range(kts):
                    wh = ring_h[:, k, slot * P:(slot + 1) * P]
                    wl = ring_l[:, k, slot * P:(slot + 1) * P]
                    mm(out_ap, wh, hi(k + k_first), start=first and k == 0, stop=False)
                    mm(out_ap, wh, lo(k + k_first), start=False, stop=False)
                    ins = mm(out_ap, wl, hi(k + k_first), start=False, stop=last and k == kts - 1)
                return ins

            pe.wait_ge(s_cst, 1)
            for k in range(KT):
                pe.wait_ge(s_sq, k + 1)
                for c, (a, b) in enumerate(CHUNKS):
                    ins = mm(ps[:, 2 + c, 0:b - a], ones0[:], sq0[:, k % 2, a:b], start=k == 0, stop=k == KT - 1)
                ins.then_inc(s_sqm, 1)
            pe.wait_ge(s_ht, KT)

            def unit_group(kind, u, c, h, shift=0):
                g = 3 * u + c
                unit = a_unit if kind == "A" else m_unit
                n1 = unit((1 if not isinstance(h, int) else h) + shift, u)
                a, b = CHUNKS[c]
                if c == 0:
                    pe.wait_ge(s_split, lin(lambda k: unit(k + shift, u) + 1, h))
                bank_free(pe, lambda k: (kind, k + shift, g), h)
                dense(ps[:, g % 2, 0:b - a], RING[n1],
                      (lambda k: ht_h[:, k, a:b], lambda k: ht_l[:, k, a:b])).then_inc(d_done, 1)

            def vo_group(blk, h, shift=0):
                g = 12 + blk
                if blk == 0:
                    pe.wait_ge(s_split, lin(lambda k: m_unit(k + shift, 7) + 1, h))
                bank_free(pe, lambda k: ("M", k + shift, g), h)
                t = slice(blk * P, (blk + 1) * P)
                for k in range(KT):
                    mm(ps[:, g % 2, :], ht_h[:, k, t], ring_h[:, k, :], start=k == 0, stop=False)
                    mm(ps[:, g % 2, :], ht_h[:, k, t], ring_l[:, k, :], start=False, stop=False)
                    ins = mm(ps[:, g % 2, :], ht_l[:, k, t], ring_h[:, k, :], start=False, stop=k == KT - 1)
                ins.then_inc(d_done, 1)

            def m_dense(g, h, shift=0):
                if g < 12:
                    unit_group("M", g // 3, g % 3, h, shift)
                else:
                    vo_group(g - 12, h, shift)

            for c, (a, b) in enumerate(CHUNKS):
                if c == 0:
                    pe.wait_ge(s_split, 1)
                bank = c % 2
                if c == 2:
                    pe.wait_ge(ev_act, 1)
                dense(ps[:, bank, 0:b - a], RING[0],
                      (lambda k: ht_h[:, k, a:b], lambda k: ht_l[:, k, a:b])).then_inc(d_done, 1)
            for g in range(22):
                m_dense(g, 0)
            pe.wait_ge(p_exp, 1)
            pe.wait_ge(s_cstp, 1)
            for q in range(4):
                ins = nc.tensor.transpose(ps[:, 2, 80 * q:80 * q + 80], r80[0:80, q], ident[0:80, 0:80])
            ins.then_inc(p_col, 1)
            pe.wait_ge(p_tc, 1)

            def m_scores(i, h):
                pe.wait_ge(m_sel, lin(lambda k: k + 1, h))
                if i > 6:
                    pe.wait_ge(m_ye, lin(lambda k: 5 * k + i - 6, h))
                if i == 0:
                    pe.wait_ge(ev_act, lin(lambda k: GROUPS[("M", k, 11)][3], h))
                    pe.wait_ge(ev_dve, lin(lambda k: GROUPS[("M", k, 21)][3], h))
                for d in range(2):
                    c = chunk_of(d, i)
                    t = slice(c * P, (c + 1) * P)
                    for dt in range(2):
                        nc.tensor.transpose(ps[:, 7, 256 * d + P * dt:256 * d + P * dt + P], mk_t[:, dt, t], ident[:])
                    for dt in range(2):
                        mm(ps[:, 2, 256 * d:256 * d + P], mk_t[:, dt, t], mq_t[:, dt, t], start=dt == 0, stop=dt == 1)
                    j = d * NB + c
                    ins = mm(ps[:, 2, 256 * d + P:256 * d + 2 * P], pick[0:80, j:j + 1].to_broadcast([80, P]),
                             urows[:], start=True, stop=True)
                ins.then_inc(m_sc, 1)

            def m_numden(i, h):
                if i > 0:
                    pe.wait_ge(m_c, lin(lambda k: 9 * k + i, h))
                for d in range(2):
                    c = chunk_of(d, i)
                    if not fresh(d, i):
                        for dt in range(2):
                            mm(ps[:, 3 + 2 * d, 0:DH + 1], mq_t[:, dt, c * P:(c + 1) * P], c_st[:, d, dt],
                               start=dt == 0, stop=dt == 1)
                pe.wait_ge(m_a, lin(lambda k: NB * k + i + 1, h))
                for d in range(2):
                    ins = mm(ps[:, 4 + 2 * d, 0:DH + 1], ex[:, d], v_tok[:, chunk_of(d, i)], start=True, stop=True)
                ins.then_inc(m_nd, 1)

            def m_update(i, h):
                if i + 1 == NB:
                    return
                pe.wait_ge(m_wk, lin(lambda k: NB * k + i + 1, h))
                pe.wait_ge(m_ndx, lin(lambda k: NB * k + i + 1, h))
                for d in range(2):
                    if updates(d, i):
                        for dt in range(2):
                            ins = mm(ps[:, 3 + 2 * d + dt, 0:DH + 1], wk[:, d, dt * P:(dt + 1) * P],
                                     v_tok[:, chunk_of(d, i)], start=True, stop=True)
                ins.then_inc(m_cu, 1)

            def m_turn(i, h):
                pe.wait_ge(m_yn, lin(lambda k: 5 * k + i - 4, h))
                if i + 1 < NB:
                    pe.wait_ge(m_wk, lin(lambda k: NB * k + i + 2, h))
                else:
                    pe.wait_ge(m_wk, lin(lambda k: NB * k + i + 1, h))
                for d in range(2):
                    for dt in range(2):
                        ins = nc.tensor.transpose(ps[:, 7, 256 * dt + P * d:256 * dt + P * d + P],
                                                  h_acc[:, chunk_of(d, i), dt * P:(dt + 1) * P], ident[:])
                ins.then_inc(m_y, 1)

            def mlstm(h):
                for i in range(NB):
                    m_scores(i, h)
                    unit_group("A", (2 * i) // 3, (2 * i) % 3, h)
                    m_numden(i, h)
                    if i > 5:
                        m_turn(i - 1, h)
                    unit_group("A", (2 * i + 1) // 3, (2 * i + 1) % 3, h)
                    m_update(i, h)
                unit_group("A", 6, 2, h)
                m_turn(NB - 1, h)

            def a_scores(j, h):
                kb = kblocks(j)
                a, b = (kb[0] - j + 1) * P, (kb[-1] - j + 2) * P
                if j == 0:
                    pe.wait_ge(ev_act, lin(lambda k: GROUPS[("A", k, 8)][3], h))
                else:
                    pe.wait_ge(a_m, lin(lambda k: NB * k + j, h))
                pieces = []
                for r in (2, 0, 1, 3):
                    lo = S_AT[r] + a
                    while lo < S_AT[r] + b:
                        hi = min(S_AT[r] + b, (lo // 512 + 1) * 512)
                        pieces.append((r % 2, r % 2 == 1 and lo // 512 == 1, r, lo, hi))
                        lo = hi
                pieces.sort(key=lambda x: x[:2])
                for n, (odd, shared, r, lo, hi) in enumerate(pieces):
                    rows = slice(HD * odd, HD * odd + HD)
                    k0 = (j - 1) * P + lo - S_AT[r]
                    if shared:
                        pe.wait_ge(a_even, lin(lambda k: NB * k + j + 1, h))
                    ins = mm(ps[:, 2 + lo // 512, lo % 512:lo % 512 + hi - lo],
                             aq_t[rows, r // 2, j * P:(j + 1) * P], kk_t[rows, k0:k0 + hi - lo],
                             start=True, stop=True)
                    if not odd and pieces[n + 1][0]:
                        ins.then_inc(a_even, 1)
                ins.then_inc(a_s_done, 1)

            def a_turn(j, h):
                pe.wait_ge(a_p, lin(lambda k: NB * k + j + 1, h))
                if j > 0:
                    pe.wait_ge(a_o, lin(lambda k: NB * k + j, h))
                else:
                    pe.wait_ge(a_av, lin(lambda k: k + 1, h))
                kb = kblocks(j)
                for n, blk in enumerate(kb):
                    o = (blk - j + 1) * P
                    for r in range(QPG):
                        ins = nc.tensor.transpose(ps[:, 5 + n, r * P:(r + 1) * P], prob[:, r, o:o + P], ident[:])
                ins.then_inc(a_t, 1)

            def a_values(j, h):
                pe.wait_ge(a_pt, lin(lambda k: NB * k + j + 1, h))
                kb = kblocks(j)
                for n, blk in enumerate(kb):
                    ins = mm(ps[0:HD, 5, :], av_tok[:, blk], prob_t[:, n], start=n == 0, stop=n == len(kb) - 1)
                ins.then_inc(a_v, 1)

            def attend(h, is_dense):
                pe.wait_ge(m_ye, lin(lambda k: 5 * (k + 1), h))
                pe.wait_ge(m_ndx, lin(lambda k: NB * (k + 1), h))
                a_scores(0, h)
                for c in range(NB):
                    ins = nc.tensor.transpose(ps[:, 6 + c // 5, (c % 5) * HD:(c % 5 + 1) * HD],
                                              av_t[HD:P, c * P:(c + 1) * P], ident[HD:P, HD:P])
                ins.then_inc(a_avt, 1)
                for j in range(NB):
                    if is_dense:
                        m_dense(2 * j, h, 1)
                    a_turn(j, h)
                    if j + 1 < NB:
                        a_scores(j + 1, h)
                    if is_dense:
                        m_dense(2 * j + 1, h, 1)
                    a_values(j, h)
                if is_dense:
                    m_dense(20, h, 1)
                    m_dense(21, h, 1)
                pe.wait_ge(a_o, lin(lambda k: NB * (k + 1), h))

            with pe.Fori(0, HEADS - 1) as h:
                mlstm(h)
                attend(h, True)
            mlstm(HEADS - 1)
            attend(HEADS - 1, False)

            def two_chunks(bank0, slot, hi, lo, chunks, **kw):
                for c, (a, b) in enumerate(chunks):
                    ins = dense(ps[:, bank0 + c, 0:b - a], slot, (lambda k: hi[:, k, a:b], lambda k: lo[:, k, a:b]), **kw)
                return ins

            def norm_sums(n, src_w):
                for k in range(KT):
                    pe.wait_ge(n_sq, n * KT + k + 1)
                    for c in range(2):
                        a, b = WCH[c] if src_w == WIN else (320 * c, 320 * c + 320)
                        ins = mm(ps[:, 6 + c, 0:b - a], ones[:], sq[:, k % 2, a:b], start=k == 0, stop=k == KT - 1)
                    ins.then_inc(n_sum, 1)

            pe.wait_ge(ev_act, GROUP_COUNT["act"])
            for half in range(2):
                u0 = U_B + half * HALF_UNITS
                pe.wait_ge(b_lo, 2 * KT * (half + 1))
                with pe.Fori(0, KT // 2) as i:
                    for s in range(2):
                        pe.wait_ge(b_mix, i * 2 + (half * (KT + 2) + s + 1))
                        for br, (hi, lo) in enumerate(((ya_h, ya_l), (ym_h, ym_l))):
                            pe.wait_ge(s_split, i * 4 + (u0 + 2 * s + br + 1))
                            two_chunks(4 * s + 2 * br, 2 * s + br, hi, lo, WCH).then_inc(s_used, 1)
                pe.wait_ge(b_ml, KT * (half + 1))
                for k in range(KT):
                    if k >= 4:
                        pe.wait_ge(o_ev, half * KT + k - 3)
                    pe.wait_ge(s_split, u0 + 2 * KT + k + 1)
                    two_chunks(2 * (k % 4), k % 4, mg_h, mg_l, WCH).then_inc(s_used, 1)
                pe.wait_ge(o_ev, KT * (half + 1))
                norm_sums(3 * half, WIN)
                pe.wait_ge(n_rs, 3 * half + 1)
                norm_sums(3 * half + 1, WIN)
                pe.wait_ge(n_rs, 3 * half + 2)
                pe.wait_ge(n_hl, KT * (half + 1))
                gate_ch = [(2 * half, 2 * half + 320), (2 * half + 320, 2 * half + 640)]
                with pe.Fori(0, FT // 2) as i:
                    for s in range(2):
                        pe.wait_ge(c_fl, i * 2 + (half * (FT + 2) + s + 1))
                        un = U_UP - U_B + 2 * s
                        pe.wait_ge(s_split, i * 4 + (u0 + un + 1))
                        two_chunks(4 * s, 2 * s, h2_h, h2_l, WCH).then_inc(s_used, 1)
                        pe.wait_ge(s_split, i * 4 + (u0 + un + 2))
                        two_chunks(4 * s + 2, 2 * s + 1, h2_h, h2_l, gate_ch).then_inc(s_used, 1)
                pe.wait_ge(c_fl, (FT + 2) * (half + 1))
                for k in range(KT):
                    if k >= 4:
                        pe.wait_ge(e_ev, half * KT + k - 3)
                    for part in range(3):
                        n = U_DOWN - U_B + 3 * k + part
                        pe.wait_ge(s_split, u0 + n + 1)
                        two_chunks(2 * (k % 4), n % 4, f_h, f_l, [(0, 320), (320, 640)],
                                   kts=8 if part < 2 else FT - 16, k_first=8 * part, first=part == 0, last=part == 2
                                   ).then_inc(s_used, 1)
                pe.wait_ge(e_ev, KT * (half + 1))
                norm_sums(3 * half + 2, HALF)
                pe.wait_ge(n_rs, 3 * half + 3)


def pack_units(w_in, w_att, w_mlstm, w_out, w_up, w_down):
    n_q, n_kv, n_m = D, HEADS * HD, D
    off_ak, off_av = n_q, n_q + n_kv
    off_mq = off_av + n_kv
    off_mk, off_mv, off_mo = off_mq + n_m, off_mq + 2 * n_m, off_mq + 3 * n_m
    off_if = off_mo + n_m
    off_g = off_if + 4 * HEADS

    def unit(wt, cols):
        return wt[:, cols].reshape(KT, P, P).transpose(1, 0, 2).reshape(P, KT * P)

    def sl(a):
        return slice(a, a + P)

    units = [unit(w_in, sl(off_if))]
    for h in range(HEADS):
        c = h * DH
        for o in (off_mq, off_mk, off_mo, off_mv):
            units += [unit(w_in, sl(o + c)), unit(w_in, sl(o + c + P))]
        units += [unit(w_in, sl(c)), unit(w_in, sl(c + P))]
        kv = np.concatenate([w_in[:, off_ak + h * HD:off_ak + (h + 1) * HD],
                             w_in[:, off_av + h * HD:off_av + (h + 1) * HD]], axis=1)
        units.append(unit(kv, slice(0, P)))
        for o in (off_g, off_g + D):
            units += [unit(w_in, sl(o + c)), unit(w_in, sl(o + c + P))]
    for k in range(KT):
        units += [unit(w_att, sl(k * P)), unit(w_mlstm, sl(k * P))]
    units += [unit(w_out, sl(k * P)) for k in range(KT)]
    for f in range(FT):
        units += [unit(w_up, sl(f * P)), unit(w_up, sl(FF + f * P))]
    down = np.concatenate([w_down, np.zeros((24 * P - FF, D), w_down.dtype)], axis=0)
    for k in range(KT):
        for part in range(3):
            units.append(unit(down[part * D:(part + 1) * D], sl(k * P)))
    return np.ascontiguousarray(np.stack(units))


def pack_cols(b_in, pre, mln, postmix, preffn, postffn, conv_w, conv_b):
    n_q, n_kv, n_m = D, HEADS * HD, D
    off_mq = n_q + 2 * n_kv
    off_if = off_mq + 4 * n_m
    off_g = off_if + 4 * HEADS
    col = []
    col += list(b_in[off_mq:off_mq + D].reshape(KT, P))
    col += list(b_in[off_mq + D:off_mq + 2 * D].reshape(KT, P))
    col += list(b_in[0:D].reshape(KT, P))
    for h in range(HEADS):
        col.append(np.concatenate([b_in[n_q + h * HD:n_q + (h + 1) * HD],
                                   b_in[n_q + n_kv + h * HD:n_q + n_kv + (h + 1) * HD]]))
    for h in range(HEADS):
        for o in (off_g, off_g + D):
            col += [b_in[o + h * DH:o + h * DH + P], b_in[o + h * DH + P:o + (h + 1) * DH]]
    col.append(b_in[off_if:off_if + P])
    for v in (pre, mln, postmix, preffn, postffn):
        col += list(v.reshape(KT, P))
    for t in range(3):
        col += list(conv_w[t].reshape(FT, P))
    col += list(conv_b.reshape(FT, P))
    return np.ascontiguousarray(np.stack(col, axis=1))


def kernel(x_prompt, x_sample, pre_mix_norm, w_in, b_in, attn_sink, mlstm_norm, w_att_branch, w_mlstm_branch,
           w_out, post_mix_norm, pre_ffn_norm, w_ffn_up, ffn_conv_w, ffn_conv_b, w_ffn_down, post_ffn_norm):
    import concourse.bacc as bacc
    from concourse.bass_utils import run_bass_kernel_spmd

    a = [np.asarray(v) for v in (x_prompt, x_sample, pre_mix_norm, w_in, b_in, attn_sink, mlstm_norm, w_att_branch,
                                 w_mlstm_branch, w_out, post_mix_norm, pre_ffn_norm, w_ffn_up, ffn_conv_w,
                                 ffn_conv_b, w_ffn_down, post_ffn_norm)]
    (xp, xsm, pre, wi, bi, snk, mln, wa, wm, wo, pom, pf, wu, cw, cb, wd, pof) = a
    x = np.concatenate([xp[0], xsm[0]], axis=0)
    off_mv = D + 2 * HEADS * HD + 2 * D
    bv, bo = bi[0, off_mv:off_mv + D].reshape(HEADS, DH), bi[0, off_mv + D:off_mv + 2 * D].reshape(HEADS, DH)
    arrays = {
        "w": pack_units(wi[0], wa[0], wm[0], wo[0], wu[0], wd[0]),
        "xt": np.ascontiguousarray(x.T.reshape(KT, P, T)),
        "cols": pack_cols(bi[0], pre[0], mln[0], pom[0], pf[0], pof[0], cw[0], cb[0]),
        "bvo": np.ascontiguousarray(np.concatenate([bv, bo], axis=1)),
        "sink": np.ascontiguousarray(snk),
    }
    nc = bacc.Bacc("TRN2", target_bir_lowering=False, num_devices=1)
    args = [nc.dram_tensor(n, v.shape, mybir.dt.from_np(v.dtype), kind="ExternalInput").ap()
            for n, v in arrays.items()]
    out = nc.dram_tensor("yt", (KT, P, T), F32, kind="ExternalOutput").ap()
    build(nc, *args, out)
    r = run_bass_kernel_spmd(nc, [arrays], core_ids=[0])
    y = r.results[0]["yt"].reshape(D, T).T
    return (np.ascontiguousarray(y[:SEQ_A]).reshape(1, SEQ_A, D),
            np.ascontiguousarray(y[SEQ_A:]).reshape(1, SEQ_B, D))
```

```python
import numpy as np
import concourse.bass as bass
from concourse import mybir

F32 = mybir.dt.float32
F32R = mybir.dt.float32r
ALU = mybir.AluOpType
ACT = mybir.ActivationFunctionType
AX = mybir.AxisListType

P = 128
D = 1024
KT = D // P
SEQ_A, SEQ_B = 256, 1024
T = SEQ_A + SEQ_B
NB = T // P
NB_A = SEQ_A // P
HEADS = 4
DH = 256
HD = 64
QPG = 4
FF = 2816
FT = FF // P
EPS = 1e-6
FORGET_BIAS = 3.0
HALF = T // 2
WIN = HALF + 2
BIG = 1e30

C_MQ, C_MK, C_AQ, C_AKV, C_G, C_IF = 0, 8, 16, 24, 28, 44
C_PRE, C_MLN, C_POSTMIX, C_PREFFN, C_POSTFFN = 45, 53, 61, 69, 77
C_CW, C_CB = 85, 85 + 3 * FT
NCOL = C_CB + FT

M_UNITS, A_UNITS = 8, 7
U_B = 1 + HEADS * (M_UNITS + A_UNITS)
W_MB, W_AB, W_OUT = U_B, U_B + KT, U_B + 2 * KT
W_UP = W_OUT + KT
W_DOWN = W_UP + 2 * FT
N_UNITS = W_DOWN + 3 * KT
B_MB, B_AB, B_OUT = 0, KT, (2 * KT, 3 * KT)
B_UP = (4 * KT, 7 * KT + 2 * FT)
B_DOWN = (B_UP[0] + 2 * FT, B_UP[1] + 2 * FT)
B_END = B_DOWN[1] + 3 * KT

S_AT = {0: 0, 2: 3 * P, 3: 6 * P, 1: 9 * P}

CHUNKS = [(0, 512), (512, 1024), (1024, 1280)]
WCH = [(0, 322), (322, WIN)]
OCH = [(0, HALF // 2), (HALF // 2, HALF)]
ACH = [(0, 432), (432, 864), (864, T)]
FZ = 14


def m_unit(h, k):
    return 1 + (M_UNITS + A_UNITS) * h + k


def a_unit(h, k):
    return 1 + (M_UNITS + A_UNITS) * h + M_UNITS + k


def dram_unit(p):
    for start, first in ((B_DOWN[1], W_DOWN), (B_UP[1], W_UP), (B_DOWN[0], W_DOWN), (B_UP[0], W_UP),
                         (B_OUT[1], W_OUT), (B_OUT[0], W_OUT), (0, W_MB)):
        if p >= start:
            return first + p - start


def unit_tables():
    ring, raw, last = [1], [1], [("if", 0, 2)]
    for h in range(HEADS):
        for k in range(M_UNITS):
            ring.append((2 + k) % 4)
            raw.append(k % 2)
            last.append(("M", h, 3 * k + 2 if k < 4 else 21))
        for k in range(A_UNITS):
            ring.append((3 + k) % 4)
            raw.append(k % 2)
            last.append(("A", h, 3 * k + 2))
    return ring, raw, last


RING, RAW, LAST_GROUP = unit_tables()
RING += [p % 4 for p in range(B_END)]
RAW += [p % 2 for p in range(B_END)]


def prev_user(slots, n):
    for m in range(n - 1, -1, -1):
        if slots[m] == slots[n]:
            return m
    return None


def group_tables():
    order = [("if", 0, c) for c in range(3)]
    out = {}
    for h in range(HEADS):
        order += [("M", h, g) for g in range(22)]
        order += [("A", h, g) for g in range(21)]
    count = {"act": 0, "dve": 0}
    last = {}
    for i, key in enumerate(order):
        bank = key[2] % 2
        eng = "dve" if key[0] == "M" and key[2] >= 12 else "act"
        count[eng] += 1
        out[key] = (i, bank, eng, count[eng], last.get(bank))
        last[bank] = (eng, count[eng])
    return out, count


GROUPS, GROUP_COUNT = group_tables()


def lin(f, h):
    if isinstance(h, int):
        return f(h)
    a, b = f(0), f(1)
    assert f(2) == 2 * b - a
    return h * (b - a) + a if b != a else a


def build(nc, w, xt, cols, bvo, sink, outs):
    zo = nc.dram_tensor("zo_scratch", (HEADS, NB, P, DH), F32).ap()
    gs = nc.dram_tensor("gate_scratch", (4 * HEADS, P, T), F32).ap()
    ya_d = nc.dram_tensor("ya_scratch", (D, T), F32).ap()
    ym_d = nc.dram_tensor("ym_scratch", (D, T), F32).ap()
    mb_d = nc.dram_tensor("mlstm_branch_scratch", (KT, P, T), F32).ap()
    h2_d = nc.dram_tensor("h2_scratch", (KT, P, WIN), F32).ap()
    yo_d = nc.dram_tensor("down_scratch", (KT, P, HALF), F32).ap()
    x1_d = nc.dram_tensor("x1_scratch", (2, KT, P, WIN), F32).ap()
    rows_d = nc.dram_tensor("rows_scratch", (5, 8, T), F32).ap()
    dec_d = nc.dram_tensor("decay_scratch", (8, NB), F32).ap()

    base = ((nc.sbuf_base + 63) // 64) * 64

    def at(name, off, shape, dt=F32):
        return nc.alloc_sbuf_tensor_at(name, shape, dt, offset=base + off)

    ring_h = at("ring_h", 0, [P, KT, 512], F32R)
    ring_l = at("ring_l", 16384, [P, KT, 512], F32R)
    raw = at("raw", 32768, [P, 2, KT, P])
    ht_h = at("ht_h", 40960, [P, KT, T], F32R)
    ht_l = at("ht_l", 81920, [P, KT, T], F32R)
    mq_t = at("mq_t", 122880, [P, 2, T])
    mk_t = at("mk_t", 133120, [P, 2, T])
    v_tok = at("v_tok", 143360, [P, NB, DH + 1])
    h_acc = at("h_acc", 153664, [P, NB, DH])
    c_st = at("c_st", 163904, [P, 2, 2, DH + 1])
    prob = at("prob", 153664, [P, QPG, 3 * P])
    prob_t = at("prob_t", 159808, [P, 3, QPG * P])
    ya_st = at("ya_st", 165952, [HD, QPG, P])
    aq_t = at("aq_t", 168032, [P, 2, T])
    kk_t = at("kk_t", 178272, [P, T])
    av_t = at("av_t", 183392, [P, T])
    ident = at("ident", 188512, [P, P])
    mask = at("mask", 189024, [P, 2, P])
    absrel = at("absrel", 190048, [P, 3 * P])
    tokcol = at("tokcol", 191584, [P, 4, 2 * HEADS * NB])
    urows = at("urows", 192864, [2 * HEADS * NB, P])
    decay = at("decay", 193376, [P, 2 * HEADS * NB])
    pick = at("pick", 193696, [P, 2 * NB])
    slope8 = at("slope8", 193792, [P, 16])
    sinks = at("sinks", 193856, [P, 16])
    bias_vo = at("bias_vo", 194240, [P, 2 * DH])
    ex = at("ex", 196288, [P, 2, P])
    nd = at("nd", 197312, [P, 2, DH + 1])
    wk = at("wk", 199392, [P, 2, DH])
    av_tok = at("av_tok", 197312, [P, NB, HD])
    g_st = at("g_st", 201440, [P, 2, 512])
    o_st = at("o_st", 205536, [P, 2, DH])
    o_ld = at("o_ld", 207584, [P, 2, DH])
    y_st = at("y_st", 209632, [P, 2, 2, P])
    small = at("small", 211680, [P, 64])
    hc = at("hc", 211936, [P, 40])
    HC_AQ, HC_AKV, HC_G, HC_MLN, HC_MQ, HC_MK = 20, 22, 23, 27, 30, 32
    colt = at("colt", 212096, [P, NCOL + 2])
    eps_col = colt[:, NCOL:NCOL + 1]
    one_col = colt[:, NCOL + 1:NCOL + 2]
    xs = at("xs", 122880, [P, KT, T])
    sq0 = at("sq0", 168032, [P, 2, T])
    rs0 = at("rs0", 178272, [P, T])
    ones0 = at("ones0", 196288, [P, P])
    r_if = at("r_if", 153664, [P, T])
    r_li = at("r_li", 158784, [P, T])
    r_f = at("r_f", 163904, [P, T])
    r_b = at("r_b", 169024, [P, T])
    r_m = at("r_m", 174144, [P, T])
    r_u = at("r_u", 179264, [P, T])
    r_mp = at("r_mp", 184384, [P, NB])
    r_dec = at("r_dec", 184448, [P, NB])
    r80 = at("r80", 184512, [P, 4, P])
    r_rst = at("r_rst", 197312, [P, T])
    yh = ht_h
    yl = ht_l
    ym_raw = at("ym_raw", 81920, [P, KT, T])
    ya_raw = at("ya_raw", 122880, [P, KT, T])
    gw = at("gw", 201440, [P, 4, 512])
    mg_h = at("mg_h", 123136, [P, KT, T], F32R)
    mg_l = at("mg_l", 164096, [P, KT, T], F32R)
    g_ld = at("g_ld", 205056, [P, 2, 2, 432])
    x1 = [at("x1_0", 40960, [P, KT, WIN]), at("x1_1", 61504, [P, KT, WIN])]
    h2_h = at("h2_h", 82048, [P, KT, WIN], F32R)
    h2_l = at("h2_l", 102592, [P, KT, WIN], F32R)
    xr = [at("xr_0", 102592, [P, KT, WIN]), at("xr_1", 40960, [P, KT, WIN])]
    h2_raw = xr[0]
    acc = [at("acc_0", 82048, [P, WIN]), at("acc_1", 207648, [P, WIN])]
    sq = [at("sq_0", 84640, [P, 4, 322]), at("sq_1", 210240, [P, 1, 322])]
    rs = at("rs", 205056, [P, WIN])
    ones = at("ones", 211552, [P, P])
    f_z = at("f_z", 123136, [P, FZ, 2, HALF], F32R)
    f_x = at("f_x", 40960, [P, FT - FZ, 2, HALF], F32R)
    a_s = at("a_s", 194816, [P, 648])
    cv = at("cv", 197408, [P, HALF])
    fs = at("fs", 199968, [P, HALF])
    yo = [at("yo_0", 40960, [P, KT, HALF]), at("yo_1", 82048, [P, KT, HALF])]
    xo = [at("xo_0", 61440, [P, KT, HALF]), at("xo_1", 102528, [P, KT, HALF])]

    def st_width(st, m):
        return WIN if m < 2 else HALF

    ps = nc.alloc_psum_tensor("ps", [P, 8, 512], F32)

    def sem(name):
        return nc.alloc_semaphore(name)

    s_raw = [sem("raw_landed0"), sem("raw_landed1")]
    s_split = sem("unit_split")
    s_used = sem("unit_used")
    s_xl = [sem(f"x_landed{k}") for k in range(KT)]
    s_cols = sem("cols_landed")
    s_cst = sem("consts_dve")
    s_cstp = sem("consts_pool")
    s_sq = sem("sq_ready")
    s_sqm = sem("sq_summed")
    s_rs = sem("rstd_ready")
    s_xn = sem("x_normed")
    s_xh = sem("x_hi")
    s_ht = sem("ht_ready")
    d_done = sem("dense_done")
    ev_act = sem("dense_evac_act")
    ev_dve = sem("dense_evac_dve")
    s_bvo = sem("bias_vo_landed")
    s_os = [sem("o_stored0"), sem("o_stored1")]
    s_g1 = sem("gate_summed")
    s_gs = [sem("gate_stored0"), sem("gate_stored1")]
    p_z = sem("rows_zeroed")
    p_in = sem("rows_split")
    p_abs = sem("abs_f")
    p_ln = sem("softplus")
    p_args = sem("row_args")
    p_out = sem("rows_stored")
    p_80 = sem("rows80_landed")
    p_exp = sem("rows80_exp")
    p_col = sem("cols_transposed")
    p_tc = sem("tokcol_ready")
    m_sel = sem("m_head_columns")
    a_sel = sem("a_next_head_columns")
    m_sc = sem("m_scores")
    m_e = sem("m_exponents")
    m_x = sem("m_exp")
    m_a = sem("m_weights")
    m_wk = sem("m_wk")
    m_nd = sem("m_numden")
    m_qc = sem("m_inter_scaled")
    m_ndx = sem("m_numden_read")
    m_cu = sem("m_update")
    m_c = sem("m_state")
    m_ol = sem("m_o_loaded")
    m_ze = sem("m_o_exp")
    m_ss = sem("m_gated")
    m_rs = sem("m_rstd")
    m_yn = sem("m_normed")
    m_y = sem("m_y_transposed")
    s_ym = sem("ym_stored")
    m_ye = sem("m_y_evacuated")
    a_avt = sem("a_v_transposed")
    a_av = sem("a_v_tokens")
    a_even = sem("a_even_heads")
    a_s_done = sem("a_scores")
    a_m = sem("a_max")
    a_x = sem("a_exp")
    a_p = sem("a_probs")
    a_t = sem("a_probs_transposed")
    a_pt = sem("a_pt_evacuated")
    a_v = sem("a_out")
    a_o = sem("a_out_evacuated")
    s_ya = sem("ya_stored")
    s_ymr = [sem(f"ym_raw_landed{k}") for k in range(KT)]
    s_yar = [sem(f"ya_raw_landed{k}") for k in range(KT)]
    b_hi = sem("b_y_hi")
    b_mlo = sem("b_ym_lo")
    b_alo = sem("b_ya_lo")
    b_done = sem("b_group_done")
    b_mix = sem("b_group_mixed")
    b_ml = sem("b_merged_lo")
    s_gw = [sem(f"gate_again{k}") for k in range(4)]
    s_mb = [sem(f"mlstm_branch_stored{k}") for k in range(4)]
    s_gl = [sem("mix_operands0"), sem("mix_operands1")]
    o_ev = sem("o_evacuated")
    q_sq = [sem("q_square0"), sem("q_square1")]
    q_acc = [sem("q_added0"), sem("q_added1")]
    n_sum = sem("n_summed")
    n_rs = sem("n_rstd")
    s_xr = sem("x_again")
    n_x1 = sem("n_x1")
    s_x1 = sem("x1_stored")
    n_h2 = sem("n_h2_value")
    s_h2 = sem("h2_stored")
    s_h2r = sem("h2_again")
    n_hh = sem("n_h2_hi")
    n_hl = sem("n_h2_lo")
    c_pad = sem("c_pads")
    c_ae = sem("c_a_evacuated")
    c_cv = sem("c_conv")
    c_ge = sem("c_gelu")
    c_fl = sem("c_f_lo")
    e_ev = sem("e_evacuated")
    s_ys = [sem("down_stored0"), sem("down_stored1")]
    s_fo = sem("final_operands")
    e_y = sem("e_out_ready")
    s_out = sem("out_stored")

    def used(p):
        return p - B_OUT[0] + 1

    def f_tile(k, part):
        return f_z[:, k, part] if k < FZ else f_x[:, k - FZ, part]

    def bank_free(eng, key_of, h):
        who = GROUPS[key_of(h if isinstance(h, int) else 1)][4]
        if who is None:
            return
        s = ev_act if who[0] == "act" else ev_dve
        eng.wait_ge(s, lin(lambda k: GROUPS[key_of(k)][4][1], h))

    def seq_of(c):
        return (0, NB_A) if c < NB_A else (NB_A, NB)

    def kblocks(j):
        lo, hi = seq_of(j)
        return list(range(max(lo, j - 1), min(hi, j + 2)))

    def chunk_of(d, i):
        return i if d == 0 else NB - 1 - i

    def fresh(d, i):
        c = chunk_of(d, i)
        lo, hi = seq_of(c)
        return c == (lo if d == 0 else hi - 1)

    def updates(d, i):
        return i + 1 < NB and not fresh(d, i + 1)

    def tcol(q, d, h, c):
        return tokcol[:, q, bass.ds(h * NB + (d * HEADS * NB + c), 1)]

    ctx_block = nc.Block()
    with ctx_block as block:

        @block.sync
        def _(sp):
            for k in range(KT):
                sp.dma_start(xs[:, k, :], xt[k]).then_inc(s_xl[k], 16)
            sp.dma_start(colt[:, 0:NCOL], cols[:]).then_inc(s_cols, 16)
            sp.dma_start(sinks[:], sink[0:1, :].to_broadcast([P, 16])).then_inc(s_cols, 16)

            def load(unit_of, h):
                n1 = unit_of(1 if not isinstance(h, int) else h)
                slot = RAW[n1]
                if prev_user(RAW, n1) is not None:
                    sp.wait_ge(s_split, lin(lambda k: prev_user(RAW, unit_of(k)) + 1, h))
                sp.dma_start(raw[:, slot], w[bass.ds(lin(unit_of, h), 1)]
                             .rearrange("o p (k c) -> (o p) k c", c=P)).then_inc(s_raw[slot], 16)

            def store_gate(k, h):
                for c, (a, b) in enumerate(CHUNKS):
                    pos = k * 3 + c
                    sp.wait_ge(s_g1, lin(lambda hh: 12 * hh + pos + 1, h))
                    sp.dma_start(gs[bass.ds(h * 4 + k, 1), :, a:b].rearrange("o p t -> (o p) t"),
                                 g_st[:, pos % 2, 0:b - a]).then_inc(s_gs[pos % 2], 16)

            def store_o(h):
                for blk in range(NB):
                    sp.wait_ge(ev_dve, lin(lambda k: GROUPS[("M", k, 12 + blk)][3], h))
                    sp.dma_start(zo[bass.ds(h, 1), blk].rearrange("o p t -> (o p) t"),
                                 o_st[:, blk % 2, :]).then_inc(s_os[blk % 2], 16)

            def m_loads(h, gates_h):
                for k in range(M_UNITS):
                    load(lambda hh, k=k: m_unit(hh + 1, k), h)
                    if k == 3:
                        if gates_h is not None:
                            sp.wait_ge(ev_dve, lin(lambda hh: NB * (hh + 1), gates_h))
                        sp.dma_start(bias_vo[:], bvo[bass.ds(h + 1, 1), :].to_broadcast([P, 2 * DH])
                                     ).then_inc(s_bvo, 16)

            def a_loads(h):
                for k in range(A_UNITS):
                    load(lambda hh, k=k: a_unit(hh, k), h)
                    if k == 1:
                        store_o(h)
                    if 2 <= k < 6:
                        store_gate(k - 2, h)

            load(lambda hh: 0, 0)
            m_first = [lambda k=k: load(lambda hh: m_unit(0, k), 0) for k in range(M_UNITS)]
            m_first[0]()
            sp.dma_start(bias_vo[:], bvo[0:1, :].to_broadcast([P, 2 * DH])).then_inc(s_bvo, 16)
            sp.wait_ge(ev_act, 3)
            sp.wait_ge(p_z, 1)
            for d in range(2):
                sp.dma_start(r_li[32 * d:32 * d + 4, :], r_if[4 * d:4 * d + 4, :]).then_inc(p_in, 16)
                sp.dma_start(r_f[32 * d:32 * d + 4, :], r_if[8 + 4 * d:12 + 4 * d, :]).then_inc(p_in, 16)
            m_first[1]()
            m_first[2]()
            sp.wait_ge(p_args, 1)
            for q, rows in enumerate((r_u, r_li, r_f, r_m, r_b)):
                for d in range(2):
                    sp.dma_start(rows_d[q, 4 * d:4 * d + 4, :], rows[32 * d:32 * d + 4, :]).then_inc(p_out, 16)
            for d in range(2):
                sp.dma_start(dec_d[4 * d:4 * d + 4, :], r_dec[32 * d:32 * d + 4, :]).then_inc(p_out, 16)
            m_first[3]()
            sp.wait_ge(p_out, 12 * 16)
            by_chunk = rows_d.rearrange("q r (c t) -> q (r c) t", t=P)
            sp.dma_start(urows[:], by_chunk[0]).then_inc(p_80, 16)
            sp.dma_start(r80[0:2 * HEADS * NB], by_chunk[1:5].rearrange("q r t -> r q t")).then_inc(p_80, 16)
            sp.dma_start(decay[:], dec_d.rearrange("(o r) c -> o (r c)", o=1).to_broadcast([P, 2 * HEADS * NB])
                         ).then_inc(p_80, 16)
            for k in range(4, M_UNITS):
                m_first[k]()
            with sp.Fori(0, HEADS - 1) as h:
                a_loads(h)
                m_loads(h, h)
            a_loads(HEADS - 1)

            def load_b(p, i=None, step=0):
                src = w[dram_unit(p):dram_unit(p) + 1] if i is None else w[bass.ds(i * step + dram_unit(p), 1)]
                done = U_B + p - 1 if p else U_B
                sp.wait_ge(s_split, done if i is None else i * step + done)
                sp.dma_start(raw[:, p % 2], src.rearrange("o p (k c) -> (o p) k c", c=P)).then_inc(s_raw[p % 2], 16)

            def load_many(p0, p1):
                with sp.Fori(0, (p1 - p0) // 2) as i:
                    load_b(p0, i, 2)
                    load_b(p0 + 1, i, 2)

            ym_tiles = ym_d.rearrange("(k p) t -> k p t", p=P)
            ya_tiles = ya_d.rearrange("(k p) t -> k p t", p=P)
            load_b(0)
            load_b(1)
            sp.wait_ge(d_done, len(GROUPS))
            sp.wait_ge(s_ym, 160 * (HEADS - 1))
            for k in range(KT - 2):
                sp.dma_start(ym_raw[:, k], ym_tiles[k]).then_inc(s_ymr[k], 16)
            sp.wait_ge(s_ym, 160 * HEADS)
            for k in range(KT - 2, KT):
                sp.dma_start(ym_raw[:, k], ym_tiles[k]).then_inc(s_ymr[k], 16)
            for p in range(2, 6):
                load_b(p)
            for s in range(2):
                sp.wait_ge(s_gs[s], 16 * HEADS * 6)
                sp.wait_ge(s_os[s], 16 * HEADS * 5)
            sp.wait_ge(m_yn, 5 * HEADS)
            sp.wait_ge(s_ya, 16 * NB * (HEADS - 1))
            sp.wait_ge(m_y, 5 * HEADS)
            for n in range(3 * KT + 2):
                if n < 3 * KT:
                    u, (a, b) = n // 3, CHUNKS[n % 3]
                    if n >= 4:
                        sp.wait_ge(s_mb[n % 4], 16 * (n // 4))
                    sp.dma_start(gw[:, n % 4, 0:b - a], gs[4 * (u // 2) + 2 + u % 2, :, a:b]).then_inc(s_gw[n % 4], 16)
                if n >= 2:
                    u, (a, b) = (n - 2) // 3, CHUNKS[(n - 2) % 3]
                    sp.wait_ge(b_mix, n - 1)
                    sp.dma_start(mb_d[u, :, a:b], gw[:, (n - 2) % 4, 0:b - a]).then_inc(s_mb[(n - 2) % 4], 16)
                if n % 3 == 2 and 1 <= n // 3 <= KT - 1:
                    load_b(n // 3 + 5)
                if n == 4:
                    for k in range(KT - 2):
                        sp.dma_start(ya_raw[:, k], ya_tiles[k]).then_inc(s_yar[k], 16)
                if n == 17:
                    sp.wait_ge(s_ya, 16 * NB * HEADS)
                    sp.wait_ge(a_v, NB * HEADS)
                    for k in range(KT - 2, KT):
                        sp.dma_start(ya_raw[:, k], ya_tiles[k]).then_inc(s_yar[k], 16)
            for s in range(4):
                sp.wait_ge(s_mb[s], 16 * 6)
            with sp.Fori(0, KT // 2) as i:
                for g in range(6):
                    s, (a, b) = g // 3, ACH[g % 3]
                    sp.wait_ge(b_mix, i * 6 + (3 * KT + g - 1))
                    for n, src in enumerate((gs[bass.ds(i * 4 + s, 1), :, a:b], mb_d[bass.ds(i * 2 + s, 1), :, a:b])):
                        sp.dma_start(g_ld[:, g % 2, n, 0:b - a], src.rearrange("o p t -> (o p) t")
                                     ).then_inc(s_gl[g % 2], 16)
                    if g % 3 == 2:
                        load_b(B_AB + 5 + s, i, 2)
            sp.wait_ge(b_done, 6 * KT)
            sp.dma_start(xr[0][:], xt[:, :, 0:WIN].rearrange("k p t -> p k t")).then_inc(s_xr, 16)
            for p in range(B_AB + 13, B_UP[0] + 2):
                load_b(p)

            def store_x1(g):
                sp.wait_ge(n_x1, KT * (g + 1))
                sp.dma_start(x1_d[g].rearrange("k p t -> p k t"), x1[g][:]).then_inc(s_x1, 16)

            store_x1(0)
            for p in range(B_UP[0] + 2, B_UP[0] + 6):
                load_b(p)
            sp.wait_ge(n_h2, KT)
            sp.wait_ge(s_x1, 16)
            sp.dma_start(xr[1][:], xt[:, :, T - WIN:T].rearrange("k p t -> p k t")).then_inc(s_xr, 16)
            load_many(B_UP[0] + 6, B_UP[0] + 22)
            store_x1(1)
            load_many(B_UP[0] + 22, B_UP[0] + 28)
            sp.wait_ge(n_h2, 2 * KT)
            sp.dma_start(h2_d.rearrange("k p t -> p k t"), xr[1][:]).then_inc(s_h2, 16)
            load_many(B_UP[0] + 28, B_DOWN[0])
            for p in range(B_DOWN[0], B_DOWN[0] + 6):
                load_b(p)
            sp.wait_ge(s_used, used(B_DOWN[0] - 1))
            sp.wait_ge(s_h2, 16)
            sp.dma_start(h2_raw[:], h2_d.rearrange("k p t -> p k t")).then_inc(s_h2r, 16)
            load_many(B_DOWN[0] + 6, B_DOWN[0] + 24)
            for p in range(B_UP[1], B_UP[1] + 6):
                load_b(p)
            sp.wait_ge(s_used, used(B_UP[1] - 1))
            for s in range(2):
                sp.wait_ge(s_ys[s], 16 * KT // 2)
            sp.dma_start(yo[0][:], yo_d.rearrange("k p t -> p k t")).then_inc(s_fo, 16)
            sp.dma_start(xo[0][:], x1_d[0, :, :, 0:HALF].rearrange("k p t -> p k t")).then_inc(s_fo, 16)
            load_many(B_UP[1] + 6, B_UP[1] + 26)
            sp.wait_ge(e_y, KT)
            sp.dma_start(outs[:, :, 0:HALF].rearrange("k p t -> p k t"), yo[0][:]).then_inc(s_out, 16)
            load_many(B_UP[1] + 26, B_DOWN[1])
            for p in range(B_DOWN[1], B_DOWN[1] + 6):
                load_b(p)
            sp.wait_ge(s_used, used(B_DOWN[1] - 1))
            sp.wait_ge(s_x1, 32)
            sp.dma_start(xo[1][:], x1_d[1, :, :, 2:WIN].rearrange("k p t -> p k t")).then_inc(s_fo, 16)
            load_many(B_DOWN[1] + 6, B_END)
            for k in range(KT):
                sp.wait_ge(e_y, KT + k + 1)
                sp.dma_start(outs[k, :, HALF:T], yo[1][:, k, :]).then_inc(s_out, 16)
            sp.wait_ge(s_out, 16 * (KT + 1))

        @block.gpsimd
        def _(pool):
            nc.gpsimd.memset(ident[:], 0.0)
            nc.gpsimd.memset(mask[:], 0.0)
            nc.gpsimd.memset(one_col, 1.0)
            nc.gpsimd.iota(absrel[:], pattern=[[1, 3 * P]], base=-P, channel_multiplier=-1,
                           allow_small_or_imprecise_dtypes=True)
            pool.drain()
            nc.gpsimd.affine_select(out=ident[:], in_=ident[:], compare_op=ALU.not_equal, fill=1.0, base=0,
                                    pattern=[[-1, P]], channel_multiplier=1)
            nc.gpsimd.affine_select(out=mask[:, 0], in_=mask[:, 0], compare_op=ALU.is_ge, fill=-BIG, base=0,
                                    pattern=[[1, P]], channel_multiplier=-1)
            nc.gpsimd.affine_select(out=mask[:, 1], in_=mask[:, 1], compare_op=ALU.is_ge, fill=-BIG, base=0,
                                    pattern=[[-1, P]], channel_multiplier=1).then_inc(s_cstp, 1)

            def split(slot, rslot):
                nc.gpsimd.tensor_tensor(ring_h[:, :, slot * P:(slot + 1) * P], raw[:, rslot],
                                        one_col.unsqueeze(2).to_broadcast([P, KT, P]), ALU.mult)
                pool.drain()
                nc.gpsimd.tensor_tensor(ring_l[:, :, slot * P:(slot + 1) * P], raw[:, rslot],
                                        ring_h[:, :, slot * P:(slot + 1) * P].bitcast(F32),
                                        ALU.subtract).then_inc(s_split, 1)

            def take(unit_of, h):
                n1 = unit_of(1 if not isinstance(h, int) else h)
                rslot, slot = RAW[n1], RING[n1]
                pool.wait_ge(s_raw[rslot], lin(lambda k: 16 * RAW[:unit_of(k) + 1].count(rslot), h))
                if prev_user(RING, n1) is not None:
                    pool.wait_ge(d_done, lin(lambda k: GROUPS[LAST_GROUP[prev_user(RING, unit_of(k))]][0] + 1, h))
                split(slot, rslot)

            take(lambda k: 0, 0)
            for u in range(M_UNITS):
                take(lambda k, u=u: m_unit(k, u), 0)
            with pool.Fori(0, HEADS - 1) as h:
                for u in range(A_UNITS):
                    take(lambda k, u=u: a_unit(k, u), h)
                for u in range(M_UNITS):
                    take(lambda k, u=u: m_unit(k + 1, u), h)
            for u in range(A_UNITS):
                take(lambda k, u=u: a_unit(k, u), HEADS - 1)
            for n in range(U_B, U_B + 4):
                take(lambda k, n=n: n, 0)
            for k in range(KT):
                pool.wait_ge(b_hi, k + 1)
                nc.gpsimd.tensor_tensor(yl[:, k], ym_raw[:, k], yh[:, k].bitcast(F32), ALU.subtract).then_inc(b_mlo, 1)
            with pool.Fori(0, 2 * KT // 4) as i:
                for s in range(4):
                    n = U_B + 4 + s
                    pool.wait_ge(s_raw[RAW[n]], i * 32 + 16 * RAW[:n + 1].count(RAW[n]))
                    pool.wait_ge(b_done, i * 12 + 3 * (s + 1))
                    split(RING[n], RAW[n])
            with pool.Fori(0, (B_END - 2 * KT - 4) // 4) as i:
                for s in range(4):
                    n = U_B + 2 * KT + 4 + s
                    pool.wait_ge(s_raw[RAW[n]], i * 32 + 16 * RAW[:n + 1].count(RAW[n]))
                    pool.wait_ge(s_used, i * 4 + s + 1)
                    split(RING[n], RAW[n])

        def square(act, st, m, k, c, src):
            a = (WCH if st_width(st, m) == WIN else OCH)[c][0]
            b = a + src.shape[-1]
            j = 2 * k + c - 2
            slots = 4 if st == 0 else 1
            if k == 0:
                if m and c == 0:
                    act.wait_ge(n_sum, {(0, 1): 1, (1, 1): 3, (1, 2): 4, (1, 3): 5}[st, m])
                nc.scalar.activation(acc[st][:, a:b], src, ACT.Square).then_inc(q_sq[st], 1)
            else:
                if j >= slots or m:
                    act.wait_ge(q_acc[st], 14 * m + max(j - slots, -1) + 1)
                nc.scalar.activation(sq[st][:, j % slots, 0:b - a], src, ACT.Square).then_inc(q_sq[st], 1)

        def rstd_half(act, number, width, bank):
            act.wait_ge(n_sum, number)
            for c, (a, b) in enumerate(WCH if width == WIN else OCH):
                nc.scalar.activation(rs[:, a:b], ps[:, bank + c, 0:b - a], ACT.Ln, bias=eps_col, scale=1.0 / D)
            act.drain()
            nc.scalar.activation(rs[:, 0:width], rs[:, 0:width], ACT.Exp, scale=-0.5).then_inc(n_rs, 1)

        def halves_act(act):
            act.wait_ge(b_done, 3 * KT)
            for k in range(KT):
                act.wait_ge(s_yar[k], 16)
                nc.scalar.activation(yh[:, k], ya_raw[:, k], ACT.Identity).then_inc(b_hi, 1)

            def evac_out(g, k):
                act.wait_ge(s_used, used(B_OUT[g] + k))
                for c, (a, b) in enumerate(WCH):
                    last = nc.scalar.activation(x1[g][:, k, a:b], ps[:, 2 * (k % 4) + c, 0:b - a], ACT.Copy)
                for c, (a, b) in enumerate(WCH):
                    square(act, g, 0, k, c, ps[:, 2 * (k % 4) + c, 0:b - a])
                act.drain()
                act.sem_inc(o_ev, 1)

            def square_x1(g, k):
                act.wait_ge(n_x1, g * KT + k + 1)
                for c, (a, b) in enumerate(WCH):
                    square(act, g, 1, k, c, x1[g][:, k, a:b])

            def h2_hi(g, k):
                act.wait_ge(n_h2, k + 1) if g == 0 else act.wait_ge(s_h2r, 16)
                nc.scalar.activation(h2_h[:, k], h2_raw[:, k], ACT.Identity).then_inc(n_hh, 1)

            for k in range(KT):
                evac_out(0, k)
            evac_out(1, 0)
            rstd_half(act, 1, WIN, 6)
            for k in range(KT):
                square_x1(0, k)
                if k in (1, 4, 7):
                    evac_out(1, (k + 2) // 3)
            evac_out(1, 4)
            rstd_half(act, 2, WIN, 6)
            for k in range(KT):
                h2_hi(0, k)
                if k in (2, 5):
                    evac_out(1, 5 + k // 3)
            evac_out(1, 7)

            def up_tile(half, i, s):
                act.wait_ge(s_used, i * 4 + used(B_UP[half] + 2 * s))
                if isinstance(i, int) and i == 0 and s == 0:
                    act.wait_ge(c_pad, half + 1)
                act.wait_ge(c_cv, i * 2 + (half * (FT + 1) + s + 1))
                if half == 0:
                    pieces = [(0, 0, 256, 1), (0, 256, 322, 258), (1, 322, WIN, 324)]
                else:
                    pieces = [(0, 0, 322, 0), (1, 322, WIN, 322)]
                for c, a, b, o in pieces:
                    w0 = WCH[c][0]
                    last = nc.scalar.activation(a_s[:, o:o + b - a], ps[:, 4 * s + c, a - w0:b - w0], ACT.Copy)
                last.then_inc(c_ae, 1)
                act.wait_ge(c_cv, i * 2 + (half * (FT + 1) + 1 + s + 1))
                act.wait_ge(c_fl, i * 2 + (half * (FT + 2) + s + 2))
                nc.scalar.activation(fs[:], cv[:], ACT.Gelu_apprx_tanh).then_inc(c_ge, 1)

            def down_tile(half, k):
                act.wait_ge(s_used, used(B_DOWN[half] + 3 * k + 2))
                dst = yo[1][:, k] if half else (cv, fs)[k % 2]
                if half == 0 and k >= 2:
                    act.wait_ge(s_ys[k % 2], 16 * (k // 2))
                for c, (a, b) in enumerate(OCH):
                    nc.scalar.activation(dst[:, a:b], ps[:, 2 * (k % 4) + c, 0:b - a], ACT.Copy)
                for c, (a, b) in enumerate(OCH):
                    square(act, 1, 2 + half, k, c, ps[:, 2 * (k % 4) + c, 0:b - a])
                act.drain()
                act.sem_inc(e_ev, 1)
                if half == 0:
                    act.wait_ge(e_ev, k + 1)
                    act.dma_start(yo_d[k], dst[:]).then_inc(s_ys[k % 2], 16)

            for half in range(2):
                for t in range(FZ):
                    up_tile(half, t // 2, t % 2)
                    if t == 1:
                        if half:
                            act.wait_ge(n_h2, 2 * KT)
                        rstd_half(act, 3 + 2 * half, WIN if half == 0 else HALF, 2)
                    if half == 0 and 2 <= t < 2 + KT:
                        square_x1(1, t - 2)
                    if half == 0 and t == 1 + KT:
                        rstd_half(act, 4, WIN, 2)
                with act.Fori(FZ // 2, FT // 2) as i:
                    for s in range(2):
                        up_tile(half, i, s)
                act.wait_ge(c_fl, (FT + 2) * (half + 1))
                act.drain()
                for k in range(KT):
                    down_tile(half, k)
                    if half == 0:
                        h2_hi(1, k)
            act.wait_ge(e_y, KT)
            rstd_half(act, 6, HALF, 0)

        @block.scalar
        def _(act):
            nc.scalar.preload_act_table_set("natural_log_exp_and_others")
            for k in range(KT):
                act.wait_ge(s_xl[k], 16)
                if k >= 2:
                    act.wait_ge(s_sqm, k - 1)
                nc.scalar.activation(sq0[:, k % 2], xs[:, k], ACT.Square).then_inc(s_sq, 1)
            act.wait_ge(s_sqm, KT)
            act.wait_ge(s_cst, 1)
            for c, (a, b) in enumerate(CHUNKS):
                nc.scalar.activation(rs0[:, a:b], ps[:, 2 + c, 0:b - a], ACT.Ln, bias=eps_col, scale=1.0 / D)
            act.drain()
            nc.scalar.activation(rs0[:], rs0[:], ACT.Exp, scale=-0.5).then_inc(s_rs, 1)
            for k in range(KT):
                act.wait_ge(s_xn, k + 1)
                nc.scalar.activation(ht_h[:, k], xs[:, k], ACT.Identity).then_inc(s_xh, 1)

            def evac(key_of, h, dst, bias, scale=1.0, func=ACT.Identity, rows=slice(0, P)):
                key1 = key_of(h if isinstance(h, int) else 1)
                a, b = CHUNKS[key1[2] % 3]
                src = ps[rows, key1[2] % 2, 0:b - a]
                act.wait_ge(d_done, lin(lambda k: GROUPS[key_of(k)][0] + 1, h))
                return nc.scalar.activation(dst, src, func, bias=bias, scale=scale)

            for c, (a, b) in enumerate(CHUNKS):
                evac(lambda k, c=c: ("if", 0, c), 0, r_if[:, a:b], colt[:, C_IF:C_IF + 1]).then_inc(ev_act, 1)

            def evac_m(g, h, shift=0):
                a, b = CHUNKS[g % 3]
                u = g // 3
                dst = (mq_t if u < 2 else mk_t)[:, u % 2, a:b]
                col = (HC_MQ if u < 2 else HC_MK) + u % 2
                if g == 0:
                    act.wait_ge(a_sel, lin(lambda k: k + shift + 1, h))
                evac(lambda k: ("M", k + shift, g), h, dst, hc[:, col:col + 1],
                     1.0 if u < 2 else DH ** -0.5).then_inc(ev_act, 1)

            for g in range(3):
                evac_m(g, 0)
            act.wait_ge(p_abs, 1)
            nc.scalar.activation(r_b[0:36], r_b[0:36], ACT.Exp, scale=-1.0)
            act.drain()
            nc.scalar.activation(r_b[0:36], r_b[0:36], ACT.Ln, bias=1.0).then_inc(p_ln, 1)
            for g in range(3, 12):
                evac_m(g, 0)
            act.wait_ge(p_80, 48)
            nc.scalar.activation(r80[0:80, 1:4], r80[0:80, 1:4], ACT.Exp)
            nc.scalar.activation(decay[:], decay[:], ACT.Exp).then_inc(p_exp, 1)

            def evac_a(g, h):
                a, b = CHUNKS[g % 3]
                u = g // 3
                if u < 4:
                    if g >= 2:
                        act.wait_ge(s_gs[g % 2], lin(lambda k: 16 * (6 * k + g // 2), h))
                    evac(lambda k: ("A", k, g), h, g_st[:, g % 2, 0:b - a],
                         hc[:, HC_G + u:HC_G + u + 1], -1.0, ACT.Exp).then_inc(ev_act, 1)
                elif u < 6:
                    evac(lambda k: ("A", k, g), h, aq_t[:, u - 4, a:b], hc[:, HC_AQ + u - 4:HC_AQ + u - 3]
                         ).then_inc(ev_act, 1)
                else:
                    for r in range(2):
                        evac(lambda k: ("A", k, g), h, kk_t[r * HD:(r + 1) * HD, a:b],
                             hc[0:HD, HC_AKV:HC_AKV + 1], rows=slice(0, HD))
                    evac(lambda k: ("A", k, g), h, av_t[HD:P, a:b], hc[HD:P, HC_AKV:HC_AKV + 1],
                         rows=slice(HD, P)).then_inc(ev_act, 1)

            def mlstm(h):
                act.wait_ge(m_sel, lin(lambda k: k + 1, h))
                for i in range(NB):
                    act.wait_ge(m_e, lin(lambda k: NB * k + i + 1, h))
                    nc.scalar.activation(ex[:], ex[:], ACT.Exp).then_inc(m_x, 1)
                    if i >= 5:
                        act.wait_ge(m_ol, lin(lambda k: 32 * (5 * k + i - 4), h))
                        nc.scalar.activation(o_ld[:], o_ld[:], ACT.Exp, scale=-1.0).then_inc(m_ze, 1)
                    evac_a(2 * i, h)
                    inter = [d for d in range(2) if not fresh(d, i)]
                    if inter:
                        act.wait_ge(m_nd, lin(lambda k: NB * k + i + 1, h))
                        for d in inter:
                            last = nc.scalar.activation(nd[:, d], ps[:, 3 + 2 * d, 0:DH + 1], ACT.Copy,
                                                        scale=hc[:, d * NB + chunk_of(d, i):d * NB + chunk_of(d, i) + 1])
                        last.then_inc(m_qc, 1)
                    if i > 5:
                        finish_y(i - 1, h)
                    evac_a(2 * i + 1, h)
                    if i >= 5:
                        rstd(i, h)
                    if i >= 4 and i < NB - 1:
                        load_o(i + 1, h)
                evac_a(20, h)
                finish_y(NB - 1, h)

            def load_o(i, h):
                if i > 5:
                    act.wait_ge(m_yn, lin(lambda k: 5 * k + i - 5, h))
                for s in range(2):
                    act.wait_ge(s_os[s], lin(lambda k: 16 * 5 * (k + 1), h))
                for d in range(2):
                    act.dma_start(o_ld[:, d, :], zo[bass.ds(h, 1), chunk_of(d, i)]
                                  .rearrange("o p t -> (o p) t")).then_inc(m_ol, 16)

            def rstd(i, h):
                act.wait_ge(m_ss, lin(lambda k: 5 * k + i - 4, h))
                nc.scalar.activation(small[:, 8:10], small[:, 6:8], ACT.Ln, bias=eps_col, scale=1.0 / DH)
                act.drain()
                nc.scalar.activation(small[:, 10:12], small[:, 8:10], ACT.Exp, scale=-0.5).then_inc(m_rs, 1)

            def finish_y(i, h):
                act.wait_ge(m_y, lin(lambda k: 5 * k + i - 4, h))
                if i > 5:
                    act.wait_ge(s_ym, lin(lambda k: 32 * (5 * k + i - 5), h))
                for dt in range(2):
                    last = nc.scalar.activation(y_st[:, dt], ps[:, 7, 256 * dt:256 * dt + 256]
                                                .rearrange("p (c t) -> p c t", c=2), ACT.Copy,
                                                scale=hc[:, HC_MLN + dt:HC_MLN + dt + 1])
                last.then_inc(m_ye, 1)
                act.wait_ge(m_ye, lin(lambda k: 5 * k + i - 4, h))
                for d in range(2):
                    c = chunk_of(d, i)
                    act.dma_start(ym_d.rearrange("(h e p) t -> h p e t", e=2, p=P)[bass.ds(h, 1), :, :, c * P:(c + 1) * P]
                                  .rearrange("o p e t -> (o p) e t"), y_st[:, :, d, :]).then_inc(s_ym, 16)

            def exps(j, h):
                act.wait_ge(a_m, lin(lambda k: NB * k + j + 1, h))
                kb = kblocks(j)
                a, b = (kb[0] - j + 1) * P, (kb[-1] - j + 2) * P
                for r in range(QPG):
                    nc.scalar.activation(prob[:, r, a:b], prob[:, r, a:b], ACT.Exp, bias=small[:, 20 + r:21 + r],
                                         scale=HD ** -0.5, accum_out=small[:, 24 + r:25 + r])
                nc.scalar.activation(small[:, 32:36], small[:, 28:32], ACT.Exp).then_inc(a_x, 1)

            def evac_pt(j, h):
                act.wait_ge(a_t, lin(lambda k: NB * k + j + 1, h))
                for n in range(len(kblocks(j))):
                    last = nc.scalar.activation(prob_t[:, n], ps[:, 5 + n, :], ACT.Copy)
                last.then_inc(a_pt, 1)

            def evac_o(j, h):
                act.wait_ge(a_v, lin(lambda k: NB * k + j + 1, h))
                if j > 0:
                    act.wait_ge(s_ya, lin(lambda k: 16 * (NB * k + j), h))
                nc.scalar.activation(ya_st[:], ps[0:HD, 5, :].rearrange("p (r t) -> p r t", r=QPG),
                                     ACT.Copy).then_inc(a_o, 1)
                act.wait_ge(a_o, lin(lambda k: NB * k + j + 1, h))
                act.dma_start(ya_d.rearrange("(h r p) t -> h p r t", r=QPG, p=HD)[bass.ds(h, 1), :, :, j * P:(j + 1) * P]
                              .rearrange("o p r t -> (o p) r t"), ya_st[:]).then_inc(s_ya, 16)

            def attend(h, dense):
                exps(0, h)
                for j in range(NB):
                    if dense and 2 * j < 12:
                        evac_m(2 * j, h, 1)
                    evac_pt(j, h)
                    if j + 1 < NB:
                        exps(j + 1, h)
                    if not dense and j < 3:
                        for k in range(3 * j, min(3 * j + 3, KT)):
                            act.wait_ge(s_ymr[k], 16)
                            nc.scalar.activation(yh[:, k], ym_raw[:, k], ACT.Identity).then_inc(b_hi, 1)
                    if dense and 2 * j + 1 < 12:
                        evac_m(2 * j + 1, h, 1)
                    evac_o(j, h)
                for s in range(2):
                    act.wait_ge(s_gs[s], lin(lambda k: 16 * 6 * (k + 1), h))
                act.wait_ge(s_ym, lin(lambda k: 160 * (k + 1), h))

            with act.Fori(0, HEADS - 1) as h:
                mlstm(h)
                attend(h, True)
            mlstm(HEADS - 1)
            attend(HEADS - 1, False)
            halves_act(act)

        @block.vector
        def _(dve):
            V = nc.vector
            V.memset(ones0[:], 1.0)
            V.memset(eps_col, EPS).then_inc(s_cst, 1)
            for r in range(16):
                V.memset(slope8[:, r:r + 1], -(2.0 ** (-8.0 * (r + 1) / 16)) * HD ** 0.5)
            dve.wait_ge(s_cstp, 1)
            V.scalar_tensor_tensor(absrel[:], absrel[:], -1.0, absrel[:], ALU.mult, ALU.max)
            dve.drain()
            V.tensor_scalar(g_st[:, 0, 0:3 * P], absrel[:], float(P), BIG, ALU.is_gt, ALU.mult)
            dve.drain()
            V.tensor_tensor(absrel[:], absrel[:], g_st[:, 0, 0:3 * P], ALU.max)
            dve.wait_ge(s_cols, 32)
            V.tensor_scalar(colt[:, C_MK:C_MK + 8], colt[:, C_MK:C_MK + 8], DH ** -0.5, None, ALU.mult)
            V.tensor_scalar(colt[:, C_G:C_G + 16], colt[:, C_G:C_G + 16], -1.0, None, ALU.mult)
            dve.drain()
            V.tensor_copy(hc[:, HC_MQ:HC_MQ + 2], colt[:, C_MQ:C_MQ + 2])
            V.tensor_copy(hc[:, HC_MK:HC_MK + 2], colt[:, C_MK:C_MK + 2]).then_inc(a_sel, 1)
            dve.wait_ge(s_rs, 1)
            for k in range(KT + 1):
                if k < KT:
                    V.scalar_tensor_tensor(xs[:, k], xs[:, k], colt[:, C_PRE + k:C_PRE + k + 1], rs0[:],
                                           ALU.mult, ALU.mult).then_inc(s_xn, 1)
                if k > 0:
                    dve.wait_ge(s_xh, k)
                    V.tensor_tensor(ht_l[:, k - 1], xs[:, k - 1], ht_h[:, k - 1].bitcast(F32),
                                    ALU.subtract).then_inc(s_ht, 1)
            dve.drain()
            V.memset(v_tok[:, :, DH:DH + 1], 1.0)
            V.memset(r_li[0:36], 0.0)
            V.memset(r_f[0:36], 0.0)
            V.memset(r_m[0:36], 0.0)
            V.memset(r_mp[0:36], 0.0)
            dve.drain()
            V.memset(r_rst[0:36], 1.0).then_inc(p_z, 1)
            dve.drain()
            V.memset(r_rst[0:4].rearrange("p (c t) -> p c t", t=P)[:, :, 0:1], 0.0)
            V.memset(r_rst[32:36].rearrange("p (c t) -> p c t", t=P)[:, :, P - 1:P], 0.0)
            dve.wait_ge(p_in, 64)
            V.tensor_scalar(r_f[0:36], r_f[0:36], FORGET_BIAS, None, ALU.add)
            dve.drain()
            V.scalar_tensor_tensor(r_b[0:36], r_f[0:36], -1.0, r_f[0:36], ALU.mult, ALU.max).then_inc(p_abs, 1)
            dve.wait_ge(p_ln, 1)
            V.scalar_tensor_tensor(r_f[0:36], r_f[0:36], 0.0, r_b[0:36], ALU.min, ALU.subtract)
            dve.drain()
            V.tensor_tensor_scan(r_b[0:4], r_rst[0:4], r_f[0:4], 0.0, ALU.mult, ALU.add)
            V.tensor_tensor_scan(r_b[32:36][:, ::-1], r_rst[32:36][:, ::-1], r_f[32:36][:, ::-1], 0.0,
                                 ALU.mult, ALU.add)
            for a, b in ((0, SEQ_A), (SEQ_A, T)):
                V.tensor_tensor_scan(r_m[0:4, a:b], r_f[0:4, a:b], r_li[0:4, a:b], 0.0, ALU.add, ALU.max)
                V.tensor_tensor_scan(r_m[32:36, a:b][:, ::-1], r_f[32:36, a:b][:, ::-1],
                                     r_li[32:36, a:b][:, ::-1], 0.0, ALU.add, ALU.max)
            dve.drain()
            mch = r_m[:, :].rearrange("p (c t) -> p c t", t=P)
            for lo, hi in ((0, NB_A), (NB_A, NB)):
                V.tensor_copy(r_mp[0:4, lo + 1:hi].unsqueeze(2), mch[0:4, lo:hi - 1, P - 1:P])
                V.tensor_copy(r_mp[32:36, lo:hi - 1].unsqueeze(2), mch[32:36, lo + 1:hi, 0:1])
            V.tensor_tensor(r_u[0:36], r_b[0:36], r_m[0:36], ALU.subtract)
            V.tensor_tensor(r_li[0:36], r_li[0:36], r_b[0:36], ALU.subtract)
            dve.drain()
            uch = r_u[:, :].rearrange("p (c t) -> p c t", t=P)
            ulast = small[:, 40:50]
            V.tensor_copy(ulast[0:36].unsqueeze(2), uch[0:36, :, P - 1:P])
            dve.drain()
            V.tensor_copy(ulast[32:36].unsqueeze(2), uch[32:36, :, 0:1])
            dve.drain()
            V.tensor_tensor(r_dec[0:36], ulast[0:36], r_mp[0:36], ALU.add)
            V.tensor_tensor(r_f[0:36].rearrange("p (c t) -> p c t", t=P), uch[0:36],
                            r_mp[0:36].unsqueeze(2).to_broadcast([36, NB, P]), ALU.add)
            V.tensor_tensor(r_b[0:36].rearrange("p (c t) -> p c t", t=P),
                            r_li[0:36].rearrange("p (c t) -> p c t", t=P),
                            ulast[0:36].unsqueeze(2).to_broadcast([36, NB, P]), ALU.add)
            V.tensor_scalar(r_m[0:36], r_m[0:36], -1.0, None, ALU.mult).then_inc(p_args, 1)

            def evac_vo(blk, h, shift=0):
                hh = h
                dve.wait_ge(d_done, lin(lambda k: GROUPS[("M", k + shift, 12 + blk)][0] + 1, hh))
                if blk == 0:
                    dve.wait_ge(s_bvo, lin(lambda k: 16 * (k + shift + 1), hh))
                if blk >= 2:
                    dve.wait_ge(s_os[blk % 2], lin(lambda k: 16 * (5 * (k + shift) + blk // 2), hh))
                elif shift:
                    dve.wait_ge(s_os[blk % 2], lin(lambda k: 16 * 5 * (k + shift), hh))
                bank = (12 + blk) % 2
                V.tensor_tensor(v_tok[:, blk, 0:DH], ps[:, bank, 0:DH], bias_vo[:, 0:DH], ALU.add)
                V.tensor_tensor(o_st[:, blk % 2], ps[:, bank, DH:2 * DH], bias_vo[:, DH:2 * DH],
                                ALU.add).then_inc(ev_dve, 1)

            for blk in range(NB):
                evac_vo(blk, 0)
            dve.wait_ge(p_col, 1)
            V.tensor_copy(tokcol[:], ps[:, 2, 0:320].rearrange("p (q r) -> p q r", q=4)).then_inc(p_tc, 1)

            def evac_gate(g, h):
                if g < 0 or g >= 12:
                    return
                a, b = CHUNKS[g % 3]
                pos = g
                dve.wait_ge(ev_act, lin(lambda k: GROUPS[("A", k, g)][3], h))
                st = g_st[:, pos % 2, 0:b - a]
                V.tensor_scalar(st, st, 1.0, None, ALU.add)
                dve.drain()
                V.reciprocal(st, st).then_inc(s_g1, 1)

            def mlstm(h):
                dve.drain()
                for d in range(2):
                    V.tensor_copy(pick[0:80, d * NB:(d + 1) * NB],
                                  ident[0:80, bass.ds(h * NB + d * HEADS * NB, NB)])
                    V.tensor_copy(hc[:, d * NB:(d + 1) * NB],
                                  tokcol[:, 1, bass.ds(h * NB + d * HEADS * NB, NB)])
                V.tensor_copy(hc[:, HC_AQ:HC_AQ + 2], colt[:, bass.ds(h * 2 + C_AQ, 2)])
                V.tensor_copy(hc[:, HC_AKV:HC_AKV + 1], colt[:, bass.ds(h + C_AKV, 1)])
                V.tensor_copy(hc[:, HC_G:HC_G + 4], colt[:, bass.ds(h * 4 + C_G, 4)])
                V.tensor_copy(hc[:, HC_MLN:HC_MLN + 2], colt[:, bass.ds(h * 2 + C_MLN, 2)]).then_inc(m_sel, 1)
                for i in range(NB):
                    step = lambda k, i=i: NB * k + i + 1
                    ch = [chunk_of(d, i) for d in range(2)]
                    dve.wait_ge(m_sc, lin(step, h))
                    for d in range(2):
                        last = V.scalar_tensor_tensor(ex[:, d], ps[:, 2, 256 * d + P:256 * d + 2 * P],
                                                      tcol(0, d, h, ch[d]), mask[:, d], ALU.add, ALU.add)
                    last.then_inc(m_e, 1)
                    for d in range(2):
                        last = V.tensor_scalar(wk[:, d], ps[:, 7, 256 * d:256 * d + 256], tcol(3, d, h, ch[d]),
                                               None, ALU.mult)
                    last.then_inc(m_wk, 1)
                    dve.wait_ge(m_x, lin(step, h))
                    V.tensor_tensor(ex[:], ex[:], ps[:, 2, :].rearrange("p (d e t) -> p d e t", d=2, e=2)[:, :, 0, :],
                                    ALU.mult).then_inc(m_a, 1)
                    evac_gate(2 * i - 1, h)
                    dve.wait_ge(m_nd, lin(step, h))
                    if any(not fresh(d, i) for d in range(2)):
                        dve.wait_ge(m_qc, lin(lambda k: 9 * k + i, h))
                    for d in range(2):
                        if fresh(d, i):
                            last = V.tensor_copy(nd[:, d], ps[:, 4 + 2 * d, 0:DH + 1])
                        else:
                            last = V.tensor_tensor(nd[:, d], nd[:, d], ps[:, 4 + 2 * d, 0:DH + 1], ALU.add)
                    last.then_inc(m_ndx, 1)
                    dve.drain()
                    V.scalar_tensor_tensor(small[:, 4:6], nd[:, :, DH], -1.0, nd[:, :, DH], ALU.mult, ALU.max)
                    dve.drain()
                    for d in range(2):
                        V.tensor_tensor(small[:, d:d + 1], small[:, 4 + d:5 + d], tcol(2, d, h, ch[d]), ALU.max)
                    dve.drain()
                    V.reciprocal(small[:, 2:4], small[:, 0:2])
                    dve.drain()
                    for d in range(2):
                        if i < 5:
                            V.tensor_scalar(h_acc[:, ch[d]], nd[:, d, 0:DH], small[:, 2 + d:3 + d], None, ALU.mult)
                        else:
                            V.scalar_tensor_tensor(h_acc[:, ch[d]], nd[:, d, 0:DH], small[:, 2 + d:3 + d],
                                                   h_acc[:, ch[d]], ALU.mult, ALU.add)
                    evac_gate(2 * i, h)
                    if i + 1 < NB:
                        dve.wait_ge(m_cu, lin(lambda k: 9 * k + i + 1, h))
                        for d in range(2):
                            if not updates(d, i):
                                continue
                            for dt in range(2):
                                src = ps[:, 3 + 2 * d + dt, 0:DH + 1]
                                if fresh(d, i):
                                    last = V.tensor_copy(c_st[:, d, dt], src)
                                else:
                                    last = V.scalar_tensor_tensor(
                                        c_st[:, d, dt], c_st[:, d, dt],
                                        decay[:, bass.ds(h * NB + (d * HEADS * NB + ch[d]), 1)], src,
                                        ALU.mult, ALU.add)
                        last.then_inc(m_c, 1)
                    if i >= 5:
                        dve.wait_ge(m_ze, lin(lambda k: 5 * k + i - 4, h))
                        V.tensor_scalar(o_ld[:], o_ld[:], 1.0, None, ALU.add)
                        dve.drain()
                        V.reciprocal(o_ld[:], o_ld[:])
                        dve.drain()
                        for d in range(2):
                            V.tensor_tensor(h_acc[:, ch[d]], h_acc[:, ch[d]], o_ld[:, d], ALU.mult)
                        dve.drain()
                        for d in range(2):
                            last = V.scalar_tensor_tensor(o_ld[:, d], h_acc[:, ch[d]], 1.0, h_acc[:, ch[d]],
                                                          ALU.mult, ALU.mult, accum_out=small[:, 6 + d:7 + d])
                        last.then_inc(m_ss, 1)
                        dve.wait_ge(m_rs, lin(lambda k: 5 * k + i - 4, h))
                        for d in range(2):
                            last = V.tensor_scalar(h_acc[:, ch[d]], h_acc[:, ch[d]], small[:, 10 + d:11 + d],
                                                   None, ALU.mult)
                        last.then_inc(m_yn, 1)

            def soften(j, h):
                kb = kblocks(j)
                a, b = (kb[0] - j + 1) * P, (kb[-1] - j + 2) * P
                dve.wait_ge(a_s_done, lin(lambda k: NB * k + j + 1, h))
                flat = ps[:, 2:5, :].rearrange("p b t -> p (b t)")
                if j > 0:
                    dve.wait_ge(a_t, lin(lambda k: NB * k + j, h))
                for r in range(QPG):
                    V.scalar_tensor_tensor(prob[:, r, a:b], absrel[:, a:b], slope8[:, bass.ds(h * QPG + r, 1)],
                                           flat[:, S_AT[r] + a:S_AT[r] + b], ALU.mult, ALU.add)
                dve.drain()
                V.tensor_reduce(small[:, 16:20], prob[:, :, a:b], AX.X, ALU.max)
                dve.drain()
                V.scalar_tensor_tensor(small[:, 16:20], sinks[:, bass.ds(h * QPG, QPG)], HD ** 0.5, small[:, 16:20],
                                       ALU.mult, ALU.max)
                dve.drain()
                V.tensor_scalar(small[:, 20:24], small[:, 16:20], -(HD ** -0.5), None, ALU.mult)
                dve.drain()
                V.tensor_tensor(small[:, 28:32], sinks[:, bass.ds(h * QPG, QPG)], small[:, 20:24],
                                ALU.add).then_inc(a_m, 1)
                dve.wait_ge(a_x, lin(lambda k: NB * k + j + 1, h))
                V.tensor_tensor(small[:, 36:40], small[:, 32:36], small[:, 24:28], ALU.add)
                dve.drain()
                V.reciprocal(small[:, 36:40], small[:, 36:40])
                dve.drain()
                for r in range(QPG):
                    last = V.tensor_scalar(prob[:, r, a:b], prob[:, r, a:b], small[:, 36 + r:37 + r], None, ALU.mult)
                last.then_inc(a_p, 1)

            def next_columns(h):
                V.tensor_copy(hc[:, HC_MQ:HC_MQ + 2], colt[:, bass.ds(h * 2 + C_MQ, 2)])
                V.tensor_copy(hc[:, HC_MK:HC_MK + 2], colt[:, bass.ds(h * 2 + C_MK, 2)]).then_inc(a_sel, 1)

            def gate_product(n):
                dve.wait_ge(b_done, n + 1)
                dve.wait_ge(s_gw[n % 4], 16 * (n // 4 + 1))
                a, b = CHUNKS[n % 3]
                V.tensor_tensor(gw[:, n % 4, 0:b - a], gw[:, n % 4, 0:b - a], ps[:, n % 2, 0:b - a],
                                ALU.mult).then_inc(b_mix, 1)

            def attend(h, dense):
                dve.drain()
                if dense:
                    next_columns(h + 1)
                dve.wait_ge(a_avt, lin(lambda k: k + 1, h))
                for n in range(2):
                    last = V.tensor_copy(av_tok[:, 5 * n:5 * n + 5], ps[:, 6 + n, 0:320]
                                         .rearrange("p (c e) -> p c e", c=5))
                last.then_inc(a_av, 1)
                dve.wait_ge(m_y, lin(lambda k: 5 * (k + 1), h))
                soften(0, h)
                for j in range(NB):
                    if dense and 2 * j >= 12:
                        evac_vo(2 * j - 12, h, 1)
                    if not dense and j >= 3:
                        gate_product(2 * j - 6)
                    if j + 1 < NB:
                        soften(j + 1, h)
                    if dense and 2 * j + 1 >= 12:
                        evac_vo(2 * j + 1 - 12, h, 1)
                    if not dense and j >= 3:
                        gate_product(2 * j - 5)
                if dense:
                    evac_vo(8, h, 1)
                    evac_vo(9, h, 1)
                else:
                    for n in range(2 * NB - 6, 3 * KT):
                        gate_product(n)
                dve.wait_ge(s_ya, lin(lambda k: 16 * NB * (k + 1), h))
                dve.wait_ge(m_ye, lin(lambda k: 5 * (k + 1), h))

            with dve.Fori(0, HEADS - 1) as h:
                mlstm(h)
                attend(h, True)
            mlstm(HEADS - 1)
            attend(HEADS - 1, False)

            for k in range(KT):
                dve.wait_ge(b_hi, KT + k + 1)
                V.tensor_tensor(yl[:, k], ya_raw[:, k], yh[:, k].bitcast(F32), ALU.subtract).then_inc(b_alo, 1)
            dve.drain()
            with dve.Fori(0, KT // 2) as i:
                for g in range(6):
                    s, (a, b) = g // 3, ACH[g % 3]
                    ga, mb = g_ld[:, g % 2, 0, 0:b - a], g_ld[:, g % 2, 1, 0:b - a]
                    dve.wait_ge(s_gl[g % 2], i * 96 + 32 * (g // 2 + 1))
                    dve.wait_ge(b_done, i * 6 + (3 * KT + g + 1))
                    V.tensor_tensor(ga, ga, ps[:, g, 0:b - a], ALU.mult)
                    dve.drain()
                    V.tensor_tensor(ga, ga, mb, ALU.add)
                    dve.drain()
                    hi = mg_h[:, bass.ds(i * 2 + s, 1), a:b].rearrange("p o t -> p (o t)")
                    lo = mg_l[:, bass.ds(i * 2 + s, 1), a:b].rearrange("p o t -> p (o t)")
                    V.tensor_scalar(hi, ga, 1.0, None, ALU.mult)
                    dve.drain()
                    V.tensor_tensor(lo, ga, hi.bitcast(F32), ALU.subtract)
                    dve.drain()
                    dve.sem_inc(b_ml, 1)
                    dve.sem_inc(b_mix, 1)
            dve.drain()
            V.memset(ones[:], 1.0)
            dve.drain()

            def add_squares(st, m, k):
                if k == 0:
                    return
                slots = 4 if st == 0 else 1
                for c, (a, b) in enumerate(WCH if st_width(st, m) == WIN else OCH):
                    j = 2 * k + c - 2
                    dve.wait_ge(q_sq[st], 16 * m + j + 3)
                    V.tensor_tensor(acc[st][:, a:b], acc[st][:, a:b], sq[st][:, j % slots, 0:b - a], ALU.add)
                    dve.drain()
                    dve.sem_inc(q_acc[st], 1)

            def residual(g, k):
                V.scalar_tensor_tensor(x1[g][:, k], x1[g][:, k], colt[:, C_POSTMIX + k:C_POSTMIX + k + 1], rs[:],
                                       ALU.mult, ALU.mult)
                dve.drain()
                V.tensor_tensor(x1[g][:, k], x1[g][:, k], xr[g][:, k], ALU.add).then_inc(n_x1, 1)

            def h2_value(g, k):
                V.scalar_tensor_tensor(xr[g][:, k], x1[g][:, k], colt[:, C_PREFFN + k:C_PREFFN + k + 1], rs[:],
                                       ALU.mult, ALU.mult).then_inc(n_h2, 1)

            def h2_lo(g, k):
                dve.wait_ge(n_hh, g * KT + k + 1)
                V.tensor_tensor(h2_l[:, k], h2_raw[:, k], h2_h[:, k].bitcast(F32), ALU.subtract).then_inc(n_hl, 1)

            for k in range(KT):
                add_squares(0, 0, k)
            add_squares(1, 0, 0)
            dve.wait_ge(n_rs, 1)
            dve.wait_ge(s_xr, 16)
            for k in range(KT):
                residual(0, k)
                add_squares(0, 1, k)
                if k in (1, 4, 7):
                    add_squares(1, 0, (k + 2) // 3)
            add_squares(1, 0, 4)
            dve.wait_ge(n_rs, 2)
            for k in range(KT):
                h2_value(0, k)
                if k:
                    h2_lo(0, k - 1)
                if k in (2, 5):
                    add_squares(1, 0, 5 + k // 3)
            h2_lo(0, KT - 1)
            add_squares(1, 0, 7)

            def up_tile(half, i, s, f_hi, f_lo):
                if half == 0:
                    segments = [(0, 256, 0), (256, HALF, 257)]
                else:
                    segments = [(0, HALF, 1)]
                dve.wait_ge(c_ae, i * 2 + (half * FT + s + 1))
                if isinstance(i, int):
                    col = lambda n: colt[:, 2 * i + C_CW + n * FT + s:2 * i + C_CW + n * FT + s + 1]
                else:
                    col = lambda n: colt[:, bass.ds(i * 2 + (C_CW + n * FT + s), 1)]
                for a, b, o in segments:
                    V.tensor_scalar(cv[:, a:b], a_s[:, o + 1:o + 1 + b - a], col(1), col(3), ALU.mult, ALU.add)
                dve.drain()
                for a, b, o in segments:
                    V.scalar_tensor_tensor(cv[:, a:b], a_s[:, o:o + b - a], col(0), cv[:, a:b], ALU.mult, ALU.add)
                dve.drain()
                for a, b, o in segments:
                    last = V.scalar_tensor_tensor(cv[:, a:b], a_s[:, o + 2:o + 2 + b - a], col(2), cv[:, a:b],
                                                  ALU.mult, ALU.add)
                last.then_inc(c_cv, 1)
                dve.wait_ge(c_ge, i * 2 + (half * FT + s + 1))
                dve.wait_ge(s_used, i * 4 + used(B_UP[half] + 2 * s + 1))
                for c, (a, b) in enumerate(OCH):
                    V.tensor_tensor(fs[:, a:b], fs[:, a:b], ps[:, 4 * s + 2 + c, 0:b - a], ALU.mult)
                dve.drain()
                V.tensor_scalar(f_hi, fs[:], 1.0, None, ALU.mult)
                dve.drain()
                V.tensor_tensor(f_lo, fs[:], f_hi.bitcast(F32), ALU.subtract).then_inc(c_fl, 1)

            def final(half, k):
                V.scalar_tensor_tensor(yo[half][:, k], yo[half][:, k], colt[:, C_POSTFFN + k:C_POSTFFN + k + 1],
                                       rs[:, 0:HALF], ALU.mult, ALU.mult)
                dve.drain()
                V.tensor_tensor(yo[half][:, k], yo[half][:, k], xo[half][:, k], ALU.add).then_inc(e_y, 1)

            for half in range(2):
                dve.drain()
                if half == 0:
                    dve.wait_ge(s_used, used(B_OUT[1] + KT - 1))
                    V.memset(a_s[:, 0:1], 0.0)
                    V.memset(a_s[:, 257:258], 0.0).then_inc(c_pad, 1)
                else:
                    for n in range(2):
                        dve.wait_ge(s_ys[n], 16 * KT // 2)
                    V.memset(a_s[:, WIN:WIN + 1], 0.0).then_inc(c_pad, 1)
                dve.drain()
                dve.sem_inc(c_cv, 1)
                dve.sem_inc(c_fl, 2)
                for t in range(FZ):
                    up_tile(half, t // 2, t % 2, f_z[:, t, 0], f_z[:, t, 1])
                    if half == 0:
                        if t == 1:
                            dve.wait_ge(n_rs, 3)
                            dve.wait_ge(s_xr, 32)
                        if 2 <= t < 2 + KT:
                            residual(1, t - 2)
                            add_squares(1, 1, t - 2)
                        if t == 1 + KT:
                            dve.wait_ge(n_rs, 4)
                        if t in (2 + KT, 3 + KT):
                            for k in range(4):
                                h2_value(1, 4 * (t - 2 - KT) + k)
                    else:
                        if t == 1:
                            dve.wait_ge(n_rs, 5)
                            dve.wait_ge(s_fo, 32)
                        if 2 <= t < 2 + KT:
                            final(0, t - 2)
                if half == 0:
                    dve.wait_ge(s_x1, 32)
                    dve.wait_ge(s_h2, 16)
                else:
                    dve.wait_ge(s_out, 16)
                with dve.Fori(FZ // 2, FT // 2) as i:
                    for s in range(2):
                        f_hi, f_lo = [f_x[:, bass.ds(i * 2 + (s - FZ), 1), part, :].rearrange("p o t -> p (o t)")
                                      for part in range(2)]
                        up_tile(half, i, s, f_hi, f_lo)
                for k in range(KT):
                    add_squares(1, 2 + half, k)
                    if half == 0:
                        h2_lo(1, k)
            dve.wait_ge(n_rs, 6)
            dve.wait_ge(s_fo, 48)
            for k in range(KT):
                final(1, k)

        @block.tensor
        def _(pe):
            mm = nc.tensor.matmul

            def dense(out_ap, slot, rhs, kts=KT, k_first=0, first=True, last=True, before=None):
                hi, lo = rhs
                for k in range(kts):
                    if before is not None:
                        before(k)
                    wh = ring_h[:, k, slot * P:(slot + 1) * P]
                    wl = ring_l[:, k, slot * P:(slot + 1) * P]
                    mm(out_ap, wh, hi(k + k_first), start=first and k == 0, stop=False)
                    mm(out_ap, wh, lo(k + k_first), start=False, stop=False)
                    ins = mm(out_ap, wl, hi(k + k_first), start=False, stop=last and k == kts - 1)
                return ins

            pe.wait_ge(s_cst, 1)
            for k in range(KT):
                pe.wait_ge(s_sq, k + 1)
                for c, (a, b) in enumerate(CHUNKS):
                    ins = mm(ps[:, 2 + c, 0:b - a], ones0[:], sq0[:, k % 2, a:b], start=k == 0, stop=k == KT - 1)
                ins.then_inc(s_sqm, 1)
            pe.wait_ge(s_ht, KT)

            def unit_group(kind, u, c, h, shift=0):
                g = 3 * u + c
                unit = a_unit if kind == "A" else m_unit
                n1 = unit((1 if not isinstance(h, int) else h) + shift, u)
                a, b = CHUNKS[c]
                if c == 0:
                    pe.wait_ge(s_split, lin(lambda k: unit(k + shift, u) + 1, h))
                bank_free(pe, lambda k: (kind, k + shift, g), h)
                dense(ps[:, g % 2, 0:b - a], RING[n1],
                      (lambda k: ht_h[:, k, a:b], lambda k: ht_l[:, k, a:b])).then_inc(d_done, 1)

            def vo_group(blk, h, shift=0):
                g = 12 + blk
                if blk == 0:
                    pe.wait_ge(s_split, lin(lambda k: m_unit(k + shift, 7) + 1, h))
                bank_free(pe, lambda k: ("M", k + shift, g), h)
                t = slice(blk * P, (blk + 1) * P)
                for k in range(KT):
                    mm(ps[:, g % 2, :], ht_h[:, k, t], ring_h[:, k, :], start=k == 0, stop=False)
                    mm(ps[:, g % 2, :], ht_h[:, k, t], ring_l[:, k, :], start=False, stop=False)
                    ins = mm(ps[:, g % 2, :], ht_l[:, k, t], ring_h[:, k, :], start=False, stop=k == KT - 1)
                ins.then_inc(d_done, 1)

            def m_dense(g, h, shift=0):
                if g < 12:
                    unit_group("M", g // 3, g % 3, h, shift)
                else:
                    vo_group(g - 12, h, shift)

            for c, (a, b) in enumerate(CHUNKS):
                if c == 0:
                    pe.wait_ge(s_split, 1)
                bank = c % 2
                if c == 2:
                    pe.wait_ge(ev_act, 1)
                dense(ps[:, bank, 0:b - a], RING[0],
                      (lambda k: ht_h[:, k, a:b], lambda k: ht_l[:, k, a:b])).then_inc(d_done, 1)
            for g in range(22):
                m_dense(g, 0)
            pe.wait_ge(p_exp, 1)
            pe.wait_ge(s_cstp, 1)
            for q in range(4):
                ins = nc.tensor.transpose(ps[:, 2, 80 * q:80 * q + 80], r80[0:80, q], ident[0:80, 0:80])
            ins.then_inc(p_col, 1)
            pe.wait_ge(p_tc, 1)

            def m_scores(i, h):
                pe.wait_ge(m_sel, lin(lambda k: k + 1, h))
                if i > 6:
                    pe.wait_ge(m_ye, lin(lambda k: 5 * k + i - 6, h))
                if i == 0:
                    pe.wait_ge(ev_act, lin(lambda k: GROUPS[("M", k, 11)][3], h))
                    pe.wait_ge(ev_dve, lin(lambda k: GROUPS[("M", k, 21)][3], h))
                for d in range(2):
                    c = chunk_of(d, i)
                    t = slice(c * P, (c + 1) * P)
                    for dt in range(2):
                        nc.tensor.transpose(ps[:, 7, 256 * d + P * dt:256 * d + P * dt + P], mk_t[:, dt, t], ident[:])
                    for dt in range(2):
                        mm(ps[:, 2, 256 * d:256 * d + P], mk_t[:, dt, t], mq_t[:, dt, t], start=dt == 0, stop=dt == 1)
                    j = d * NB + c
                    ins = mm(ps[:, 2, 256 * d + P:256 * d + 2 * P], pick[0:80, j:j + 1].to_broadcast([80, P]),
                             urows[:], start=True, stop=True)
                ins.then_inc(m_sc, 1)

            def m_numden(i, h):
                if i > 0:
                    pe.wait_ge(m_c, lin(lambda k: 9 * k + i, h))
                for d in range(2):
                    c = chunk_of(d, i)
                    if not fresh(d, i):
                        for dt in range(2):
                            mm(ps[:, 3 + 2 * d, 0:DH + 1], mq_t[:, dt, c * P:(c + 1) * P], c_st[:, d, dt],
                               start=dt == 0, stop=dt == 1)
                pe.wait_ge(m_a, lin(lambda k: NB * k + i + 1, h))
                for d in range(2):
                    ins = mm(ps[:, 4 + 2 * d, 0:DH + 1], ex[:, d], v_tok[:, chunk_of(d, i)], start=True, stop=True)
                ins.then_inc(m_nd, 1)

            def m_update(i, h):
                if i + 1 == NB:
                    return
                pe.wait_ge(m_wk, lin(lambda k: NB * k + i + 1, h))
                pe.wait_ge(m_ndx, lin(lambda k: NB * k + i + 1, h))
                for d in range(2):
                    if updates(d, i):
                        for dt in range(2):
                            ins = mm(ps[:, 3 + 2 * d + dt, 0:DH + 1], wk[:, d, dt * P:(dt + 1) * P],
                                     v_tok[:, chunk_of(d, i)], start=True, stop=True)
                ins.then_inc(m_cu, 1)

            def m_turn(i, h):
                pe.wait_ge(m_yn, lin(lambda k: 5 * k + i - 4, h))
                if i + 1 < NB:
                    pe.wait_ge(m_wk, lin(lambda k: NB * k + i + 2, h))
                else:
                    pe.wait_ge(m_wk, lin(lambda k: NB * k + i + 1, h))
                for d in range(2):
                    for dt in range(2):
                        ins = nc.tensor.transpose(ps[:, 7, 256 * dt + P * d:256 * dt + P * d + P],
                                                  h_acc[:, chunk_of(d, i), dt * P:(dt + 1) * P], ident[:])
                ins.then_inc(m_y, 1)

            def mlstm(h):
                for i in range(NB):
                    m_scores(i, h)
                    unit_group("A", (2 * i) // 3, (2 * i) % 3, h)
                    m_numden(i, h)
                    if i > 5:
                        m_turn(i - 1, h)
                    unit_group("A", (2 * i + 1) // 3, (2 * i + 1) % 3, h)
                    m_update(i, h)
                unit_group("A", 6, 2, h)
                m_turn(NB - 1, h)

            def a_scores(j, h):
                kb = kblocks(j)
                a, b = (kb[0] - j + 1) * P, (kb[-1] - j + 2) * P
                if j == 0:
                    pe.wait_ge(ev_act, lin(lambda k: GROUPS[("A", k, 8)][3], h))
                else:
                    pe.wait_ge(a_m, lin(lambda k: NB * k + j, h))
                pieces = []
                for r in (2, 0, 1, 3):
                    lo = S_AT[r] + a
                    while lo < S_AT[r] + b:
                        hi = min(S_AT[r] + b, (lo // 512 + 1) * 512)
                        pieces.append((r % 2, r % 2 == 1 and lo // 512 == 1, r, lo, hi))
                        lo = hi
                pieces.sort(key=lambda x: x[:2])
                for n, (odd, shared, r, lo, hi) in enumerate(pieces):
                    rows = slice(HD * odd, HD * odd + HD)
                    k0 = (j - 1) * P + lo - S_AT[r]
                    if shared:
                        pe.wait_ge(a_even, lin(lambda k: NB * k + j + 1, h))
                    ins = mm(ps[:, 2 + lo // 512, lo % 512:lo % 512 + hi - lo],
                             aq_t[rows, r // 2, j * P:(j + 1) * P], kk_t[rows, k0:k0 + hi - lo],
                             start=True, stop=True)
                    if not odd and pieces[n + 1][0]:
                        ins.then_inc(a_even, 1)
                ins.then_inc(a_s_done, 1)

            def a_turn(j, h):
                pe.wait_ge(a_p, lin(lambda k: NB * k + j + 1, h))
                if j > 0:
                    pe.wait_ge(a_o, lin(lambda k: NB * k + j, h))
                else:
                    pe.wait_ge(a_av, lin(lambda k: k + 1, h))
                kb = kblocks(j)
                for n, blk in enumerate(kb):
                    o = (blk - j + 1) * P
                    for r in range(QPG):
                        ins = nc.tensor.transpose(ps[:, 5 + n, r * P:(r + 1) * P], prob[:, r, o:o + P], ident[:])
                ins.then_inc(a_t, 1)

            def a_values(j, h):
                pe.wait_ge(a_pt, lin(lambda k: NB * k + j + 1, h))
                kb = kblocks(j)
                for n, blk in enumerate(kb):
                    ins = mm(ps[0:HD, 5, :], av_tok[:, blk], prob_t[:, n], start=n == 0, stop=n == len(kb) - 1)
                ins.then_inc(a_v, 1)

            def branch_m(n):
                u, (a, b) = n // 3, CHUNKS[n % 3]
                if n == 0:
                    pe.wait_ge(b_mlo, KT)
                    pe.wait_ge(ev_act, GROUP_COUNT["act"])
                if n % 3 == 0:
                    pe.wait_ge(s_split, U_B + B_MB + u + 1)
                if n >= 2:
                    pe.wait_ge(b_mix, n - 1)
                dense(ps[:, n % 2, 0:b - a], u % 4, (lambda k: yh[:, k, a:b], lambda k: yl[:, k, a:b])
                      ).then_inc(b_done, 1)

            def attend(h, is_dense):
                pe.wait_ge(m_ye, lin(lambda k: 5 * (k + 1), h))
                pe.wait_ge(m_ndx, lin(lambda k: NB * (k + 1), h))
                a_scores(0, h)
                for c in range(NB):
                    ins = nc.tensor.transpose(ps[:, 6 + c // 5, (c % 5) * HD:(c % 5 + 1) * HD],
                                              av_t[HD:P, c * P:(c + 1) * P], ident[HD:P, HD:P])
                ins.then_inc(a_avt, 1)
                for j in range(NB):
                    if is_dense:
                        m_dense(2 * j, h, 1)
                    elif j >= 3:
                        branch_m(2 * j - 6)
                    a_turn(j, h)
                    if j + 1 < NB:
                        a_scores(j + 1, h)
                    if is_dense:
                        m_dense(2 * j + 1, h, 1)
                    elif j >= 3:
                        branch_m(2 * j - 5)
                    a_values(j, h)
                if is_dense:
                    m_dense(20, h, 1)
                    m_dense(21, h, 1)
                else:
                    for n in range(2 * NB - 6, 3 * KT):
                        branch_m(n)
                pe.wait_ge(a_o, lin(lambda k: NB * (k + 1), h))

            with pe.Fori(0, HEADS - 1) as h:
                mlstm(h)
                attend(h, True)
            mlstm(HEADS - 1)
            attend(HEADS - 1, False)

            pe.wait_ge(b_mix, 3 * KT)
            for k in range(KT):
                pe.wait_ge(b_alo, k + 1)
            with pe.Fori(0, KT // 4) as i:
                for g in range(12):
                    u, (a, b) = g // 3, ACH[g % 3]
                    if g % 3 == 0:
                        pe.wait_ge(s_split, i * 4 + (U_B + B_AB + u + 1))
                    pe.wait_ge(b_mix, i * 12 + (3 * KT + g - 5))
                    dense(ps[:, g % 6, 0:b - a], u, (lambda k: yh[:, k, a:b], lambda k: yl[:, k, a:b])
                          ).then_inc(b_done, 1)

            def two_chunks(bank0, slot, hi, lo, chunks, **kw):
                for c, (a, b) in enumerate(chunks):
                    ins = dense(ps[:, bank0 + c, 0:b - a], slot, (lambda k: hi(k)[:, a:b], lambda k: lo(k)[:, a:b]),
                                **kw)
                return ins

            def feature_sum(st, m, bank):
                pe.wait_ge(q_acc[st], 14 * (m + 1))
                for c, (a, b) in enumerate(WCH if st_width(st, m) == WIN else OCH):
                    ins = mm(ps[:, bank + c, 0:b - a], ones[:], acc[st][:, a:b], start=True, stop=True)
                ins.then_inc(n_sum, 1)

            for g in range(2):
                for k in range(KT):
                    n = g * KT + k
                    before = None
                    if n == 0:
                        pe.wait_ge(b_ml, 3 * (KT - 1))
                        pe.wait_ge(b_mix, 6 * KT - 3)
                        before = lambda kk: pe.wait_ge(b_ml, 3 * KT) if kk == KT - 1 else None
                    if n >= 4:
                        pe.wait_ge(o_ev, n - 3)
                    pe.wait_ge(s_split, U_B + B_OUT[0] + n + 1)
                    t0 = g * (T - WIN)
                    two_chunks(2 * (k % 4), n % 4, lambda kk: mg_h[:, kk, t0:t0 + WIN],
                               lambda kk: mg_l[:, kk, t0:t0 + WIN], WCH, before=before).then_inc(s_used, 1)
                    if n == KT:
                        pe.wait_ge(o_ev, KT)
                        feature_sum(0, 0, 6)
                    if n == KT + 4:
                        pe.wait_ge(o_ev, KT + 4)
                        feature_sum(0, 1, 6)
                    if n in (KT + 2, KT + 6):
                        pe.wait_ge(n_rs, 1 if n == KT + 2 else 2)

            def up_tiles(half, lo, hi, sums):
                gate_ch = [(2 * half, 2 * half + 320), (2 * half + 320, 2 * half + 640)]
                with pe.Fori(lo // 2, hi // 2) as i:
                    for s in range(2):
                        pe.wait_ge(c_fl, i * 2 + (half * (FT + 2) + s + 1))
                        p = B_UP[half] + 2 * s
                        pe.wait_ge(s_split, i * 4 + (U_B + p + 1))
                        two_chunks(4 * s, 2 * s, lambda k: h2_h[:, k], lambda k: h2_l[:, k], WCH).then_inc(s_used, 1)
                        pe.wait_ge(s_split, i * 4 + (U_B + p + 2))
                        pe.wait_ge(n_rs, sums)
                        two_chunks(4 * s + 2, 2 * s + 1, lambda k: h2_h[:, k], lambda k: h2_l[:, k], gate_ch
                                   ).then_inc(s_used, 1)

            for half in range(2):
                if half == 0:
                    pe.wait_ge(o_ev, 2 * KT)
                else:
                    pe.wait_ge(e_ev, KT)
                pe.wait_ge(n_hl, KT * (half + 1))
                up_tiles(half, 0, 2, 2 + 2 * half)
                pe.wait_ge(c_fl, half * (FT + 2) + 3)
                feature_sum(1, 2 * half, 2)
                if half == 0:
                    up_tiles(half, 2, 2 + KT, 3)
                    pe.wait_ge(c_fl, KT + 3)
                    feature_sum(1, 1, 2)
                    up_tiles(half, 2 + KT, FT, 4)
                else:
                    up_tiles(half, 2, FT, 5)
                pe.wait_ge(c_fl, (FT + 2) * half + 2 + FT - 1)
                for k in range(KT):
                    if k >= 4:
                        pe.wait_ge(e_ev, half * KT + k - 3)
                    for part in range(3):
                        p = B_DOWN[half] + 3 * k + part
                        if k == 0 and part == 2:
                            pe.wait_ge(c_fl, (FT + 2) * (half + 1))
                        pe.wait_ge(s_split, U_B + p + 1)
                        two_chunks(2 * (k % 4), p % 4, lambda kk: f_tile(kk, 0), lambda kk: f_tile(kk, 1), OCH,
                                   kts=8 if part < 2 else FT - 16, k_first=8 * part, first=part == 0, last=part == 2
                                   ).then_inc(s_used, 1)
            pe.wait_ge(e_ev, 2 * KT)
            feature_sum(1, 3, 0)


def pack_units(w_in, w_att, w_mlstm, w_out, w_up, w_down):
    n_q, n_kv, n_m = D, HEADS * HD, D
    off_ak, off_av = n_q, n_q + n_kv
    off_mq = off_av + n_kv
    off_mk, off_mv, off_mo = off_mq + n_m, off_mq + 2 * n_m, off_mq + 3 * n_m
    off_if = off_mo + n_m
    off_g = off_if + 4 * HEADS

    def unit(wt, cols):
        return wt[:, cols].reshape(KT, P, P).transpose(1, 0, 2).reshape(P, KT * P)

    def sl(a):
        return slice(a, a + P)

    units = [unit(w_in, sl(off_if))]
    for h in range(HEADS):
        c = h * DH
        for o in (off_mq, off_mk, off_mo, off_mv):
            units += [unit(w_in, sl(o + c)), unit(w_in, sl(o + c + P))]
        for o in (off_g, off_g + D):
            units += [unit(w_in, sl(o + c)), unit(w_in, sl(o + c + P))]
        units += [unit(w_in, sl(c)), unit(w_in, sl(c + P))]
        kv = np.concatenate([w_in[:, off_ak + h * HD:off_ak + (h + 1) * HD],
                             w_in[:, off_av + h * HD:off_av + (h + 1) * HD]], axis=1)
        units.append(unit(kv, slice(0, P)))
    units += [unit(w_mlstm, sl(k * P)) for k in range(KT)]
    units += [unit(w_att, sl(k * P)) for k in range(KT)]
    units += [unit(w_out, sl(k * P)) for k in range(KT)]
    for f in range(FT):
        units += [unit(w_up, sl(f * P)), unit(w_up, sl(FF + f * P))]
    down = np.concatenate([w_down, np.zeros((24 * P - FF, D), w_down.dtype)], axis=0)
    for k in range(KT):
        for part in range(3):
            units.append(unit(down[part * D:(part + 1) * D], sl(k * P)))
    return np.ascontiguousarray(np.stack(units))


def pack_cols(b_in, pre, mln, postmix, preffn, postffn, conv_w, conv_b):
    n_q, n_kv, n_m = D, HEADS * HD, D
    off_mq = n_q + 2 * n_kv
    off_if = off_mq + 4 * n_m
    off_g = off_if + 4 * HEADS
    col = []
    col += list(b_in[off_mq:off_mq + D].reshape(KT, P))
    col += list(b_in[off_mq + D:off_mq + 2 * D].reshape(KT, P))
    col += list(b_in[0:D].reshape(KT, P))
    for h in range(HEADS):
        col.append(np.concatenate([b_in[n_q + h * HD:n_q + (h + 1) * HD],
                                   b_in[n_q + n_kv + h * HD:n_q + n_kv + (h + 1) * HD]]))
    for h in range(HEADS):
        for o in (off_g, off_g + D):
            col += [b_in[o + h * DH:o + h * DH + P], b_in[o + h * DH + P:o + (h + 1) * DH]]
    col.append(b_in[off_if:off_if + P])
    for v in (pre, mln, postmix, preffn, postffn):
        col += list(v.reshape(KT, P))
    for t in range(3):
        col += list(conv_w[t].reshape(FT, P))
    col += list(conv_b.reshape(FT, P))
    return np.ascontiguousarray(np.stack(col, axis=1))


def kernel(x_prompt, x_sample, pre_mix_norm, w_in, b_in, attn_sink, mlstm_norm, w_att_branch, w_mlstm_branch,
           w_out, post_mix_norm, pre_ffn_norm, w_ffn_up, ffn_conv_w, ffn_conv_b, w_ffn_down, post_ffn_norm):
    import concourse.bacc as bacc
    from concourse.bass_utils import run_bass_kernel_spmd

    a = [np.asarray(v) for v in (x_prompt, x_sample, pre_mix_norm, w_in, b_in, attn_sink, mlstm_norm, w_att_branch,
                                 w_mlstm_branch, w_out, post_mix_norm, pre_ffn_norm, w_ffn_up, ffn_conv_w,
                                 ffn_conv_b, w_ffn_down, post_ffn_norm)]
    (xp, xsm, pre, wi, bi, snk, mln, wa, wm, wo, pom, pf, wu, cw, cb, wd, pof) = a
    x = np.concatenate([xp[0], xsm[0]], axis=0)
    off_mv = D + 2 * HEADS * HD + 2 * D
    bv, bo = bi[0, off_mv:off_mv + D].reshape(HEADS, DH), bi[0, off_mv + D:off_mv + 2 * D].reshape(HEADS, DH)
    arrays = {
        "w": pack_units(wi[0], wa[0], wm[0], wo[0], wu[0], wd[0]),
        "xt": np.ascontiguousarray(x.T.reshape(KT, P, T)),
        "cols": pack_cols(bi[0], pre[0], mln[0], pom[0], pf[0], pof[0], cw[0], cb[0]),
        "bvo": np.ascontiguousarray(np.concatenate([bv, bo], axis=1)),
        "sink": np.ascontiguousarray(snk),
    }
    nc = bacc.Bacc("TRN2", target_bir_lowering=False, num_devices=1)
    args = [nc.dram_tensor(n, v.shape, mybir.dt.from_np(v.dtype), kind="ExternalInput").ap()
            for n, v in arrays.items()]
    out = nc.dram_tensor("yt", (KT, P, T), F32, kind="ExternalOutput").ap()
    build(nc, *args, out)
    r = run_bass_kernel_spmd(nc, [arrays], core_ids=[0])
    y = r.results[0]["yt"].reshape(D, T).T
    return (np.ascontiguousarray(y[:SEQ_A]).reshape(1, SEQ_A, D),
            np.ascontiguousarray(y[SEQ_A:]).reshape(1, SEQ_B, D))
```

```python
import numpy as np
import concourse.bass as bass
from concourse import mybir

F32 = mybir.dt.float32
F32R = mybir.dt.float32r
ALU = mybir.AluOpType
ACT = mybir.ActivationFunctionType
AX = mybir.AxisListType

P = 128
D = 1024
KT = D // P
SEQ_A, SEQ_B = 256, 1024
T = SEQ_A + SEQ_B
NB = T // P
NB_A = SEQ_A // P
HEADS = 4
DH = 256
HD = 64
QPG = 4
FF = 2816
FT = FF // P
EPS = 1e-6
FORGET_BIAS = 3.0
HALF = T // 2
WIN = HALF + 2
BIG = 1e30

C_MQ, C_MK, C_AQ, C_AKV, C_G, C_IF = 0, 8, 16, 24, 28, 44
C_PRE, C_MLN, C_POSTMIX, C_PREFFN, C_POSTFFN = 45, 53, 61, 69, 77
C_CW, C_CB = 85, 85 + 3 * FT
NCOL = C_CB + FT

M_UNITS, A_UNITS = 8, 7
U_B = 1 + HEADS * (M_UNITS + A_UNITS)
W_MB, W_OUT = U_B, U_B + 2 * KT
W_UP = W_OUT + KT
W_DOWN = W_UP + 2 * FT
B_MB, B_AB, B_OUT = 0, KT, (2 * KT, 3 * KT)
B_UP = (4 * KT, 7 * KT + 2 * FT)
B_DOWN = (B_UP[0] + 2 * FT, B_UP[1] + 2 * FT)
B_END = B_DOWN[1] + 3 * KT

S_AT = [3 * P * r for r in range(4)]

M_FIRST = [2, 3]
M_BESIDE = [[2 * j + 4, 2 * j + 5] for j in range(NB - 2)] + [[20], [21]]
TURN_BANK = [6, 7, 5]

CHUNKS = [(0, 512), (512, 1024), (1024, T)]
WCH = [(0, 322), (322, WIN)]
OCH = [(0, HALF // 2), (HALF // 2, HALF)]
ACH = [(0, 432), (432, 864), (864, T)]
POOL_ADDS = (1, 3, 5)
FZ = 14


def m_unit(h, k):
    return 1 + (M_UNITS + A_UNITS) * h + k


def a_unit(h, k):
    return 1 + (M_UNITS + A_UNITS) * h + M_UNITS + k


def dram_unit(p):
    for start, first in ((B_DOWN[1], W_DOWN), (B_UP[1], W_UP), (B_DOWN[0], W_DOWN), (B_UP[0], W_UP),
                         (B_OUT[1], W_OUT), (B_OUT[0], W_OUT), (0, W_MB)):
        if p >= start:
            return first + p - start


def unit_tables():
    ring, raw, last = [1], [1], [("if", 0, 2)]
    for h in range(HEADS):
        for k in range(M_UNITS):
            ring.append((2 + k) % 4)
            raw.append(k % 2)
            last.append(("M", h, 3 * k + 2 if k < 4 else 21))
        for k in range(A_UNITS):
            ring.append((3 + k) % 4)
            raw.append(k % 2)
            last.append(("A", h, 3 * k + 2))
    return ring, raw, last


RING, RAW, LAST_GROUP = unit_tables()
RING += [p % 4 for p in range(B_END)]
RAW += [p % 2 for p in range(B_END)]


def prev_user(slots, n):
    for m in range(n - 1, -1, -1):
        if slots[m] == slots[n]:
            return m
    return None


def group_tables():
    order = [("if", 0, c) for c in range(3)]
    out = {}
    for h in range(HEADS):
        order += [("M", h, g) for g in range(22)]
        order += [("A", h, g) for g in range(21)]
    count = {"act": 0, "dve": 0}
    last = {}
    for i, key in enumerate(order):
        bank = key[2] % 2
        eng = "dve" if key[0] == "M" and key[2] >= 12 else "act"
        count[eng] += 1
        out[key] = (i, bank, eng, count[eng], last.get(bank))
        last[bank] = (eng, count[eng])
    return out, count


GROUPS, GROUP_COUNT = group_tables()


def lin(f, h):
    if isinstance(h, int):
        return f(h)
    a, b = f(0), f(1)
    assert f(2) == 2 * b - a
    return h * (b - a) + a if b != a else a


def build(nc, w, xt, cols, bvo, sink, outs):
    zo = nc.dram_tensor("zo_scratch", (HEADS, NB, P, DH), F32).ap()
    gs = nc.dram_tensor("gate_scratch", (4 * HEADS, P, T), F32).ap()
    ya_d = nc.dram_tensor("ya_scratch", (D, T), F32).ap()
    ym_d = nc.dram_tensor("ym_scratch", (D, T), F32).ap()
    mb_d = nc.dram_tensor("mlstm_branch_scratch", (KT, P, T), F32).ap()
    h2_d = nc.dram_tensor("h2_scratch", (KT, P, WIN), F32).ap()
    yo_d = nc.dram_tensor("down_scratch", (KT, P, HALF), F32).ap()
    x1_d = nc.dram_tensor("x1_scratch", (2, KT, P, WIN), F32).ap()
    rows_d = nc.dram_tensor("rows_scratch", (5, 8, T), F32).ap()
    dec_d = nc.dram_tensor("decay_scratch", (8, NB), F32).ap()

    base = ((nc.sbuf_base + 63) // 64) * 64

    def at(name, off, shape, dt=F32):
        return nc.alloc_sbuf_tensor_at(name, shape, dt, offset=base + off)

    ring_h = at("ring_h", 0, [P, KT, 512], F32R)
    ring_l = at("ring_l", 16384, [P, KT, 512], F32R)
    raw = at("raw", 32768, [P, 2, KT, P])
    ht_h = at("ht_h", 40960, [P, KT, T], F32R)
    ht_l = at("ht_l", 81920, [P, KT, T], F32R)
    mq_t = at("mq_t", 122880, [P, 2, T])
    mk_t = at("mk_t", 133120, [P, 2, T])
    v_tok = at("v_tok", 143360, [P, NB, DH + 1])
    h_acc = at("h_acc", 153664, [P, NB, DH])
    c_st = at("c_st", 163904, [P, 2, 2, DH + 1])
    prob = at("prob", 153664, [P, QPG, 3 * P])
    prob_h = at("prob_h", 159808, [P, 3, QPG * P], F32R)
    prob_l = at("prob_l", 199392, [P, 3, QPG * P], F32R)
    ya_st = at("ya_st", 165952, [HD, QPG, P])
    aq_t = at("aq_t", 168032, [P, 2, T])
    kk_t = at("kk_t", 178272, [P, T])
    av_t = at("av_t", 183392, [P, T])
    ident = at("ident", 188512, [P, P])
    mask = at("mask", 189024, [P, 2, P])
    absrel = at("absrel", 190048, [P, 3 * P])
    tokcol = at("tokcol", 191584, [P, 4, 2 * HEADS * NB])
    urows = at("urows", 192864, [2 * HEADS * NB, P])
    decay = at("decay", 193376, [P, 2 * HEADS * NB])
    pick = at("pick", 193696, [P, 2 * NB])
    slope8 = at("slope8", 193792, [P, 16])
    sinks = at("sinks", 193856, [P, 16])
    bias_vo = at("bias_vo", 194240, [P, 2 * DH])
    ex = at("ex", 196288, [P, 2, P])
    nd = at("nd", 197312, [P, 2, DH + 1])
    wk = at("wk", 199392, [P, 2, DH])
    v_hl = [at("v_hl_a", 196288, [P, 6, 2, HD], F32R), at("v_hl_b", 207584, [P, NB - 6, 2, HD], F32R)]
    kk_h = at("kk_h", 183392, [P, T], F32R)
    kk_l = at("kk_l", 178272, [P, T], F32R)
    q_st = [at("q_st_first", 205536, [P, 2, 2, P], F32R), at("q_st", 209632, [P, 2, 2, P], F32R)]
    g_st = at("g_st", 201440, [P, 2, 512])
    o_st = at("o_st", 205536, [P, 2, DH])
    o_ld = at("o_ld", 207584, [P, 2, DH])
    y_st = at("y_st", 209632, [P, 2, 2, P])
    small = at("small", 211680, [P, 64])
    hc = at("hc", 211936, [P, 40])
    HC_AQ, HC_AKV, HC_G, HC_MLN, HC_MQ, HC_MK = 20, 22, 23, 27, 30, 32
    colt = at("colt", 212096, [P, NCOL + 2])
    eps_col = colt[:, NCOL:NCOL + 1]
    one_col = colt[:, NCOL + 1:NCOL + 2]
    xs = at("xs", 122880, [P, KT, T])
    sq0 = at("sq0", 168032, [P, 2, T])
    rs0 = at("rs0", 178272, [P, T])
    ones0 = at("ones0", 196288, [P, P])
    r_if = at("r_if", 203008, [P, T])
    r_li = at("r_li", 158784, [P, T])
    r_f = at("r_f", 163904, [P, T])
    r_b = at("r_b", 169024, [P, T])
    r_m = at("r_m", 174144, [P, T])
    r_u = at("r_u", 179264, [P, T])
    r_mp = at("r_mp", 184384, [P, NB])
    r_dec = at("r_dec", 184448, [P, NB])
    r80 = at("r80", 184512, [P, 4, P])
    r_rst = at("r_rst", 197312, [P, T])
    yh = ht_h
    yl = ht_l
    ym_raw = at("ym_raw", 81920, [P, KT, T])
    ya_raw = at("ya_raw", 122880, [P, KT, T])
    YA_AT = [0, 1, 2, 3, 4, 6, 7, 5]
    gw = at("gw", 148480, [P, T])
    mg_h = at("mg_h", 123136, [P, KT, T], F32R)
    mg_l = at("mg_l", 164096, [P, KT, T], F32R)
    g_ld = at("g_ld", 205056, [P, 2, 2, 432])
    x1 = [at("x1_0", 40960, [P, KT, WIN]), at("x1_1", 61504, [P, KT, WIN])]
    h2_h = at("h2_h", 82048, [P, KT, WIN], F32R)
    h2_l = at("h2_l", 102592, [P, KT, WIN], F32R)
    xr = [at("xr_0", 102592, [P, KT, WIN]), at("xr_1", 40960, [P, KT, WIN])]
    h2_raw = xr[0]
    acc = [at("acc_0", 82048, [P, WIN]), at("acc_1", 207648, [P, WIN])]
    sq = [at("sq_0", 84640, [P, 4, 322]), at("sq_1", 210240, [P, 1, 322])]
    rs = at("rs", 205056, [P, WIN])
    ones = at("ones", 211552, [P, P])
    f_z = at("f_z", 123136, [P, FZ, 2, HALF], F32R)
    f_x = at("f_x", 40960, [P, FT - FZ, 2, HALF], F32R)
    a_s = at("a_s", 194816, [P, 648])
    cv = at("cv", 197408, [P, HALF])
    fs = at("fs", 199968, [P, HALF])
    yo = [at("yo_0", 40960, [P, KT, HALF]), at("yo_1", 82048, [P, KT, HALF])]
    xo = [at("xo_0", 61440, [P, KT, HALF]), at("xo_1", 102528, [P, KT, HALF])]

    def st_width(st, m):
        return WIN if m < 2 else HALF

    ps = nc.alloc_psum_tensor("ps", [P, 8, 512], F32)

    def sem(name):
        return nc.alloc_semaphore(name)

    s_raw = [sem("raw_landed0"), sem("raw_landed1")]
    s_split = sem("unit_split")
    s_used = sem("unit_used")
    s_xl = [sem(f"x_landed{c}") for c in range(3)]
    s_cols = sem("cols_landed")
    s_cst = sem("consts_dve")
    s_cstp = sem("consts_pool")
    s_sq = sem("sq_ready")
    s_sqm = sem("sq_summed")
    s_rs = sem("rstd_ready")
    s_xn = sem("x_normed")
    s_xh = sem("x_hi")
    s_htd = sem("ht_even_tiles")
    s_htp = sem("ht_odd_tiles")
    d_done = sem("dense_done")
    ev_act = sem("dense_evac_act")
    ev_dve = sem("dense_evac_dve")
    s_bvo = sem("bias_vo_landed")
    s_os = [sem("o_stored0"), sem("o_stored1")]
    s_g1 = sem("gate_summed")
    s_gs = [sem("gate_stored0"), sem("gate_stored1")]
    p_z = sem("rows_zeroed")
    p_in = sem("rows_split")
    p_abs = sem("abs_f")
    p_ln = sem("softplus")
    p_args = sem("row_args")
    p_out = sem("rows_stored")
    p_80 = sem("rows80_landed")
    p_exp = sem("rows80_exp")
    p_col = sem("cols_transposed")
    p_tc = sem("tokcol_ready")
    m_sel = sem("m_head_columns")
    m_pick = sem("m_head_pick")
    a_sel = sem("a_next_head_columns")
    m_sc = sem("m_scores")
    m_e = sem("m_exponents")
    m_x = sem("m_exp")
    m_a = sem("m_weights")
    m_wk = sem("m_wk")
    m_nd = sem("m_numden")
    m_qc = sem("m_inter_scaled")
    m_ndx = sem("m_numden_read")
    m_cu = sem("m_update")
    m_c = sem("m_state")
    m_ol = sem("m_o_loaded")
    m_ze = sem("m_o_exp")
    m_ss = sem("m_gated")
    m_yn = sem("m_normed")
    m_y = sem("m_y_transposed")
    s_ym = sem("ym_stored")
    m_ye = sem("m_y_evacuated")
    a_avt = sem("a_v_transposed")
    a_av = sem("a_v_tokens")
    a_kh = sem("a_keys_hi")
    a_kl = sem("a_keys_lo")
    a_qh = sem("a_query_hi")
    a_ql = sem("a_query_lo")
    a_s_done = sem("a_scores")
    a_m = sem("a_max")
    a_x = sem("a_exp")
    a_p = sem("a_probs")
    a_t = sem("a_probs_transposed")
    a_pt = sem("a_probs_hi")
    a_pl = sem("a_probs_lo")
    a_v = sem("a_out")
    a_oc = sem("a_out_lo_part")
    a_o = sem("a_out_added")
    s_ya = sem("ya_stored")
    s_ymr = [sem(f"ym_raw_landed{k}") for k in range(KT)]
    s_yar = [sem(f"ya_raw_landed{k}") for k in range(KT)]
    b_hi = sem("b_y_hi")
    b_mlo = sem("b_ym_lo")
    b_mlod = sem("b_ym_lo_last_two")
    b_alo = sem("b_ya_lo")
    b_done = sem("b_group_done")
    b_mix = sem("b_group_mixed")
    b_ml = sem("b_merged_lo")
    s_gw = [sem(f"gate_again{k}") for k in range(3)]
    s_mb = [sem(f"mlstm_branch_stored{k}") for k in range(3)]
    s_gl = [sem("mix_operands0"), sem("mix_operands1")]
    o_ev = sem("o_evacuated")
    q_sq = [sem("q_square0"), sem("q_square1")]
    q_acc = [sem("q_added0"), sem("q_added1")]
    n_sum = sem("n_summed")
    n_rs = sem("n_rstd")
    s_xr = sem("x_again")
    n_x1 = sem("n_x1")
    s_x1 = sem("x1_stored")
    n_h2 = sem("n_h2_value")
    s_h2 = sem("h2_stored")
    s_h2r = sem("h2_again")
    n_hh = sem("n_h2_hi")
    n_hl = sem("n_h2_lo")
    c_pad = sem("c_pads")
    c_ae = sem("c_a_evacuated")
    c_cv = sem("c_conv")
    c_ge = sem("c_gelu")
    c_fl = sem("c_f_lo")
    e_ev = sem("e_evacuated")
    s_ys = [sem("down_stored0"), sem("down_stored1")]
    s_fo = sem("final_operands")
    e_y = sem("e_out_ready")
    e_yn = sem("e_normed_for_pool")
    e_yp = sem("e_out_ready_pool")
    s_out = sem("out_stored")

    def used(p):
        return p - B_OUT[0] + 1

    def f_tile(k, part):
        return f_z[:, k, part] if k < FZ else f_x[:, k - FZ, part]

    def bank_free(eng, key_of, h):
        who = GROUPS[key_of(h if isinstance(h, int) else 1)][4]
        if who is None:
            return
        s = ev_act if who[0] == "act" else ev_dve
        eng.wait_ge(s, lin(lambda k: GROUPS[key_of(k)][4][1], h))

    def seq_of(c):
        return (0, NB_A) if c < NB_A else (NB_A, NB)

    def kblocks(j):
        lo, hi = seq_of(j)
        return list(range(max(lo, j - 1), min(hi, j + 2)))

    def v_block(blk):
        return v_hl[0][:, blk] if blk < 6 else v_hl[1][:, blk - 6]

    def tiles_before(j):
        return sum(len(kblocks(n)) for n in range(j))

    def chunk_of(d, i):
        return i if d == 0 else NB - 1 - i

    def fresh(d, i):
        c = chunk_of(d, i)
        lo, hi = seq_of(c)
        return c == (lo if d == 0 else hi - 1)

    def updates(d, i):
        return i + 1 < NB and not fresh(d, i + 1)

    def tcol(q, d, h, c):
        return tokcol[:, q, bass.ds(h * NB + (d * HEADS * NB + c), 1)]

    ctx_block = nc.Block()
    with ctx_block as block:

        @block.sync
        def _(sp):
            for c, (a, b) in enumerate(CHUNKS):
                sp.dma_start(xs[:, :, a:b], xt[:, :, a:b].rearrange("k p t -> p k t")).then_inc(s_xl[c], 16)
                if c == 0:
                    sp.dma_start(raw[:, RAW[0]], w[0:1].rearrange("o p (k c) -> (o p) k c", c=P)
                                 ).then_inc(s_raw[RAW[0]], 16)
            sp.dma_start(colt[:, 0:NCOL], cols[:]).then_inc(s_cols, 16)
            sp.dma_start(sinks[:], sink[0:1, :].to_broadcast([P, 16])).then_inc(s_cols, 16)

            def load(unit_of, h):
                n1 = unit_of(1 if not isinstance(h, int) else h)
                slot = RAW[n1]
                if prev_user(RAW, n1) is not None:
                    sp.wait_ge(s_split, lin(lambda k: prev_user(RAW, unit_of(k)) + 1, h))
                sp.dma_start(raw[:, slot], w[bass.ds(lin(unit_of, h), 1)]
                             .rearrange("o p (k c) -> (o p) k c", c=P)).then_inc(s_raw[slot], 16)

            def store_gate(k, h):
                for c, (a, b) in enumerate(CHUNKS):
                    pos = k * 3 + c
                    sp.wait_ge(s_g1, lin(lambda hh: 12 * hh + pos + 1, h))
                    sp.dma_start(gs[bass.ds(h * 4 + k, 1), :, a:b].rearrange("o p t -> (o p) t"),
                                 g_st[:, pos % 2, 0:b - a]).then_inc(s_gs[pos % 2], 16)

            def store_o(h):
                for blk in range(NB):
                    sp.wait_ge(ev_dve, lin(lambda k: GROUPS[("M", k, 12 + blk)][3], h))
                    sp.dma_start(zo[bass.ds(h, 1), blk].rearrange("o p t -> (o p) t"),
                                 o_st[:, blk % 2, :]).then_inc(s_os[blk % 2], 16)

            def m_loads(h, gates_h):
                for k in range(M_UNITS):
                    load(lambda hh, k=k: m_unit(hh + 1, k), h)
                    if k == 3:
                        if gates_h is not None:
                            sp.wait_ge(ev_dve, lin(lambda hh: NB * (hh + 1), gates_h))
                        sp.dma_start(bias_vo[:], bvo[bass.ds(h + 1, 1), :].to_broadcast([P, 2 * DH])
                                     ).then_inc(s_bvo, 16)

            def a_loads(h):
                for k in range(A_UNITS):
                    load(lambda hh, k=k: a_unit(hh, k), h)
                    if k == 1:
                        store_o(h)
                    if 2 <= k < 6:
                        store_gate(k - 2, h)

            m_first = [lambda k=k: load(lambda hh: m_unit(0, k), 0) for k in range(M_UNITS)]
            m_first[0]()
            sp.dma_start(bias_vo[:], bvo[0:1, :].to_broadcast([P, 2 * DH])).then_inc(s_bvo, 16)
            sp.wait_ge(ev_act, 3)
            sp.wait_ge(p_z, 1)
            for d in range(2):
                sp.dma_start(r_li[32 * d:32 * d + 4, :], r_if[4 * d:4 * d + 4, :]).then_inc(p_in, 16)
                sp.dma_start(r_f[32 * d:32 * d + 4, :], r_if[8 + 4 * d:12 + 4 * d, :]).then_inc(p_in, 16)
            for k in range(1, 7):
                m_first[k]()
            sp.wait_ge(p_args, 1)
            for q, rows in enumerate((r_u, r_li, r_f, r_m, r_b)):
                for d in range(2):
                    sp.dma_start(rows_d[q, 4 * d:4 * d + 4, :], rows[32 * d:32 * d + 4, :]).then_inc(p_out, 16)
            for d in range(2):
                sp.dma_start(dec_d[4 * d:4 * d + 4, :], r_dec[32 * d:32 * d + 4, :]).then_inc(p_out, 16)
            sp.wait_ge(p_out, 12 * 16)
            by_chunk = rows_d.rearrange("q r (c t) -> q (r c) t", t=P)
            sp.dma_start(urows[:], by_chunk[0]).then_inc(p_80, 16)
            sp.dma_start(r80[0:2 * HEADS * NB], by_chunk[1:5].rearrange("q r t -> r q t")).then_inc(p_80, 16)
            sp.dma_start(decay[:], dec_d.rearrange("(o r) c -> o (r c)", o=1).to_broadcast([P, 2 * HEADS * NB])
                         ).then_inc(p_80, 16)
            m_first[7]()
            with sp.Fori(0, HEADS - 1) as h:
                a_loads(h)
                m_loads(h, h)
            a_loads(HEADS - 1)

            def load_b(p, i=None, step=0):
                src = w[dram_unit(p):dram_unit(p) + 1] if i is None else w[bass.ds(i * step + dram_unit(p), 1)]
                done = U_B + p - 1 if p else U_B
                sp.wait_ge(s_split, done if i is None else i * step + done)
                sp.dma_start(raw[:, p % 2], src.rearrange("o p (k c) -> (o p) k c", c=P)).then_inc(s_raw[p % 2], 16)

            def load_many(p0, p1):
                with sp.Fori(0, (p1 - p0) // 2) as i:
                    load_b(p0, i, 2)
                    load_b(p0 + 1, i, 2)

            ym_tiles = ym_d.rearrange("(k p) t -> k p t", p=P)
            ya_tiles = ya_d.rearrange("(k p) t -> k p t", p=P)
            load_b(0)
            load_b(1)
            sp.wait_ge(d_done, len(GROUPS))
            sp.wait_ge(s_ym, 160 * (HEADS - 1))
            for k in range(KT - 2):
                sp.dma_start(ym_raw[:, k], ym_tiles[k]).then_inc(s_ymr[k], 16)
            sp.wait_ge(s_ym, 160 * HEADS)
            for k in range(KT - 2, KT):
                sp.dma_start(ym_raw[:, k], ym_tiles[k]).then_inc(s_ymr[k], 16)
            for p in range(2, 6):
                load_b(p)
            for s in range(2):
                sp.wait_ge(s_gs[s], 16 * HEADS * 6)
            sp.wait_ge(s_ya, 16 * NB * (HEADS - 1))
            sp.wait_ge(m_y, 5 * HEADS)

            def load_ya(k):
                sp.dma_start(ya_raw[:, YA_AT[k]], ya_tiles[k]).then_inc(s_yar[k], 16)

            for n in range(3 * KT + 2):
                if n < 3 * KT:
                    u, (a, b) = n // 3, CHUNKS[n % 3]
                    if n >= 3:
                        sp.wait_ge(s_mb[n % 3], 16 * (n // 3))
                    sp.dma_start(gw[:, a:b], gs[4 * (u // 2) + 2 + u % 2, :, a:b]).then_inc(s_gw[n % 3], 16)
                if n >= 2:
                    u, (a, b) = (n - 2) // 3, CHUNKS[(n - 2) % 3]
                    sp.wait_ge(b_mix, n - 1)
                    sp.dma_start(mb_d[u, :, a:b], gw[:, a:b]).then_inc(s_mb[(n - 2) % 3], 16)
                if n % 3 == 2 and 1 <= n // 3 <= KT - 1:
                    load_b(n // 3 + 5)
                if n == 4:
                    for k in range(5):
                        load_ya(k)
                if n == 17:
                    sp.wait_ge(s_ya, 16 * NB * HEADS)
                    sp.wait_ge(a_v, NB * HEADS)
                    load_ya(5)
                    load_ya(6)
            for s in range(3):
                sp.wait_ge(s_mb[s], 16 * KT)
            load_ya(7)
            with sp.Fori(0, KT // 2) as i:
                for g in range(6):
                    s, (a, b) = g // 3, ACH[g % 3]
                    sp.wait_ge(b_mix, i * 6 + (3 * KT + g - 1))
                    for n, src in enumerate((gs[bass.ds(i * 4 + s, 1), :, a:b], mb_d[bass.ds(i * 2 + s, 1), :, a:b])):
                        sp.dma_start(g_ld[:, g % 2, n, 0:b - a], src.rearrange("o p t -> (o p) t")
                                     ).then_inc(s_gl[g % 2], 16)
                    if g % 3 == 2:
                        load_b(B_AB + 5 + s, i, 2)
            sp.wait_ge(b_done, 6 * KT)
            sp.dma_start(xr[0][:], xt[:, :, 0:WIN].rearrange("k p t -> p k t")).then_inc(s_xr, 16)
            for p in range(B_AB + 13, B_UP[0] + 2):
                load_b(p)

            def store_x1(g):
                sp.wait_ge(n_x1, KT * (g + 1))
                sp.dma_start(x1_d[g].rearrange("k p t -> p k t"), x1[g][:]).then_inc(s_x1, 16)

            store_x1(0)
            for p in range(B_UP[0] + 2, B_UP[0] + 6):
                load_b(p)
            sp.wait_ge(n_h2, KT)
            sp.wait_ge(s_x1, 16)
            sp.dma_start(xr[1][:], xt[:, :, T - WIN:T].rearrange("k p t -> p k t")).then_inc(s_xr, 16)
            load_many(B_UP[0] + 6, B_UP[0] + 24)
            store_x1(1)
            load_many(B_UP[0] + 24, B_UP[0] + 30)
            sp.wait_ge(n_h2, 2 * KT)
            sp.dma_start(h2_d.rearrange("k p t -> p k t"), xr[1][:]).then_inc(s_h2, 16)
            load_many(B_UP[0] + 30, B_DOWN[0])
            for p in range(B_DOWN[0], B_DOWN[0] + 6):
                load_b(p)
            sp.wait_ge(s_used, used(B_DOWN[0] - 1))
            sp.wait_ge(s_h2, 16)
            sp.dma_start(h2_raw[:], h2_d.rearrange("k p t -> p k t")).then_inc(s_h2r, 16)
            load_many(B_DOWN[0] + 6, B_DOWN[0] + 24)
            for p in range(B_UP[1], B_UP[1] + 6):
                load_b(p)
            sp.wait_ge(s_used, used(B_UP[1] - 1))
            for s in range(2):
                sp.wait_ge(s_ys[s], 16 * KT // 2)
            sp.dma_start(yo[0][:], yo_d.rearrange("k p t -> p k t")).then_inc(s_fo, 16)
            sp.dma_start(xo[0][:], x1_d[0, :, :, 0:HALF].rearrange("k p t -> p k t")).then_inc(s_fo, 16)
            load_many(B_UP[1] + 6, B_UP[1] + 26)
            sp.wait_ge(e_y, KT)
            sp.dma_start(outs[:, :, 0:HALF].rearrange("k p t -> p k t"), yo[0][:]).then_inc(s_out, 16)
            load_many(B_UP[1] + 26, B_DOWN[1])
            for p in range(B_DOWN[1], B_DOWN[1] + 6):
                load_b(p)
            sp.wait_ge(s_used, used(B_DOWN[1] - 1))
            sp.wait_ge(s_x1, 32)
            sp.dma_start(xo[1][:], x1_d[1, :, :, 2:WIN].rearrange("k p t -> p k t")).then_inc(s_fo, 16)
            load_many(B_DOWN[1] + 6, B_END)
            for k in range(KT):
                if k in POOL_ADDS:
                    sp.wait_ge(e_yp, POOL_ADDS.index(k) + 1)
                else:
                    sp.wait_ge(e_y, KT + k + 1 - sum(n < k for n in POOL_ADDS))
                sp.dma_start(outs[k, :, HALF:T], yo[1][:, k, :]).then_inc(s_out, 16)
            sp.wait_ge(s_out, 16 * (KT + 1))

        @block.gpsimd
        def _(pool):
            nc.gpsimd.memset(ident[:], 0.0)
            nc.gpsimd.memset(mask[:], 0.0)
            nc.gpsimd.memset(one_col, 1.0)
            nc.gpsimd.iota(absrel[:], pattern=[[1, 3 * P]], base=-P, channel_multiplier=-1,
                           allow_small_or_imprecise_dtypes=True)
            pool.drain()
            nc.gpsimd.affine_select(out=ident[:], in_=ident[:], compare_op=ALU.not_equal, fill=1.0, base=0,
                                    pattern=[[-1, P]], channel_multiplier=1)
            nc.gpsimd.affine_select(out=mask[:, 0], in_=mask[:, 0], compare_op=ALU.is_ge, fill=-BIG, base=0,
                                    pattern=[[1, P]], channel_multiplier=-1)
            nc.gpsimd.affine_select(out=mask[:, 1], in_=mask[:, 1], compare_op=ALU.is_ge, fill=-BIG, base=0,
                                    pattern=[[-1, P]], channel_multiplier=1).then_inc(s_cstp, 1)

            def split(slot, rslot):
                nc.gpsimd.tensor_tensor(ring_h[:, :, slot * P:(slot + 1) * P], raw[:, rslot],
                                        one_col.unsqueeze(2).to_broadcast([P, KT, P]), ALU.mult)
                pool.drain()
                nc.gpsimd.tensor_tensor(ring_l[:, :, slot * P:(slot + 1) * P], raw[:, rslot],
                                        ring_h[:, :, slot * P:(slot + 1) * P].bitcast(F32),
                                        ALU.subtract).then_inc(s_split, 1)

            def take(unit_of, h):
                n1 = unit_of(1 if not isinstance(h, int) else h)
                rslot, slot = RAW[n1], RING[n1]
                pool.wait_ge(s_raw[rslot], lin(lambda k: 16 * RAW[:unit_of(k) + 1].count(rslot), h))
                if prev_user(RING, n1) is not None:
                    pool.wait_ge(d_done, lin(lambda k: GROUPS[LAST_GROUP[prev_user(RING, unit_of(k))]][0] + 1, h))
                split(slot, rslot)

            take(lambda k: 0, 0)
            take(lambda k: m_unit(k, 0), 0)
            for c, (a, b) in enumerate(CHUNKS):
                for k in range(1, KT, 2):
                    pool.wait_ge(s_xh, c * KT + k + 1)
                    nc.gpsimd.tensor_tensor(ht_l[:, k, a:b], xs[:, k, a:b], ht_h[:, k, a:b].bitcast(F32),
                                            ALU.subtract).then_inc(s_htp, 1)
            for u in range(1, M_UNITS):
                take(lambda k, u=u: m_unit(k, u), 0)
            with pool.Fori(0, HEADS - 1) as h:
                for u in range(A_UNITS):
                    take(lambda k, u=u: a_unit(k, u), h)
                for u in range(M_UNITS):
                    take(lambda k, u=u: m_unit(k + 1, u), h)
            for u in range(A_UNITS):
                take(lambda k, u=u: a_unit(k, u), HEADS - 1)
            for n in range(U_B, U_B + 2):
                take(lambda k, n=n: n, 0)
            for k in range(KT - 2):
                pool.wait_ge(b_hi, k + 1)
                nc.gpsimd.tensor_tensor(yl[:, k], ym_raw[:, k], yh[:, k].bitcast(F32), ALU.subtract).then_inc(b_mlo, 1)
            for n in range(U_B + 2, U_B + 4):
                take(lambda k, n=n: n, 0)
            with pool.Fori(0, 2 * KT // 4) as i:
                for s in range(4):
                    n = U_B + 4 + s
                    pool.wait_ge(s_raw[RAW[n]], i * 32 + 16 * RAW[:n + 1].count(RAW[n]))
                    pool.wait_ge(b_done, i * 12 + 3 * (s + 1))
                    split(RING[n], RAW[n])
            with pool.Fori(0, (B_END - 2 * KT - 4) // 4) as i:
                for s in range(4):
                    n = U_B + 2 * KT + 4 + s
                    pool.wait_ge(s_raw[RAW[n]], i * 32 + 16 * RAW[:n + 1].count(RAW[n]))
                    pool.wait_ge(s_used, i * 4 + s + 1)
                    split(RING[n], RAW[n])
            for n, k in enumerate(POOL_ADDS):
                pool.wait_ge(e_yn, n + 1)
                nc.gpsimd.tensor_tensor(yo[1][:, k], yo[1][:, k], xo[1][:, k], ALU.add).then_inc(e_yp, 1)

        def square(act, st, m, k, c, src):
            a = (WCH if st_width(st, m) == WIN else OCH)[c][0]
            b = a + src.shape[-1]
            j = 2 * k + c - 2
            slots = 4 if st == 0 else 1
            if k == 0:
                if m and c == 0:
                    act.wait_ge(n_sum, {(0, 1): 1, (1, 1): 3, (1, 2): 4, (1, 3): 5}[st, m])
                nc.scalar.activation(acc[st][:, a:b], src, ACT.Square).then_inc(q_sq[st], 1)
            else:
                if j >= slots or m:
                    act.wait_ge(q_acc[st], 14 * m + max(j - slots, -1) + 1)
                nc.scalar.activation(sq[st][:, j % slots, 0:b - a], src, ACT.Square).then_inc(q_sq[st], 1)

        def rstd_half(act, number, width, bank):
            act.wait_ge(n_sum, number)
            for c, (a, b) in enumerate(WCH if width == WIN else OCH):
                nc.scalar.activation(rs[:, a:b], ps[:, bank + c, 0:b - a], ACT.Ln, bias=eps_col, scale=1.0 / D)
            act.drain()
            nc.scalar.activation(rs[:, 0:width], rs[:, 0:width], ACT.Exp, scale=-0.5).then_inc(n_rs, 1)

        def halves_act(act):
            act.wait_ge(b_done, 3 * KT)
            for k in range(KT):
                act.wait_ge(s_yar[k], 16)
                nc.scalar.activation(yh[:, k], ya_raw[:, YA_AT[k]], ACT.Identity).then_inc(b_hi, 1)

            def evac_out(g, k):
                act.wait_ge(s_used, used(B_OUT[g] + k))
                for c, (a, b) in enumerate(WCH):
                    last = nc.scalar.activation(x1[g][:, k, a:b], ps[:, 2 * (k % 4) + c, 0:b - a], ACT.Copy)
                last.then_inc(o_ev, 1)
                if g == 0:
                    act.drain()
                    square_y(0, k)

            def square_y(g, k):
                for c, (a, b) in enumerate(WCH):
                    square(act, g, 0, k, c, x1[g][:, k, a:b])

            def square_x1(g, k):
                act.wait_ge(n_x1, g * KT + k + 1)
                for c, (a, b) in enumerate(WCH):
                    square(act, g, 1, k, c, x1[g][:, k, a:b])

            def h2_hi(g, k):
                act.wait_ge(n_h2, k + 1) if g == 0 else act.wait_ge(s_h2r, 16)
                nc.scalar.activation(h2_h[:, k], h2_raw[:, k], ACT.Identity).then_inc(n_hh, 1)

            for k in range(KT):
                evac_out(0, k)
            evac_out(1, 0)
            rstd_half(act, 1, WIN, 6)
            for k in range(KT):
                square_x1(0, k)
                if k in (2, 5, 7):
                    evac_out(1, k // 2)
            evac_out(1, 4)
            rstd_half(act, 2, WIN, 6)
            for k in range(KT):
                h2_hi(0, k)
                if k == 3:
                    evac_out(1, 5)
            evac_out(1, 6)
            evac_out(1, 7)
            act.drain()

            def up_tile(half, i, s):
                act.wait_ge(s_used, i * 4 + used(B_UP[half] + 2 * s))
                if isinstance(i, int) and i == 0 and s == 0:
                    act.wait_ge(c_pad, half + 1)
                act.wait_ge(c_cv, i * 2 + (half * (FT + 1) + s + 1))
                if half == 0:
                    pieces = [(0, 0, 256, 1), (0, 256, 322, 258), (1, 322, WIN, 324)]
                else:
                    pieces = [(0, 0, 322, 0), (1, 322, WIN, 322)]
                for c, a, b, o in pieces:
                    w0 = WCH[c][0]
                    last = nc.scalar.activation(a_s[:, o:o + b - a], ps[:, 4 * s + c, a - w0:b - w0], ACT.Copy)
                last.then_inc(c_ae, 1)
                act.wait_ge(c_cv, i * 2 + (half * (FT + 1) + 1 + s + 1))
                act.wait_ge(c_fl, i * 2 + (half * (FT + 2) + s + 2))
                nc.scalar.activation(fs[:], cv[:], ACT.Gelu_apprx_tanh).then_inc(c_ge, 1)

            def down_tile(half, k):
                act.wait_ge(s_used, used(B_DOWN[half] + 3 * k + 2))
                dst = yo[1][:, k] if half else (cv, fs)[k % 2]
                if half == 0 and k >= 2:
                    act.wait_ge(s_ys[k % 2], 16 * (k // 2))
                for c, (a, b) in enumerate(OCH):
                    nc.scalar.activation(dst[:, a:b], ps[:, 2 * (k % 4) + c, 0:b - a], ACT.Copy)
                for c, (a, b) in enumerate(OCH):
                    square(act, 1, 2 + half, k, c, ps[:, 2 * (k % 4) + c, 0:b - a])
                act.drain()
                act.sem_inc(e_ev, 1)
                if half == 0:
                    act.wait_ge(e_ev, k + 1)
                    act.dma_start(yo_d[k], dst[:]).then_inc(s_ys[k % 2], 16)

            for half in range(2):
                for t in range(FZ):
                    if half == 0 and t < 2:
                        for k in range(4 * t, 4 * t + 4):
                            square_y(1, k)
                    up_tile(half, t // 2, t % 2)
                    if t == 3 and half == 0:
                        act.wait_ge(n_h2, KT)
                        rstd_half(act, 3, WIN, 2)
                    if t == 1 and half == 1:
                        act.wait_ge(n_h2, 2 * KT)
                        rstd_half(act, 5, HALF, 2)
                    if half == 0 and 4 <= t < 8:
                        square_x1(1, 2 * t - 8)
                        square_x1(1, 2 * t - 7)
                    if half == 0 and t == 9:
                        rstd_half(act, 4, WIN, 2)
                with act.Fori(FZ // 2, FT // 2) as i:
                    for s in range(2):
                        up_tile(half, i, s)
                act.wait_ge(c_fl, (FT + 2) * (half + 1))
                act.drain()
                for k in range(KT):
                    down_tile(half, k)
                    if half == 0 and 2 <= k < 6:
                        h2_hi(1, 2 * k - 4)
                        h2_hi(1, 2 * k - 3)
            nc.scalar.preload_act_table_set("natural_log_exp_and_others")
            act.wait_ge(e_y, KT)
            rstd_half(act, 6, HALF, 0)

        @block.scalar
        def _(act):
            nc.scalar.preload_act_table_set("natural_log_exp_and_others")
            def square_x(c, k):
                a, b = CHUNKS[c]
                act.wait_ge(s_xl[c], 16)
                if k >= 2:
                    act.wait_ge(s_sqm, c * KT + k - 1)
                nc.scalar.activation(sq0[:, k % 2, a:b], xs[:, k, a:b], ACT.Square).then_inc(s_sq, 1)

            for k in range(KT):
                square_x(0, k)
            act.wait_ge(s_cst, 1)
            for c, (a, b) in enumerate(CHUNKS):
                act.wait_ge(s_sqm, (c + 1) * KT)
                nc.scalar.activation(rs0[:, a:b], ps[:, 2 + c, 0:b - a], ACT.Ln, bias=eps_col, scale=1.0 / D)
                act.drain()
                nc.scalar.activation(rs0[:, a:b], rs0[:, a:b], ACT.Exp, scale=-0.5).then_inc(s_rs, 1)
                for k in range(KT):
                    if c + 1 < len(CHUNKS):
                        square_x(c + 1, k)
                    act.wait_ge(s_xn, c * KT + k + 1)
                    nc.scalar.activation(ht_h[:, k, a:b], xs[:, k, a:b], ACT.Identity).then_inc(s_xh, 1)

            def evac(key_of, h, dst, bias, scale=1.0, func=ACT.Identity, rows=slice(0, P)):
                key1 = key_of(h if isinstance(h, int) else 1)
                a, b = CHUNKS[key1[2] % 3]
                src = ps[rows, key1[2] % 2, 0:b - a]
                act.wait_ge(d_done, lin(lambda k: GROUPS[key_of(k)][0] + 1, h))
                return nc.scalar.activation(dst, src, func, bias=bias, scale=scale)

            for c, (a, b) in enumerate(CHUNKS):
                evac(lambda k, c=c: ("if", 0, c), 0, r_if[:, a:b], colt[:, C_IF:C_IF + 1]).then_inc(ev_act, 1)

            def evac_m(g, h, shift=0):
                a, b = CHUNKS[g % 3]
                u = g // 3
                dst = (mq_t if u < 2 else mk_t)[:, u % 2, a:b]
                col = (HC_MQ if u < 2 else HC_MK) + u % 2
                if g == 0:
                    act.wait_ge(a_sel, lin(lambda k: k + shift + 1, h))
                evac(lambda k: ("M", k + shift, g), h, dst, hc[:, col:col + 1],
                     1.0 if u < 2 else DH ** -0.5).then_inc(ev_act, 1)

            act.drain()
            for g in range(3):
                evac_m(g, 0)
            act.wait_ge(p_abs, 1)
            nc.scalar.activation(r_b[0:36], r_b[0:36], ACT.Exp, scale=-1.0)
            act.drain()
            nc.scalar.activation(r_b[0:36], r_b[0:36], ACT.Ln, bias=1.0).then_inc(p_ln, 1)
            for g in range(3, 12):
                evac_m(g, 0)
            act.wait_ge(p_80, 48)
            nc.scalar.activation(r80[0:80, 1:4], r80[0:80, 1:4], ACT.Exp)
            nc.scalar.activation(decay[:], decay[:], ACT.Exp).then_inc(p_exp, 1)

            def evac_a(g, h):
                a, b = CHUNKS[g % 3]
                u = g // 3
                if u < 4:
                    if g >= 2:
                        act.wait_ge(s_gs[g % 2], lin(lambda k: 16 * (6 * k + g // 2), h))
                    evac(lambda k: ("A", k, g), h, g_st[:, g % 2, 0:b - a],
                         hc[:, HC_G + u:HC_G + u + 1], -1.0, ACT.Exp).then_inc(ev_act, 1)
                elif u < 6:
                    evac(lambda k: ("A", k, g), h, aq_t[:, u - 4, a:b], hc[:, HC_AQ + u - 4:HC_AQ + u - 3]
                         ).then_inc(ev_act, 1)
                else:
                    for r in range(2):
                        evac(lambda k: ("A", k, g), h, kk_t[r * HD:(r + 1) * HD, a:b],
                             hc[0:HD, HC_AKV:HC_AKV + 1], rows=slice(0, HD))
                    evac(lambda k: ("A", k, g), h, av_t[HD:P, a:b], hc[HD:P, HC_AKV:HC_AKV + 1],
                         rows=slice(HD, P)).then_inc(ev_act, 1)

            def mlstm(h, dense):
                act.wait_ge(m_sel, lin(lambda k: k + 1, h))
                for i in range(NB):
                    act.wait_ge(m_e, lin(lambda k: NB * k + i + 1, h))
                    nc.scalar.activation(ex[:], ex[:], ACT.Exp).then_inc(m_x, 1)
                    if i >= 5:
                        act.wait_ge(m_ol, lin(lambda k: 32 * (5 * k + i - 4), h))
                        nc.scalar.activation(o_ld[:], o_ld[:], ACT.Exp, scale=-1.0)
                        act.drain()
                        nc.scalar.activation(o_ld[:], o_ld[:], ACT.Identity, bias=one_col).then_inc(m_ze, 1)
                    evac_a(2 * i, h)
                    inter = [d for d in range(2) if not fresh(d, i)]
                    if inter:
                        act.wait_ge(m_nd, lin(lambda k: NB * k + i + 1, h))
                        for d in inter:
                            last = nc.scalar.activation(nd[:, d], ps[:, 3 + 2 * d, 0:DH + 1], ACT.Copy,
                                                        scale=hc[:, d * NB + chunk_of(d, i):][:, 0:1])
                        last.then_inc(m_qc, 1)
                    if i > 5:
                        finish_y(i - 1, h)
                    evac_a(2 * i + 1, h)
                    if i == NB - 1:
                        evac_a(20, h)
                    if i >= 5:
                        rstd(i, h)
                    if i >= 4 and i < NB - 1:
                        load_o(i + 1, h)
                if dense:
                    evac_m(0, h, 1)
                split_keys(h)
                split_query(0, h)
                finish_y(NB - 1, h)

            def load_o(i, h):
                if i > 5:
                    act.wait_ge(m_yn, lin(lambda k: 5 * k + i - 5, h))
                for s in range(2):
                    act.wait_ge(s_os[s], lin(lambda k: 16 * 5 * (k + 1), h))
                for d in range(2):
                    act.dma_start(o_ld[:, d, :], zo[bass.ds(h, 1), chunk_of(d, i)]
                                  .rearrange("o p t -> (o p) t")).then_inc(m_ol, 16)

            def rstd(i, h):
                act.wait_ge(m_ss, lin(lambda k: 5 * k + i - 4, h))
                nc.scalar.activation(small[:, 8:10], small[:, 6:8], ACT.Ln, bias=eps_col, scale=1.0 / DH)
                act.drain()
                nc.scalar.activation(small[:, 10:12], small[:, 8:10], ACT.Exp, scale=-0.5)
                act.drain()
                for d in range(2):
                    c = chunk_of(d, i)
                    last = nc.scalar.activation(h_acc[:, c], h_acc[:, c], ACT.Copy, scale=small[:, 10 + d:11 + d])
                last.then_inc(m_yn, 1)

            def finish_y(i, h):
                act.wait_ge(m_y, lin(lambda k: 5 * k + i - 4, h))
                if i > 5:
                    act.wait_ge(s_ym, lin(lambda k: 32 * (5 * k + i - 5), h))
                for dt in range(2):
                    last = nc.scalar.activation(y_st[:, dt], ps[:, 7, 256 * dt:256 * dt + 256]
                                                .rearrange("p (c t) -> p c t", c=2), ACT.Copy,
                                                scale=hc[:, HC_MLN + dt:HC_MLN + dt + 1])
                last.then_inc(m_ye, 1)
                act.wait_ge(m_ye, lin(lambda k: 5 * k + i - 4, h))
                for d in range(2):
                    c = chunk_of(d, i)
                    act.dma_start(ym_d.rearrange("(h e p) t -> h p e t", e=2, p=P)
                                  [bass.ds(h, 1), :, :, c * P:(c + 1) * P].rearrange("o p e t -> (o p) e t"),
                                  y_st[:, :, d, :]).then_inc(s_ym, 16)

            def exps(j, h):
                act.wait_ge(a_m, lin(lambda k: NB * k + j + 1, h))
                kb = kblocks(j)
                a, b = (kb[0] - j + 1) * P, (kb[-1] - j + 2) * P
                for r in range(QPG):
                    nc.scalar.activation(prob[:, r, a:b], prob[:, r, a:b], ACT.Exp, bias=small[:, 20 + r:21 + r],
                                         scale=HD ** -0.5, accum_out=small[:, 24 + r:25 + r])
                nc.scalar.activation(small[:, 32:36], small[:, 28:32], ACT.Exp).then_inc(a_x, 1)

            def evac_pt(j, h):
                act.wait_ge(a_t, lin(lambda k: NB * k + j + 1, h))
                for n in range(len(kblocks(j))):
                    nc.scalar.activation(prob_h[:, n], ps[:, TURN_BANK[n], :], ACT.Identity).then_inc(a_pt, 1)

            def split_keys(h):
                act.drain()
                act.wait_ge(a_avt, lin(lambda k: k + 1, h))
                nc.scalar.activation(kk_h[:], kk_t[:], ACT.Identity).then_inc(a_kh, 1)

            def split_query(j, h):
                if j == 1:
                    act.wait_ge(s_ym, lin(lambda k: 160 * (k + 1), h))
                elif j > 1:
                    act.wait_ge(a_s_done, lin(lambda k: NB * k + j, h))
                for odd in range(2):
                    rows = slice(HD * odd, HD * odd + HD)
                    last = nc.scalar.activation(q_st[j > 0][rows, odd], aq_t[rows, :, j * P:(j + 1) * P], ACT.Identity)
                last.then_inc(a_qh, 1)

            def evac_o(j, h):
                act.wait_ge(a_v, lin(lambda k: NB * k + j + 1, h))
                if j > 0:
                    act.wait_ge(s_ya, lin(lambda k: 16 * (NB * k + j), h))
                nc.scalar.activation(ya_st[:], ps[HD:P, 5, :].rearrange("p (r t) -> p r t", r=QPG),
                                     ACT.Copy).then_inc(a_oc, 1)

            def store_o(j, h):
                act.wait_ge(a_o, lin(lambda k: NB * k + j + 1, h))
                act.dma_start(ya_d.rearrange("(h r p) t -> h p r t", r=QPG, p=HD)
                              [bass.ds(h, 1), :, :, j * P:(j + 1) * P].rearrange("o p r t -> (o p) r t"),
                              ya_st[:]).then_inc(s_ya, 16)

            def ym_hi(*tiles):
                for k in tiles:
                    act.wait_ge(s_ymr[k], 16)
                    nc.scalar.activation(yh[:, k], ym_raw[:, k], ACT.Identity).then_inc(b_hi, 1)

            def attend(h, dense):
                if dense:
                    evac_m(1, h, 1)
                split_query(1, h)
                if dense:
                    evac_m(M_FIRST[0], h, 1)
                exps(0, h)
                if dense:
                    for g in M_FIRST[1:]:
                        evac_m(g, h, 1)
                if not dense:
                    ym_hi(0, 1)
                for j in range(NB):
                    evac_pt(j, h)
                    if not dense and j == 1:
                        ym_hi(6, 7)
                    if j > 0:
                        store_o(j - 1, h)
                    if j + 2 < NB:
                        split_query(j + 2, h)
                    if j + 1 < NB:
                        exps(j + 1, h)
                    if not dense and j == 0:
                        ym_hi(2, 3, 4)
                    for g in M_BESIDE[j]:
                        if dense and g < 12:
                            evac_m(g, h, 1)
                    evac_o(j, h)
                    if not dense and j == 0:
                        ym_hi(5)
                store_o(NB - 1, h)
                for s in range(2):
                    act.wait_ge(s_gs[s], lin(lambda k: 16 * 6 * (k + 1), h))
                act.wait_ge(s_ym, lin(lambda k: 160 * (k + 1), h))

            with act.Fori(0, HEADS - 1) as h:
                mlstm(h, True)
                attend(h, True)
            mlstm(HEADS - 1, False)
            attend(HEADS - 1, False)
            halves_act(act)

        @block.vector
        def _(dve):
            V = nc.vector
            V.memset(ones0[:], 1.0)
            V.memset(eps_col, EPS).then_inc(s_cst, 1)
            for r in range(16):
                V.memset(slope8[:, r:r + 1], -(2.0 ** (-8.0 * (r + 1) / 16)) * HD ** 0.5)
            dve.wait_ge(s_cstp, 1)
            V.scalar_tensor_tensor(absrel[:], absrel[:], -1.0, absrel[:], ALU.mult, ALU.max)
            dve.drain()
            V.tensor_scalar(g_st[:, 0, 0:3 * P], absrel[:], float(P), BIG, ALU.is_gt, ALU.mult)
            dve.drain()
            V.tensor_tensor(absrel[:], absrel[:], g_st[:, 0, 0:3 * P], ALU.max)
            dve.wait_ge(s_cols, 32)
            V.tensor_scalar(colt[:, C_MK:C_MK + 8], colt[:, C_MK:C_MK + 8], DH ** -0.5, None, ALU.mult)
            V.tensor_scalar(colt[:, C_G:C_G + 16], colt[:, C_G:C_G + 16], -1.0, None, ALU.mult)
            dve.drain()
            V.tensor_copy(hc[:, HC_MQ:HC_MQ + 2], colt[:, C_MQ:C_MQ + 2])
            V.tensor_copy(hc[:, HC_MK:HC_MK + 2], colt[:, C_MK:C_MK + 2]).then_inc(a_sel, 1)
            for c, (a, b) in enumerate(CHUNKS):
                dve.wait_ge(s_rs, c + 1)
                for k in range(KT + 1):
                    if k < KT:
                        V.scalar_tensor_tensor(xs[:, k, a:b], xs[:, k, a:b], colt[:, C_PRE + k:C_PRE + k + 1],
                                               rs0[:, a:b], ALU.mult, ALU.mult).then_inc(s_xn, 1)
                    if k % 2 == 1:
                        dve.wait_ge(s_xh, c * KT + k)
                        V.tensor_tensor(ht_l[:, k - 1, a:b], xs[:, k - 1, a:b], ht_h[:, k - 1, a:b].bitcast(F32),
                                        ALU.subtract).then_inc(s_htd, 1)
            dve.wait_ge(s_htp, 3 * KT // 2)
            dve.drain()
            V.memset(v_tok[:, :, DH:DH + 1], 1.0)
            V.memset(r_li[0:36], 0.0)
            V.memset(r_f[0:36], 0.0)
            V.memset(r_m[0:36], 0.0)
            V.memset(r_mp[0:36], 0.0)
            dve.drain()
            V.memset(r_rst[0:36], 1.0).then_inc(p_z, 1)
            dve.drain()
            V.memset(r_rst[0:4].rearrange("p (c t) -> p c t", t=P)[:, :, 0:1], 0.0)
            V.memset(r_rst[32:36].rearrange("p (c t) -> p c t", t=P)[:, :, P - 1:P], 0.0)
            dve.wait_ge(p_in, 64)
            V.tensor_scalar(r_f[0:36], r_f[0:36], FORGET_BIAS, None, ALU.add)
            dve.drain()
            V.scalar_tensor_tensor(r_b[0:36], r_f[0:36], -1.0, r_f[0:36], ALU.mult, ALU.max).then_inc(p_abs, 1)
            dve.wait_ge(p_ln, 1)
            V.scalar_tensor_tensor(r_f[0:36], r_f[0:36], 0.0, r_b[0:36], ALU.min, ALU.subtract)
            dve.drain()
            V.tensor_tensor_scan(r_b[0:4], r_rst[0:4], r_f[0:4], 0.0, ALU.mult, ALU.add)
            V.tensor_tensor_scan(r_b[32:36][:, ::-1], r_rst[32:36][:, ::-1], r_f[32:36][:, ::-1], 0.0,
                                 ALU.mult, ALU.add)
            for a, b in ((0, SEQ_A), (SEQ_A, T)):
                V.tensor_tensor_scan(r_m[0:4, a:b], r_f[0:4, a:b], r_li[0:4, a:b], 0.0, ALU.add, ALU.max)
                V.tensor_tensor_scan(r_m[32:36, a:b][:, ::-1], r_f[32:36, a:b][:, ::-1],
                                     r_li[32:36, a:b][:, ::-1], 0.0, ALU.add, ALU.max)
            dve.drain()
            mch = r_m[:, :].rearrange("p (c t) -> p c t", t=P)
            for lo, hi in ((0, NB_A), (NB_A, NB)):
                V.tensor_copy(r_mp[0:4, lo + 1:hi].unsqueeze(2), mch[0:4, lo:hi - 1, P - 1:P])
                V.tensor_copy(r_mp[32:36, lo:hi - 1].unsqueeze(2), mch[32:36, lo + 1:hi, 0:1])
            V.tensor_tensor(r_u[0:36], r_b[0:36], r_m[0:36], ALU.subtract)
            V.tensor_tensor(r_li[0:36], r_li[0:36], r_b[0:36], ALU.subtract)
            dve.drain()
            uch = r_u[:, :].rearrange("p (c t) -> p c t", t=P)
            ulast = small[:, 40:50]
            V.tensor_copy(ulast[0:36].unsqueeze(2), uch[0:36, :, P - 1:P])
            dve.drain()
            V.tensor_copy(ulast[32:36].unsqueeze(2), uch[32:36, :, 0:1])
            dve.drain()
            V.tensor_tensor(r_dec[0:36], ulast[0:36], r_mp[0:36], ALU.add)
            V.tensor_tensor(r_f[0:36].rearrange("p (c t) -> p c t", t=P), uch[0:36],
                            r_mp[0:36].unsqueeze(2).to_broadcast([36, NB, P]), ALU.add)
            V.tensor_tensor(r_b[0:36].rearrange("p (c t) -> p c t", t=P),
                            r_li[0:36].rearrange("p (c t) -> p c t", t=P),
                            ulast[0:36].unsqueeze(2).to_broadcast([36, NB, P]), ALU.add)
            V.tensor_scalar(r_m[0:36], r_m[0:36], -1.0, None, ALU.mult).then_inc(p_args, 1)

            def evac_vo(blk, h, shift=0):
                dve.wait_ge(d_done, lin(lambda k: GROUPS[("M", k + shift, 12 + blk)][0] + 1, h))
                if blk == 0:
                    dve.wait_ge(s_bvo, lin(lambda k: 16 * (k + shift + 1), h))
                if blk >= 2:
                    dve.wait_ge(s_os[blk % 2], lin(lambda k: 16 * (5 * (k + shift) + blk // 2), h))
                elif shift:
                    dve.wait_ge(s_os[blk % 2], lin(lambda k: 16 * 5 * (k + shift), h))
                bank = (12 + blk) % 2
                V.tensor_tensor(v_tok[:, blk, 0:DH], ps[:, bank, 0:DH], bias_vo[:, 0:DH], ALU.add)
                V.tensor_tensor(o_st[:, blk % 2], ps[:, bank, DH:2 * DH], bias_vo[:, DH:2 * DH],
                                ALU.add).then_inc(ev_dve, 1)

            for blk in range(NB):
                evac_vo(blk, 0)
            dve.wait_ge(p_col, 1)
            V.tensor_copy(tokcol[:], ps[:, 2, 0:320].rearrange("p (q r) -> p q r", q=4)).then_inc(p_tc, 1)

            def evac_gate(g, h):
                if g < 0 or g >= 12:
                    return
                a, b = CHUNKS[g % 3]
                pos = g
                dve.wait_ge(ev_act, lin(lambda k: GROUPS[("A", k, g)][3], h))
                st = g_st[:, pos % 2, 0:b - a]
                V.tensor_scalar(st, st, 1.0, None, ALU.add)
                dve.drain()
                V.reciprocal(st, st).then_inc(s_g1, 1)

            def pick_rows(h):
                for d in range(2):
                    last = V.tensor_copy(pick[0:80, d * NB:(d + 1) * NB],
                                         ident[0:80, bass.ds(h * NB + d * HEADS * NB, NB)])
                last.then_inc(m_pick, 1)

            def mlstm(h, dense):
                dve.drain()
                for d in range(2):
                    V.tensor_copy(hc[:, d * NB:(d + 1) * NB],
                                  tokcol[:, 1, bass.ds(h * NB + d * HEADS * NB, NB)])
                V.tensor_copy(hc[:, HC_AQ:HC_AQ + 2], colt[:, bass.ds(h * 2 + C_AQ, 2)])
                V.tensor_copy(hc[:, HC_AKV:HC_AKV + 1], colt[:, bass.ds(h + C_AKV, 1)])
                V.tensor_copy(hc[:, HC_G:HC_G + 4], colt[:, bass.ds(h * 4 + C_G, 4)])
                V.tensor_copy(hc[:, HC_MLN:HC_MLN + 2], colt[:, bass.ds(h * 2 + C_MLN, 2)]).then_inc(m_sel, 1)
                if dense:
                    next_columns(h + 1)
                for i in range(NB):
                    step = lambda k, i=i: NB * k + i + 1
                    ch = [chunk_of(d, i) for d in range(2)]
                    dve.wait_ge(m_sc, lin(step, h))
                    for d in range(2):
                        last = V.scalar_tensor_tensor(ex[:, d], ps[:, 2, 256 * d + P:256 * d + 2 * P],
                                                      tcol(0, d, h, ch[d]), mask[:, d], ALU.add, ALU.add)
                    last.then_inc(m_e, 1)
                    for d in range(2):
                        last = V.tensor_scalar(wk[:, d], ps[:, 7, 256 * d:256 * d + 256], tcol(3, d, h, ch[d]),
                                               None, ALU.mult)
                    last.then_inc(m_wk, 1)
                    dve.wait_ge(m_x, lin(step, h))
                    V.tensor_tensor(ex[:], ex[:], ps[:, 2, :].rearrange("p (d e t) -> p d e t", d=2, e=2)[:, :, 0, :],
                                    ALU.mult).then_inc(m_a, 1)
                    evac_gate(2 * i - 1, h)
                    dve.wait_ge(m_nd, lin(step, h))
                    if any(not fresh(d, i) for d in range(2)):
                        dve.wait_ge(m_qc, lin(lambda k: 9 * k + i, h))
                    for d in range(2):
                        if fresh(d, i):
                            last = V.tensor_copy(nd[:, d], ps[:, 4 + 2 * d, 0:DH + 1])
                        else:
                            last = V.tensor_tensor(nd[:, d], nd[:, d], ps[:, 4 + 2 * d, 0:DH + 1], ALU.add)
                    last.then_inc(m_ndx, 1)
                    dve.drain()
                    V.scalar_tensor_tensor(small[:, 4:6], nd[:, :, DH], -1.0, nd[:, :, DH], ALU.mult, ALU.max)
                    dve.drain()
                    for d in range(2):
                        V.tensor_tensor(small[:, d:d + 1], small[:, 4 + d:5 + d], tcol(2, d, h, ch[d]), ALU.max)
                    dve.drain()
                    V.reciprocal(small[:, 2:4], small[:, 0:2])
                    dve.drain()
                    for d in range(2):
                        if i < 5:
                            V.tensor_scalar(h_acc[:, ch[d]], nd[:, d, 0:DH], small[:, 2 + d:3 + d], None, ALU.mult)
                        else:
                            V.scalar_tensor_tensor(h_acc[:, ch[d]], nd[:, d, 0:DH], small[:, 2 + d:3 + d],
                                                   h_acc[:, ch[d]], ALU.mult, ALU.add)
                    evac_gate(2 * i, h)
                    if i >= 5:
                        dve.wait_ge(m_ze, lin(lambda k: 5 * k + i - 4, h))
                        V.reciprocal(o_ld[:], o_ld[:])
                        dve.drain()
                        for d in range(2):
                            V.tensor_tensor(h_acc[:, ch[d]], h_acc[:, ch[d]], o_ld[:, d], ALU.mult)
                        dve.drain()
                        for d in range(2):
                            last = V.scalar_tensor_tensor(o_ld[:, d], h_acc[:, ch[d]], 1.0, h_acc[:, ch[d]],
                                                          ALU.mult, ALU.mult, accum_out=small[:, 6 + d:7 + d])
                        last.then_inc(m_ss, 1)
                    if i + 1 < NB:
                        dve.wait_ge(m_cu, lin(lambda k: 9 * k + i + 1, h))
                        for d in range(2):
                            if not updates(d, i):
                                continue
                            for dt in range(2):
                                src = ps[:, 3 + 2 * d + dt, 0:DH + 1]
                                if fresh(d, i):
                                    last = V.tensor_copy(c_st[:, d, dt], src)
                                else:
                                    last = V.scalar_tensor_tensor(
                                        c_st[:, d, dt], c_st[:, d, dt],
                                        decay[:, bass.ds(h * NB + (d * HEADS * NB + ch[d]), 1)], src,
                                        ALU.mult, ALU.add)
                        last.then_inc(m_c, 1)
            def scores_max(j, h):
                kb = kblocks(j)
                a, b = (kb[0] - j + 1) * P, (kb[-1] - j + 2) * P
                dve.wait_ge(a_s_done, lin(lambda k: NB * k + j + 1, h))
                flat = ps[:, 2:5, :].rearrange("p b t -> p (b t)")
                if j > 0:
                    dve.wait_ge(a_t, lin(lambda k: NB * k + j, h))
                for r in range(QPG):
                    V.scalar_tensor_tensor(prob[:, r, a:b], absrel[:, a:b], slope8[:, bass.ds(h * QPG + r, 1)],
                                           flat[:, S_AT[r] + a:S_AT[r] + b], ALU.mult, ALU.add)
                dve.drain()
                V.tensor_reduce(small[:, 16:20], prob[:, :, a:b], AX.X, ALU.max)

            def exp_bias(j, h):
                dve.drain()
                V.scalar_tensor_tensor(small[:, 16:20], sinks[:, bass.ds(h * QPG, QPG)], HD ** 0.5, small[:, 16:20],
                                       ALU.mult, ALU.max)
                dve.drain()
                V.tensor_scalar(small[:, 20:24], small[:, 16:20], -(HD ** -0.5), None, ALU.mult)
                dve.drain()
                V.tensor_tensor(small[:, 28:32], sinks[:, bass.ds(h * QPG, QPG)], small[:, 20:24],
                                ALU.add).then_inc(a_m, 1)

            def normalise(j, h):
                kb = kblocks(j)
                a, b = (kb[0] - j + 1) * P, (kb[-1] - j + 2) * P
                dve.wait_ge(a_x, lin(lambda k: NB * k + j + 1, h))
                V.tensor_tensor(small[:, 36:40], small[:, 32:36], small[:, 24:28], ALU.add)
                dve.drain()
                V.reciprocal(small[:, 36:40], small[:, 36:40])
                dve.drain()
                for r in range(QPG):
                    last = V.tensor_scalar(prob[:, r, a:b], prob[:, r, a:b], small[:, 36 + r:37 + r], None, ALU.mult)
                last.then_inc(a_p, 1)

            def next_columns(h):
                V.tensor_copy(hc[:, HC_MQ:HC_MQ + 2], colt[:, bass.ds(h * 2 + C_MQ, 2)])
                V.tensor_copy(hc[:, HC_MK:HC_MK + 2], colt[:, bass.ds(h * 2 + C_MK, 2)]).then_inc(a_sel, 1)

            def gate_product(n):
                dve.wait_ge(b_done, n + 1)
                dve.wait_ge(s_gw[n % 3], 16 * (n // 3 + 1))
                a, b = CHUNKS[n % 3]
                V.tensor_tensor(gw[:, a:b], gw[:, a:b], ps[:, n % 2, 0:b - a], ALU.mult).then_inc(b_mix, 1)

            def split_values(h):
                dve.wait_ge(a_avt, lin(lambda k: k + 1, h))
                for n, blocks in enumerate((6, NB - 6)):
                    src = ps[:, 5 + n, 0:blocks * HD].rearrange("p (c e) -> p c e", c=blocks)
                    V.tensor_scalar(v_hl[n][:, :, 0], src, 1.0, None, ALU.mult)
                    dve.drain()
                    last = V.tensor_tensor(v_hl[n][:, :, 1], src, v_hl[n][:, :, 0].bitcast(F32), ALU.subtract)
                last.then_inc(a_av, 1)

            def split_query(j, h):
                dve.wait_ge(a_qh, lin(lambda k: NB * k + j + 1, h))
                for odd in range(2):
                    rows, other = slice(HD * odd, HD * odd + HD), slice(HD - HD * odd, P - HD * odd)
                    last = V.tensor_tensor(q_st[j > 0][other, odd], aq_t[rows, :, j * P:(j + 1) * P],
                                           q_st[j > 0][rows, odd].bitcast(F32), ALU.subtract)
                last.then_inc(a_ql, 1)

            def split_probs(j, h):
                if j == 0:
                    for s in range(2):
                        dve.wait_ge(s_gs[s], lin(lambda k: 16 * 6 * (k + 1), h))
                for n in range(len(kblocks(j))):
                    dve.wait_ge(a_pt, lin(lambda k: tiles_before(NB) * k + tiles_before(j) + n + 1, h))
                    last = V.tensor_tensor(prob_l[:, n], ps[:, TURN_BANK[n], :], prob_h[:, n].bitcast(F32),
                                           ALU.subtract)
                last.then_inc(a_pl, 1)

            def add_out(j, h):
                dve.wait_ge(a_oc, lin(lambda k: NB * k + j + 1, h))
                V.tensor_tensor(ya_st[:], ya_st[:], ps[0:HD, 5, :].rearrange("p (r t) -> p r t", r=QPG),
                                ALU.add).then_inc(a_o, 1)

            def attend(h, dense):
                dve.drain()
                split_values(h)
                dve.wait_ge(a_kh, lin(lambda k: k + 1, h))
                V.tensor_tensor(kk_l[:], kk_t[:], kk_h[:].bitcast(F32), ALU.subtract).then_inc(a_kl, 1)
                split_query(0, h)
                dve.wait_ge(m_y, lin(lambda k: 5 * (k + 1), h))
                scores_max(0, h)
                exp_bias(0, h)
                split_query(1, h)
                normalise(0, h)
                for j in range(NB):
                    if j + 1 < NB:
                        scores_max(j + 1, h)
                        exp_bias(j + 1, h)
                    split_probs(j, h)
                    if j + 2 < NB:
                        split_query(j + 2, h)
                    vo = [g - 12 for g in M_BESIDE[j] if dense and g >= 12]
                    for blk in vo[:1]:
                        evac_vo(blk, h, 1)
                    if not dense and j == 1:
                        for k in range(KT - 2, KT):
                            dve.wait_ge(b_hi, k + 1)
                            V.tensor_tensor(yl[:, k], ym_raw[:, k], yh[:, k].bitcast(F32), ALU.subtract
                                            ).then_inc(b_mlod, 1)
                    if j + 1 < NB:
                        normalise(j + 1, h)
                    for blk in vo[1:]:
                        evac_vo(blk, h, 1)
                    if not dense and j >= 1:
                        gate_product(2 * j - 2)
                        gate_product(2 * j - 1)
                    add_out(j, h)
                if dense:
                    pick_rows(h + 1)
                if not dense:
                    for n in range(2 * NB - 2, 3 * KT):
                        gate_product(n)
                dve.wait_ge(s_ya, lin(lambda k: 16 * NB * (k + 1), h))
                dve.wait_ge(m_ye, lin(lambda k: 5 * (k + 1), h))

            pick_rows(0)
            with dve.Fori(0, HEADS - 1) as h:
                mlstm(h, True)
                attend(h, True)
            mlstm(HEADS - 1, False)
            attend(HEADS - 1, False)

            for k in range(KT):
                dve.wait_ge(b_hi, KT + k + 1)
                V.tensor_tensor(yl[:, k], ya_raw[:, YA_AT[k]], yh[:, k].bitcast(F32), ALU.subtract).then_inc(b_alo, 1)
            dve.drain()
            with dve.Fori(0, KT // 2) as i:
                for g in range(6):
                    s, (a, b) = g // 3, ACH[g % 3]
                    ga, mb = g_ld[:, g % 2, 0, 0:b - a], g_ld[:, g % 2, 1, 0:b - a]
                    dve.wait_ge(s_gl[g % 2], i * 96 + 32 * (g // 2 + 1))
                    dve.wait_ge(b_done, i * 6 + (3 * KT + g + 1))
                    V.tensor_tensor(ga, ga, ps[:, g, 0:b - a], ALU.mult)
                    dve.drain()
                    V.tensor_tensor(ga, ga, mb, ALU.add)
                    dve.drain()
                    hi = mg_h[:, bass.ds(i * 2 + s, 1), a:b].rearrange("p o t -> p (o t)")
                    lo = mg_l[:, bass.ds(i * 2 + s, 1), a:b].rearrange("p o t -> p (o t)")
                    V.tensor_scalar(hi, ga, 1.0, None, ALU.mult)
                    dve.drain()
                    V.tensor_tensor(lo, ga, hi.bitcast(F32), ALU.subtract)
                    dve.drain()
                    dve.sem_inc(b_ml, 1)
                    dve.sem_inc(b_mix, 1)
            dve.drain()
            V.memset(ones[:], 1.0)
            dve.drain()

            def add_squares(st, m, k):
                if k == 0:
                    return
                slots = 4 if st == 0 else 1
                for c, (a, b) in enumerate(WCH if st_width(st, m) == WIN else OCH):
                    j = 2 * k + c - 2
                    dve.wait_ge(q_sq[st], 16 * m + j + 3)
                    V.tensor_tensor(acc[st][:, a:b], acc[st][:, a:b], sq[st][:, j % slots, 0:b - a], ALU.add)
                    dve.drain()
                    dve.sem_inc(q_acc[st], 1)

            def residual(g, k):
                V.scalar_tensor_tensor(x1[g][:, k], x1[g][:, k], colt[:, C_POSTMIX + k:C_POSTMIX + k + 1], rs[:],
                                       ALU.mult, ALU.mult)
                dve.drain()
                V.tensor_tensor(x1[g][:, k], x1[g][:, k], xr[g][:, k], ALU.add).then_inc(n_x1, 1)

            def h2_value(g, k):
                V.scalar_tensor_tensor(xr[g][:, k], x1[g][:, k], colt[:, C_PREFFN + k:C_PREFFN + k + 1], rs[:],
                                       ALU.mult, ALU.mult).then_inc(n_h2, 1)

            def h2_lo(g, k):
                dve.wait_ge(n_hh, g * KT + k + 1)
                V.tensor_tensor(h2_l[:, k], h2_raw[:, k], h2_h[:, k].bitcast(F32), ALU.subtract).then_inc(n_hl, 1)

            for k in range(KT):
                add_squares(0, 0, k)
            dve.wait_ge(n_rs, 1)
            dve.wait_ge(s_xr, 16)
            for k in range(KT):
                residual(0, k)
                if k:
                    add_squares(0, 1, k - 1)
            add_squares(0, 1, KT - 1)
            dve.wait_ge(n_rs, 2)
            for k in range(KT):
                h2_value(0, k)
                if k:
                    h2_lo(0, k - 1)
            h2_lo(0, KT - 1)

            def up_tile(half, i, s, f_hi, f_lo):
                if half == 0:
                    segments = [(0, 256, 0), (256, HALF, 257)]
                else:
                    segments = [(0, HALF, 1)]
                dve.wait_ge(c_ae, i * 2 + (half * FT + s + 1))
                if isinstance(i, int):
                    col = lambda n: colt[:, 2 * i + C_CW + n * FT + s:2 * i + C_CW + n * FT + s + 1]
                else:
                    col = lambda n: colt[:, bass.ds(i * 2 + (C_CW + n * FT + s), 1)]
                for a, b, o in segments:
                    V.tensor_scalar(cv[:, a:b], a_s[:, o + 1:o + 1 + b - a], col(1), col(3), ALU.mult, ALU.add)
                dve.drain()
                for a, b, o in segments:
                    V.scalar_tensor_tensor(cv[:, a:b], a_s[:, o:o + b - a], col(0), cv[:, a:b], ALU.mult, ALU.add)
                dve.drain()
                for a, b, o in segments:
                    last = V.scalar_tensor_tensor(cv[:, a:b], a_s[:, o + 2:o + 2 + b - a], col(2), cv[:, a:b],
                                                  ALU.mult, ALU.add)
                last.then_inc(c_cv, 1)
                dve.wait_ge(c_ge, i * 2 + (half * FT + s + 1))
                dve.wait_ge(s_used, i * 4 + used(B_UP[half] + 2 * s + 1))
                for c, (a, b) in enumerate(OCH):
                    V.tensor_tensor(fs[:, a:b], fs[:, a:b], ps[:, 4 * s + 2 + c, 0:b - a], ALU.mult)
                dve.drain()
                V.tensor_scalar(f_hi, fs[:], 1.0, None, ALU.mult)
                dve.drain()
                V.tensor_tensor(f_lo, fs[:], f_hi.bitcast(F32), ALU.subtract).then_inc(c_fl, 1)

            def final(half, k):
                V.scalar_tensor_tensor(yo[half][:, k], yo[half][:, k], colt[:, C_POSTFFN + k:C_POSTFFN + k + 1],
                                       rs[:, 0:HALF], ALU.mult, ALU.mult)
                dve.drain()
                V.tensor_tensor(yo[half][:, k], yo[half][:, k], xo[half][:, k], ALU.add).then_inc(e_y, 1)

            for half in range(2):
                dve.drain()
                dve.sem_inc(c_cv, 1)
                dve.sem_inc(c_fl, 2)
                if half == 0:
                    dve.wait_ge(s_used, used(B_OUT[1] + KT - 1))
                    V.memset(a_s[:, 0:1], 0.0)
                    V.memset(a_s[:, 257:258], 0.0).then_inc(c_pad, 1)
                else:
                    for n in range(2):
                        dve.wait_ge(s_ys[n], 16 * KT // 2)
                    V.memset(a_s[:, WIN:WIN + 1], 0.0).then_inc(c_pad, 1)
                dve.drain()
                for t in range(FZ):
                    if half == 0 and t < 2:
                        for k in range(4 * t, 4 * t + 4):
                            add_squares(1, 0, k)
                    up_tile(half, t // 2, t % 2, f_z[:, t, 0], f_z[:, t, 1])
                    if half == 0:
                        if t == 3:
                            dve.wait_ge(n_rs, 3)
                            dve.wait_ge(s_xr, 32)
                        if 4 <= t < 8:
                            for k in (2 * t - 8, 2 * t - 7):
                                residual(1, k)
                                add_squares(1, 1, k)
                        if t == 9:
                            dve.wait_ge(n_rs, 4)
                        if t in (10, 11):
                            for k in range(4):
                                h2_value(1, 4 * (t - 10) + k)
                    else:
                        if t == 1:
                            dve.wait_ge(n_rs, 5)
                            dve.wait_ge(s_fo, 32)
                        if 2 <= t < 2 + KT:
                            final(0, t - 2)
                if half == 0:
                    dve.wait_ge(s_x1, 32)
                    dve.wait_ge(s_h2, 16)
                else:
                    dve.wait_ge(s_out, 16)
                with dve.Fori(FZ // 2, FT // 2) as i:
                    for s in range(2):
                        f_hi, f_lo = [f_x[:, bass.ds(i * 2 + (s - FZ), 1), part, :].rearrange("p o t -> p (o t)")
                                      for part in range(2)]
                        up_tile(half, i, s, f_hi, f_lo)
                for k in range(KT):
                    add_squares(1, 2 + half, k)
                    if half == 0 and 2 <= k < 6:
                        h2_lo(1, 2 * k - 4)
                        h2_lo(1, 2 * k - 3)
            dve.wait_ge(n_rs, 6)
            dve.wait_ge(s_fo, 48)
            for k in range(KT):
                if k in POOL_ADDS:
                    V.scalar_tensor_tensor(yo[1][:, k], yo[1][:, k], colt[:, C_POSTFFN + k:C_POSTFFN + k + 1],
                                           rs[:, 0:HALF], ALU.mult, ALU.mult).then_inc(e_yn, 1)
                else:
                    final(1, k)

        @block.tensor
        def _(pe):
            mm = nc.tensor.matmul

            def dense(out_ap, slot, rhs, kts=KT, k_first=0, first=True, last=True, before=None):
                hi, lo = rhs
                for k in range(kts):
                    if before is not None:
                        before(k)
                    wh = ring_h[:, k, slot * P:(slot + 1) * P]
                    wl = ring_l[:, k, slot * P:(slot + 1) * P]
                    mm(out_ap, wh, hi(k + k_first), start=first and k == 0, stop=False)
                    mm(out_ap, wh, lo(k + k_first), start=False, stop=False)
                    ins = mm(out_ap, wl, hi(k + k_first), start=False, stop=last and k == kts - 1)
                return ins

            pe.wait_ge(s_cst, 1)
            def sum_squares(c):
                a, b = CHUNKS[c]
                for k in range(KT):
                    pe.wait_ge(s_sq, c * KT + k + 1)
                    mm(ps[:, 2 + c, 0:b - a], ones0[:], sq0[:, k % 2, a:b], start=k == 0, stop=k == KT - 1
                       ).then_inc(s_sqm, 1)

            def unit_group(kind, u, c, h, shift=0, before=None):
                g = 3 * u + c
                unit = a_unit if kind == "A" else m_unit
                n1 = unit((1 if not isinstance(h, int) else h) + shift, u)
                a, b = CHUNKS[c]
                if c == 0:
                    pe.wait_ge(s_split, lin(lambda k: unit(k + shift, u) + 1, h))
                bank_free(pe, lambda k: (kind, k + shift, g), h)
                dense(ps[:, g % 2, 0:b - a], RING[n1],
                      (lambda k: ht_h[:, k, a:b], lambda k: ht_l[:, k, a:b]), before=before).then_inc(d_done, 1)

            def vo_group(blk, h, shift=0):
                g = 12 + blk
                if blk == 0:
                    pe.wait_ge(s_split, lin(lambda k: m_unit(k + shift, 7) + 1, h))
                bank_free(pe, lambda k: ("M", k + shift, g), h)
                t = slice(blk * P, (blk + 1) * P)
                for k in range(KT):
                    mm(ps[:, g % 2, :], ht_h[:, k, t], ring_h[:, k, :], start=k == 0, stop=False)
                    mm(ps[:, g % 2, :], ht_h[:, k, t], ring_l[:, k, :], start=False, stop=False)
                    ins = mm(ps[:, g % 2, :], ht_l[:, k, t], ring_h[:, k, :], start=False, stop=k == KT - 1)
                ins.then_inc(d_done, 1)

            def m_dense(g, h, shift=0):
                if g < 12:
                    unit_group("M", g // 3, g % 3, h, shift)
                else:
                    vo_group(g - 12, h, shift)

            sum_squares(0)
            for c, (a, b) in enumerate(CHUNKS):
                if c + 1 < len(CHUNKS):
                    sum_squares(c + 1)
                if c == 0:
                    pe.wait_ge(s_split, 1)
                if c == 2:
                    pe.wait_ge(ev_act, 1)

                def ht_tile(k):
                    pe.wait_ge((s_htd, s_htp)[k % 2], c * KT // 2 + k // 2 + 1)

                dense(ps[:, c % 2, 0:b - a], RING[0], (lambda k: ht_h[:, k, a:b], lambda k: ht_l[:, k, a:b]),
                      before=ht_tile).then_inc(d_done, 1)
            for g in range(22):
                m_dense(g, 0)
            pe.wait_ge(p_exp, 1)
            pe.wait_ge(s_cstp, 1)
            for q in range(4):
                ins = nc.tensor.transpose(ps[:, 2, 80 * q:80 * q + 80], r80[0:80, q], ident[0:80, 0:80])
            ins.then_inc(p_col, 1)
            pe.wait_ge(p_tc, 1)

            def m_scores(i, h):
                pe.wait_ge(m_pick, lin(lambda k: k + 1, h))
                if i > 6:
                    pe.wait_ge(m_ye, lin(lambda k: 5 * k + i - 6, h))
                if i == 0:
                    pe.wait_ge(ev_act, lin(lambda k: GROUPS[("M", k, 11)][3], h))
                for d in range(2):
                    c = chunk_of(d, i)
                    t = slice(c * P, (c + 1) * P)
                    for dt in range(2):
                        nc.tensor.transpose(ps[:, 7, 256 * d + P * dt:256 * d + P * dt + P], mk_t[:, dt, t], ident[:])
                    for dt in range(2):
                        mm(ps[:, 2, 256 * d:256 * d + P], mk_t[:, dt, t], mq_t[:, dt, t], start=dt == 0, stop=dt == 1)
                    j = d * NB + c
                    ins = mm(ps[:, 2, 256 * d + P:256 * d + 2 * P], pick[0:80, j:j + 1].to_broadcast([80, P]),
                             urows[:], start=True, stop=True)
                ins.then_inc(m_sc, 1)

            def m_numden(i, h):
                if i == 0:
                    pe.wait_ge(ev_dve, lin(lambda k: GROUPS[("M", k, 21)][3], h))
                if i > 0:
                    pe.wait_ge(m_c, lin(lambda k: 9 * k + i, h))
                for d in range(2):
                    c = chunk_of(d, i)
                    if not fresh(d, i):
                        for dt in range(2):
                            mm(ps[:, 3 + 2 * d, 0:DH + 1], mq_t[:, dt, c * P:(c + 1) * P], c_st[:, d, dt],
                               start=dt == 0, stop=dt == 1)
                pe.wait_ge(m_a, lin(lambda k: NB * k + i + 1, h))
                for d in range(2):
                    ins = mm(ps[:, 4 + 2 * d, 0:DH + 1], ex[:, d], v_tok[:, chunk_of(d, i)], start=True, stop=True)
                ins.then_inc(m_nd, 1)

            def m_update(i, h):
                if i + 1 == NB:
                    return
                pe.wait_ge(m_wk, lin(lambda k: NB * k + i + 1, h))
                pe.wait_ge(m_ndx, lin(lambda k: NB * k + i + 1, h))
                for d in range(2):
                    if updates(d, i):
                        for dt in range(2):
                            ins = mm(ps[:, 3 + 2 * d + dt, 0:DH + 1], wk[:, d, dt * P:(dt + 1) * P],
                                     v_tok[:, chunk_of(d, i)], start=True, stop=True)
                ins.then_inc(m_cu, 1)

            def m_turn(i, h):
                pe.wait_ge(m_yn, lin(lambda k: 5 * k + i - 4, h))
                if i + 1 < NB:
                    pe.wait_ge(m_wk, lin(lambda k: NB * k + i + 2, h))
                else:
                    pe.wait_ge(m_wk, lin(lambda k: NB * k + i + 1, h))
                for d in range(2):
                    for dt in range(2):
                        ins = nc.tensor.transpose(ps[:, 7, 256 * dt + P * d:256 * dt + P * d + P],
                                                  h_acc[:, chunk_of(d, i), dt * P:(dt + 1) * P], ident[:])
                ins.then_inc(m_y, 1)

            def turn_values(h):
                for c in range(NB):
                    bank, at_c = (5, c) if c < 6 else (6, c - 6)
                    ins = nc.tensor.transpose(ps[:, bank, at_c * HD:(at_c + 1) * HD],
                                              av_t[HD:P, c * P:(c + 1) * P], ident[HD:P, HD:P])
                ins.then_inc(a_avt, 1)

            def mlstm(h, is_dense):
                for i in range(NB):
                    m_scores(i, h)
                    unit_group("A", (2 * i) // 3, (2 * i) % 3, h)
                    m_numden(i, h)
                    if i > 5:
                        m_turn(i - 1, h)
                    unit_group("A", (2 * i + 1) // 3, (2 * i + 1) % 3, h)
                    m_update(i, h)
                unit_group("A", 6, 2, h)

                def before_values(k):
                    if k == KT - 1:
                        pe.wait_ge(m_ndx, lin(lambda k: NB * (k + 1), h))
                        pe.wait_ge(ev_act, lin(lambda k: GROUPS[("A", k, 20)][3], h))

                if is_dense:
                    unit_group("M", 0, 0, h, 1, before=before_values)
                else:
                    before_values(KT - 1)
                turn_values(h)
                m_turn(NB - 1, h)

            def a_scores(j, h):
                kb = kblocks(j)
                a, b = (kb[0] - j + 1) * P, (kb[-1] - j + 2) * P
                if j == 0:
                    pe.wait_ge(a_kl, lin(lambda k: k + 1, h))
                else:
                    pe.wait_ge(a_m, lin(lambda k: NB * k + j, h))
                pe.wait_ge(a_ql, lin(lambda k: NB * k + j + 1, h))
                for r in range(QPG):
                    lo = S_AT[r] + a
                    while lo < S_AT[r] + b:
                        hi = min(S_AT[r] + b, (lo // 512 + 1) * 512)
                        k0 = (j - 1) * P + lo - S_AT[r]
                        for n, keys in enumerate((kk_h, kk_l)):
                            ins = mm(ps[:, 2 + lo // 512, lo % 512:lo % 512 + hi - lo], q_st[j > 0][:, r % 2, r // 2],
                                     keys[:, k0:k0 + hi - lo], start=n == 0, stop=n == 1)
                        lo = hi
                ins.then_inc(a_s_done, 1)

            def a_turn(j, h):
                pe.wait_ge(a_p, lin(lambda k: NB * k + j + 1, h))
                if j == 0:
                    pe.wait_ge(a_av, lin(lambda k: k + 1, h))
                kb = kblocks(j)
                for n, blk in enumerate(kb):
                    o = (blk - j + 1) * P
                    if n == 2:
                        if j + 1 < NB:
                            a_scores(j + 1, h)
                        pe.wait_ge(a_o, lin(lambda k: NB * k + j, h))
                    for r in range(QPG):
                        ins = nc.tensor.transpose(ps[:, TURN_BANK[n], r * P:(r + 1) * P], prob[:, r, o:o + P], ident[:])
                ins.then_inc(a_t, 1)
                if len(kb) < 3 and j + 1 < NB:
                    a_scores(j + 1, h)

            def a_values(j, h):
                pe.wait_ge(a_pl, lin(lambda k: NB * k + j + 1, h))
                kb = kblocks(j)
                if len(kb) < 3 and j > 0:
                    pe.wait_ge(a_o, lin(lambda k: NB * k + j, h))
                for n, blk in enumerate(kb):
                    vals = v_block(blk).rearrange("p s e -> p (s e)")
                    mm(ps[:, 5, :], vals, prob_h[:, n], start=n == 0, stop=False)
                    ins = mm(ps[:, 5, :], vals, prob_l[:, n], start=False, stop=n == len(kb) - 1)
                ins.then_inc(a_v, 1)

            def branch_m(n):
                u, (a, b) = n // 3, CHUNKS[n % 3]
                if n == 0:
                    pe.wait_ge(ev_act, GROUP_COUNT["act"])
                if n % 3 == 0:
                    pe.wait_ge(s_split, U_B + B_MB + u + 1)
                if n >= 2:
                    pe.wait_ge(b_mix, n - 1)

                def ym_tile(k):
                    if k < KT - 2:
                        pe.wait_ge(b_mlo, k + 1)
                    else:
                        pe.wait_ge(b_mlod, k - KT + 3)

                dense(ps[:, n % 2, 0:b - a], u % 4, (lambda k: yh[:, k, a:b], lambda k: yl[:, k, a:b]),
                      before=ym_tile if n == 0 else None).then_inc(b_done, 1)

            def attend(h, is_dense):
                if is_dense:
                    m_dense(1, h, 1)
                pe.wait_ge(m_ye, lin(lambda k: 5 * (k + 1), h))
                a_scores(0, h)
                if is_dense:
                    for g in M_FIRST:
                        m_dense(g, h, 1)
                for j in range(NB):
                    a_turn(j, h)
                    if is_dense:
                        for g in M_BESIDE[j]:
                            m_dense(g, h, 1)
                    elif j >= 1:
                        branch_m(2 * j - 2)
                        branch_m(2 * j - 1)
                    a_values(j, h)
                if not is_dense:
                    for n in range(2 * NB - 2, 3 * KT):
                        branch_m(n)
                pe.wait_ge(a_o, lin(lambda k: NB * (k + 1), h))

            with pe.Fori(0, HEADS - 1) as h:
                mlstm(h, True)
                attend(h, True)
            mlstm(HEADS - 1, False)
            attend(HEADS - 1, False)

            pe.wait_ge(b_mix, 3 * KT)
            with pe.Fori(0, KT // 4) as i:
                for g in range(12):
                    u, (a, b) = g // 3, ACH[g % 3]
                    if g % 3 == 0:
                        pe.wait_ge(s_split, i * 4 + (U_B + B_AB + u + 1))
                    pe.wait_ge(b_mix, i * 12 + (3 * KT + g - 5))
                    before = (lambda k: pe.wait_ge(b_alo, k + 1)) if g == 0 else None
                    dense(ps[:, g % 6, 0:b - a], u, (lambda k: yh[:, k, a:b], lambda k: yl[:, k, a:b]),
                          before=before).then_inc(b_done, 1)

            def two_chunks(bank0, slot, hi, lo, chunks, **kw):
                for c, (a, b) in enumerate(chunks):
                    ins = dense(ps[:, bank0 + c, 0:b - a], slot, (lambda k: hi(k)[:, a:b], lambda k: lo(k)[:, a:b]),
                                **kw)
                return ins

            def feature_sum(st, m, bank):
                pe.wait_ge(q_acc[st], 14 * (m + 1))
                for c, (a, b) in enumerate(WCH if st_width(st, m) == WIN else OCH):
                    ins = mm(ps[:, bank + c, 0:b - a], ones[:], acc[st][:, a:b], start=True, stop=True)
                ins.then_inc(n_sum, 1)

            for g in range(2):
                for k in range(KT):
                    n = g * KT + k
                    before = None
                    if n == 0:
                        pe.wait_ge(b_ml, 3 * (KT - 1))
                        pe.wait_ge(b_mix, 6 * KT - 3)
                        before = lambda kk: pe.wait_ge(b_ml, 3 * KT) if kk == KT - 1 else None
                    if n >= 4:
                        pe.wait_ge(o_ev, n - 3)
                    pe.wait_ge(s_split, U_B + B_OUT[0] + n + 1)
                    t0 = g * (T - WIN)
                    two_chunks(2 * (k % 4), n % 4, lambda kk: mg_h[:, kk, t0:t0 + WIN],
                               lambda kk: mg_l[:, kk, t0:t0 + WIN], WCH, before=before).then_inc(s_used, 1)
                    if n == KT:
                        pe.wait_ge(o_ev, KT)
                        feature_sum(0, 0, 6)
                    if n == KT + 4:
                        pe.wait_ge(o_ev, KT + 4)
                        feature_sum(0, 1, 6)
                    if n in (KT + 2, KT + 6):
                        pe.wait_ge(n_rs, 1 if n == KT + 2 else 2)

            def up_tiles(half, lo, hi, sums, start=False):
                gate_ch = [(2 * half, 2 * half + 320), (2 * half + 320, 2 * half + 640)]
                with pe.Fori(lo // 2, hi // 2) as i:
                    for s in range(2):
                        pe.wait_ge(c_fl, i * 2 + (half * (FT + 2) + s + 1))
                        p = B_UP[half] + 2 * s
                        pe.wait_ge(s_split, i * 4 + (U_B + p + 1))
                        before = None
                        if start:
                            pe.wait_ge((o_ev, e_ev)[half], (2 - half) * KT - 2 + 2 * s)
                            before = (lambda k: pe.wait_ge(n_hl, KT * half + k + 1)) if s == 0 else None
                        two_chunks(4 * s, 2 * s, lambda k: h2_h[:, k], lambda k: h2_l[:, k], WCH,
                                   before=before).then_inc(s_used, 1)
                        pe.wait_ge(s_split, i * 4 + (U_B + p + 2))
                        pe.wait_ge(n_rs, sums)
                        two_chunks(4 * s + 2, 2 * s + 1, lambda k: h2_h[:, k], lambda k: h2_l[:, k], gate_ch
                                   ).then_inc(s_used, 1)

            for half in range(2):
                up_tiles(half, 0, 2, 2 + 2 * half, start=True)
                if half == 0:
                    up_tiles(half, 2, 4, 2)
                    pe.wait_ge(c_fl, 5)
                    feature_sum(1, 0, 2)
                    up_tiles(half, 4, 10, 3)
                    pe.wait_ge(c_fl, 11)
                    feature_sum(1, 1, 2)
                    up_tiles(half, 10, FT, 4)
                else:
                    pe.wait_ge(c_fl, FT + 5)
                    feature_sum(1, 2, 2)
                    up_tiles(half, 2, FT, 5)
                pe.wait_ge(c_fl, (FT + 2) * half + 2 + FT - 1)
                for k in range(KT):
                    if k >= 4:
                        pe.wait_ge(e_ev, half * KT + k - 3)
                    for part in range(3):
                        p = B_DOWN[half] + 3 * k + part
                        if k == 0 and part == 2:
                            pe.wait_ge(c_fl, (FT + 2) * (half + 1))
                        pe.wait_ge(s_split, U_B + p + 1)
                        two_chunks(2 * (k % 4), p % 4, lambda kk: f_tile(kk, 0), lambda kk: f_tile(kk, 1), OCH,
                                   kts=8 if part < 2 else FT - 16, k_first=8 * part, first=part == 0, last=part == 2
                                   ).then_inc(s_used, 1)
            pe.wait_ge(e_ev, 2 * KT)
            feature_sum(1, 3, 0)


def pack_units(w_in, w_att, w_mlstm, w_out, w_up, w_down):
    n_q, n_kv, n_m = D, HEADS * HD, D
    off_ak, off_av = n_q, n_q + n_kv
    off_mq = off_av + n_kv
    off_mk, off_mv, off_mo = off_mq + n_m, off_mq + 2 * n_m, off_mq + 3 * n_m
    off_if = off_mo + n_m
    off_g = off_if + 4 * HEADS

    def unit(wt, cols):
        return wt[:, cols].reshape(KT, P, P).transpose(1, 0, 2).reshape(P, KT * P)

    def sl(a):
        return slice(a, a + P)

    units = [unit(w_in, sl(off_if))]
    for h in range(HEADS):
        c = h * DH
        for o in (off_mq, off_mk, off_mo, off_mv):
            units += [unit(w_in, sl(o + c)), unit(w_in, sl(o + c + P))]
        for o in (off_g, off_g + D):
            units += [unit(w_in, sl(o + c)), unit(w_in, sl(o + c + P))]
        units += [unit(w_in, sl(c)), unit(w_in, sl(c + P))]
        kv = np.concatenate([w_in[:, off_ak + h * HD:off_ak + (h + 1) * HD],
                             w_in[:, off_av + h * HD:off_av + (h + 1) * HD]], axis=1)
        units.append(unit(kv, slice(0, P)))
    units += [unit(w_mlstm, sl(k * P)) for k in range(KT)]
    units += [unit(w_att, sl(k * P)) for k in range(KT)]
    units += [unit(w_out, sl(k * P)) for k in range(KT)]
    for f in range(FT):
        units += [unit(w_up, sl(f * P)), unit(w_up, sl(FF + f * P))]
    down = np.concatenate([w_down, np.zeros((24 * P - FF, D), w_down.dtype)], axis=0)
    for k in range(KT):
        for part in range(3):
            units.append(unit(down[part * D:(part + 1) * D], sl(k * P)))
    return np.ascontiguousarray(np.stack(units))


def pack_cols(b_in, pre, mln, postmix, preffn, postffn, conv_w, conv_b):
    n_q, n_kv, n_m = D, HEADS * HD, D
    off_mq = n_q + 2 * n_kv
    off_if = off_mq + 4 * n_m
    off_g = off_if + 4 * HEADS
    col = []
    col += list(b_in[off_mq:off_mq + D].reshape(KT, P))
    col += list(b_in[off_mq + D:off_mq + 2 * D].reshape(KT, P))
    col += list(b_in[0:D].reshape(KT, P))
    for h in range(HEADS):
        col.append(np.concatenate([b_in[n_q + h * HD:n_q + (h + 1) * HD],
                                   b_in[n_q + n_kv + h * HD:n_q + n_kv + (h + 1) * HD]]))
    for h in range(HEADS):
        for o in (off_g, off_g + D):
            col += [b_in[o + h * DH:o + h * DH + P], b_in[o + h * DH + P:o + (h + 1) * DH]]
    col.append(b_in[off_if:off_if + P])
    for v in (pre, mln, postmix, preffn, postffn):
        col += list(v.reshape(KT, P))
    for t in range(3):
        col += list(conv_w[t].reshape(FT, P))
    col += list(conv_b.reshape(FT, P))
    return np.ascontiguousarray(np.stack(col, axis=1))


def kernel(x_prompt, x_sample, pre_mix_norm, w_in, b_in, attn_sink, mlstm_norm, w_att_branch, w_mlstm_branch,
           w_out, post_mix_norm, pre_ffn_norm, w_ffn_up, ffn_conv_w, ffn_conv_b, w_ffn_down, post_ffn_norm):
    import concourse.bacc as bacc
    from concourse.bass_utils import run_bass_kernel_spmd

    a = [np.asarray(v) for v in (x_prompt, x_sample, pre_mix_norm, w_in, b_in, attn_sink, mlstm_norm, w_att_branch,
                                 w_mlstm_branch, w_out, post_mix_norm, pre_ffn_norm, w_ffn_up, ffn_conv_w,
                                 ffn_conv_b, w_ffn_down, post_ffn_norm)]
    (xp, xsm, pre, wi, bi, snk, mln, wa, wm, wo, pom, pf, wu, cw, cb, wd, pof) = a
    x = np.concatenate([xp[0], xsm[0]], axis=0)
    off_mv = D + 2 * HEADS * HD + 2 * D
    bv, bo = bi[0, off_mv:off_mv + D].reshape(HEADS, DH), bi[0, off_mv + D:off_mv + 2 * D].reshape(HEADS, DH)
    arrays = {
        "w": pack_units(wi[0], wa[0], wm[0], wo[0], wu[0], wd[0]),
        "xt": np.ascontiguousarray(x.T.reshape(KT, P, T)),
        "cols": pack_cols(bi[0], pre[0], mln[0], pom[0], pf[0], pof[0], cw[0], cb[0]),
        "bvo": np.ascontiguousarray(np.concatenate([bv, bo], axis=1)),
        "sink": np.ascontiguousarray(snk),
    }
    nc = bacc.Bacc("TRN2", target_bir_lowering=False, num_devices=1)
    args = [nc.dram_tensor(n, v.shape, mybir.dt.from_np(v.dtype), kind="ExternalInput").ap()
            for n, v in arrays.items()]
    out = nc.dram_tensor("yt", (KT, P, T), F32, kind="ExternalOutput").ap()
    build(nc, *args, out)
    r = run_bass_kernel_spmd(nc, [arrays], core_ids=[0])
    y = r.results[0]["yt"].reshape(D, T).T
    return (np.ascontiguousarray(y[:SEQ_A]).reshape(1, SEQ_A, D),
            np.ascontiguousarray(y[SEQ_A:]).reshape(1, SEQ_B, D))
```
